# Optimizing a Trainium2 kernel written in Bass

```python
import math
import jax, jax.numpy as jnp
from jax import lax
import numpy as np

D_MODEL = 1024
BATCH = 1
SEQ = 512
DEPTH = 2

N_MEM = 256
NORM_EPS = 1e-6
ROPE_THETA = 500000.0
HEAD_DIM = 64
ROT_DIM = HEAD_DIM // 4
BLOCK = 128
LRU_WIDTH = D_MODEL
LRU_HEADS = 4
LRU_HEAD_DIM = LRU_WIDTH // LRU_HEADS
CONV_WIDTH = 4
LRU_C = 8.0
B_HEADS = 8
B_WIDTH = B_HEADS * HEAD_DIM
DILATED_PATTERN = ((128, 1), (512, 4), (2048, 16))
C_HEADS = 16
C_KV_HEADS = 2
C_WINDOW = 128
C_Q_WIDTH = C_HEADS * HEAD_DIM
C_KV_WIDTH = C_KV_HEADS * HEAD_DIM
C_QKV = C_Q_WIDTH + 2 * C_KV_WIDTH
XA_HEADS = 4
XA_HEAD_DIM = 128
XA_WIDTH = XA_HEADS * XA_HEAD_DIM
D_FF = -(-8 * D_MODEL // (3 * 256)) * 256
AB_IN = 2 * LRU_WIDTH + 3 * B_WIDTH
AB_SPLITS = (LRU_WIDTH, 2 * LRU_WIDTH, 2 * LRU_WIDTH + B_WIDTH, 2 * LRU_WIDTH + 2 * B_WIDTH)
AB_OUT = LRU_WIDTH + B_WIDTH
N_EVEN = (DEPTH + 1) // 2
N_ODD = DEPTH // 2
NEG = -1e30

kernel_name = "hybrid_rglru_dilated_swa_sink_block"

def rms_norm(x, g):
    xf = x.astype(jnp.float32)
    xf = xf * lax.rsqrt(jnp.mean(xf * xf, axis=-1, keepdims=True) + NORM_EPS)
    return (xf * g.astype(jnp.float32)).astype(x.dtype)

def rope_tables(L):
    inv = ROPE_THETA ** (-jnp.arange(0, ROT_DIM, 2, dtype=jnp.float32) / ROT_DIM)
    ang = jnp.arange(L, dtype=jnp.float32)[:, None] * inv[None, :]
    return jnp.cos(ang), jnp.sin(ang)

def partial_rope(x, cos, sin):
    half = ROT_DIM // 2
    cos = cos.astype(x.dtype)
    sin = sin.astype(x.dtype)
    x1 = x[..., :half]
    x2 = x[..., half:ROT_DIM]
    return jnp.concatenate([x1 * cos - x2 * sin, x2 * cos + x1 * sin, x[..., ROT_DIM:]], axis=-1)

def banded_attention(q, k, v, max_dist, sinks=None):
    Bsz, Hq, L, hd = q.shape
    Hkv = k.shape[1]
    G = Hq // Hkv
    nb = -(-L // BLOCK)
    Lp = nb * BLOCK
    pad = ((0, 0), (0, 0), (0, Lp - L), (0, 0))
    qb = jnp.pad(q, pad).reshape(Bsz, Hkv, G, nb, BLOCK, hd)
    kb = jnp.pad(k, pad).reshape(Bsz, Hkv, nb, BLOCK, hd)
    vb = jnp.pad(v, pad).reshape(Bsz, Hkv, nb, BLOCK, hd)

    def band(t):
        prev = jnp.pad(t, ((0, 0), (0, 0), (1, 0), (0, 0), (0, 0)))[:, :, :nb]
        return jnp.concatenate([prev, t], axis=3)

    kband, vband = band(kb), band(vb)
    s = jnp.einsum('bhgnqd,bhnkd->bhgnqk', qb, kband).astype(jnp.float32) * (hd ** -0.5)
    blk = jnp.arange(nb)[:, None, None]
    qpos = blk * BLOCK + jnp.arange(BLOCK)[None, :, None]
    kpos = (blk - 1) * BLOCK + jnp.arange(2 * BLOCK)[None, None, :]
    dist = qpos - kpos
    mask = (dist >= 0) & (dist <= max_dist) & (kpos >= 0)
    s = jnp.where(mask, s, NEG)
    m = jnp.max(s, axis=-1, keepdims=True)
    if sinks is not None:
        sk = sinks.astype(jnp.float32).reshape(1, Hkv, G, 1, 1, 1)
        m = jnp.maximum(m, sk)
        e = jnp.exp(s - m)
        den = jnp.sum(e, axis=-1, keepdims=True) + jnp.exp(sk - m)
    else:
        e = jnp.exp(s - m)
        den = jnp.sum(e, axis=-1, keepdims=True)
    p = e / den
    lse = (m + jnp.log(den))[..., 0]
    o = jnp.einsum('bhgnqk,bhnkd->bhgnqd', p.astype(v.dtype), vband)
    o = o.reshape(Bsz, Hq, Lp, hd)[:, :, :L]
    lse = lse.reshape(Bsz, Hq, Lp)[:, :, :L]
    return o, lse

def dilated_attention(q, k, v):
    Bsz, H, L, hd = q.shape
    outs, lses = [], []
    for window, d in DILATED_PATTERN:
        Ld = L // d

        def to_strided(t):
            return t.reshape(Bsz, H, Ld, d, hd).transpose(0, 1, 3, 2, 4).reshape(Bsz, H * d, Ld, hd)

        o, lse = banded_attention(to_strided(q), to_strided(k), to_strided(v), window // d)
        outs.append(o.reshape(Bsz, H, d, Ld, hd).transpose(0, 1, 3, 2, 4).reshape(Bsz, H, L, hd))
        lses.append(lse.reshape(Bsz, H, d, Ld).transpose(0, 1, 3, 2).reshape(Bsz, H, L))
    w = jax.nn.softmax(jnp.stack(lses, axis=0), axis=0)
    o = jnp.sum(w[..., None] * jnp.stack(outs, axis=0).astype(jnp.float32), axis=0)
    return o.astype(q.dtype)

def causal_depthwise_conv(x, w, b):
    L = x.shape[1]
    xp = jnp.pad(x, ((0, 0), (CONV_WIDTH - 1, 0), (0, 0)))
    y = b + xp[:, 0:L] * w[0]
    for tap in range(1, CONV_WIDTH):
        y = y + xp[:, tap:tap + L] * w[tap]
    return y

def block_diag_linear(x, w, b):
    Bsz, L, _ = x.shape
    xh = x.reshape(Bsz, L, LRU_HEADS, LRU_HEAD_DIM)
    y = jnp.einsum('blhi,hij->blhj', xh, w) + b
    return y.reshape(Bsz, L, LRU_WIDTH)

def rg_lru(x, wa, ba, wx, bx, lam):
    r = jax.nn.sigmoid(block_diag_linear(x, wa, ba).astype(jnp.float32))
    i = jax.nn.sigmoid(block_diag_linear(x, wx, bx).astype(jnp.float32))
    log_a = -LRU_C * r * jax.nn.softplus(-lam.astype(jnp.float32))
    a = jnp.exp(log_a)
    u = jnp.sqrt(-jnp.expm1(2.0 * log_a)) * (i * x.astype(jnp.float32))

    def combine(left, right):
        a1, b1 = left
        a2, b2 = right
        return a1 * a2, a2 * b1 + b2

    _, h = lax.associative_scan(combine, (a, u), axis=1)
    return h.astype(x.dtype)

def lru_dilated_mixer(h, cos, sin, w_in, conv_w, conv_b, wa, ba, wx, bx, lam, w_out):
    Bsz, L, _ = h.shape
    proj = h @ w_in
    x_br, y_br, q, k, v = jnp.split(proj, list(AB_SPLITS), axis=-1)
    rec = rg_lru(causal_depthwise_conv(x_br, conv_w, conv_b), wa, ba, wx, bx, lam) * jax.nn.gelu(y_br)

    def heads(t):
        return t.reshape(Bsz, L, B_HEADS, HEAD_DIM).transpose(0, 2, 1, 3)

    q = partial_rope(heads(q), cos, sin)
    k = partial_rope(heads(k), cos, sin)
    att = dilated_attention(q, k, heads(v)).transpose(0, 2, 1, 3).reshape(Bsz, L, B_WIDTH)
    return jnp.concatenate([rec, att], axis=-1) @ w_out

def swa_sink_mixer(h, cos, sin, w_qkv, b_qkv, sinks, w_out, b_out):
    Bsz, L, _ = h.shape
    proj = h @ w_qkv + b_qkv
    q, k, v = jnp.split(proj, [C_Q_WIDTH, C_Q_WIDTH + C_KV_WIDTH], axis=-1)
    q = partial_rope(q.reshape(Bsz, L, C_HEADS, HEAD_DIM).transpose(0, 2, 1, 3), cos, sin)
    k = partial_rope(k.reshape(Bsz, L, C_KV_HEADS, HEAD_DIM).transpose(0, 2, 1, 3), cos, sin)
    v = v.reshape(Bsz, L, C_KV_HEADS, HEAD_DIM).transpose(0, 2, 1, 3)
    o, _ = banded_attention(q, k, v, C_WINDOW - 1, sinks)
    return o.transpose(0, 2, 1, 3).reshape(Bsz, L, C_Q_WIDTH) @ w_out + b_out

def memory_cross_attention(h, mem_n, wq, wkv, wo):
    Bsz, L, _ = h.shape
    M = mem_n.shape[1]
    q = (h @ wq).reshape(Bsz, L, XA_HEADS, XA_HEAD_DIM)
    k, v = jnp.split(mem_n @ wkv, 2, axis=-1)
    k = k.reshape(Bsz, M, XA_HEADS, XA_HEAD_DIM)
    v = v.reshape(Bsz, M, XA_HEADS, XA_HEAD_DIM)
    s = jnp.einsum('blhd,bmhd->bhlm', q, k).astype(jnp.float32) * (XA_HEAD_DIM ** -0.5)
    p = jax.nn.softmax(s, axis=-1)
    o = jnp.einsum('bhlm,bmhd->blhd', p.astype(v.dtype), v).reshape(Bsz, L, XA_WIDTH)
    return o @ wo

def swiglu(h, w_gate_up, w_down):
    gate, up = jnp.split(h @ w_gate_up, 2, axis=-1)
    return (jax.nn.silu(gate) * up) @ w_down

def setup_inputs(seed: int = 0) -> dict:
    key = jax.random.key(seed)
    ks = jax.random.split(key, 32)
    f32 = jnp.float32

    def nrm(k, shape, fan_in):
        return jax.random.normal(k, shape, f32) * (fan_in ** -0.5)

    def gain(k, shape):
        return 1.0 + 0.02 * jax.random.normal(k, shape, f32)

    def small(k, shape):
        return 0.01 * jax.random.normal(k, shape, f32)

    a_c = jax.random.uniform(ks[8], (N_EVEN, LRU_WIDTH), f32, 0.9, 0.999)
    a0 = a_c ** (1.0 / LRU_C)
    lru_lambda = jnp.log(a0) - jnp.log1p(-a0)

    return {
        "x": jax.random.normal(ks[0], (BATCH, SEQ, D_MODEL), f32),
        "mem": jax.random.normal(ks[1], (BATCH, N_MEM, D_MODEL), f32),
        "mix_norm": gain(ks[2], (DEPTH, D_MODEL)),
        "ab_w_in": nrm(ks[3], (N_EVEN, D_MODEL, AB_IN), D_MODEL),
        "lru_conv_w": nrm(ks[4], (N_EVEN, CONV_WIDTH, LRU_WIDTH), CONV_WIDTH),
        "lru_conv_b": small(ks[5], (N_EVEN, LRU_WIDTH)),
        "lru_wa": nrm(ks[6], (N_EVEN, LRU_HEADS, LRU_HEAD_DIM, LRU_HEAD_DIM), LRU_HEAD_DIM),
        "lru_ba": small(ks[7], (N_EVEN, LRU_HEADS, LRU_HEAD_DIM)),
        "lru_wx": nrm(ks[9], (N_EVEN, LRU_HEADS, LRU_HEAD_DIM, LRU_HEAD_DIM), LRU_HEAD_DIM),
        "lru_bx": small(ks[10], (N_EVEN, LRU_HEADS, LRU_HEAD_DIM)),
        "lru_lambda": lru_lambda,
        "ab_w_out": nrm(ks[11], (N_EVEN, AB_OUT, D_MODEL), AB_OUT),
        "c_w_qkv": nrm(ks[12], (N_ODD, D_MODEL, C_QKV), D_MODEL),
        "c_b_qkv": small(ks[13], (N_ODD, C_QKV)),
        "c_sinks": 0.5 * jax.random.normal(ks[14], (N_ODD, C_HEADS), f32),
        "c_w_out": nrm(ks[15], (N_ODD, C_Q_WIDTH, D_MODEL), C_Q_WIDTH),
        "c_b_out": small(ks[16], (N_ODD, D_MODEL)),
        "xa_norm": gain(ks[17], (DEPTH, D_MODEL)),
        "xa_mem_norm": gain(ks[18], (DEPTH, D_MODEL)),
        "xa_wq": nrm(ks[19], (DEPTH, D_MODEL, XA_WIDTH), D_MODEL),
        "xa_wkv": nrm(ks[20], (DEPTH, D_MODEL, 2 * XA_WIDTH), D_MODEL),
        "xa_wo": nrm(ks[21], (DEPTH, XA_WIDTH, D_MODEL), XA_WIDTH),
        "ffn_norm": gain(ks[22], (DEPTH, D_MODEL)),
        "ffn_w_gate_up": nrm(ks[23], (DEPTH, D_MODEL, 2 * D_FF), D_MODEL),
        "ffn_w_down": nrm(ks[24], (DEPTH, D_FF, D_MODEL), D_FF),
        "final_norm": gain(ks[25], (D_MODEL,)),
    }

def reference(x, mem, mix_norm, ab_w_in, lru_conv_w, lru_conv_b, lru_wa, lru_ba, lru_wx, lru_bx,
              lru_lambda, ab_w_out, c_w_qkv, c_b_qkv, c_sinks, c_w_out, c_b_out, xa_norm,
              xa_mem_norm, xa_wq, xa_wkv, xa_wo, ffn_norm, ffn_w_gate_up, ffn_w_down, final_norm):
    cos, sin = rope_tables(x.shape[1])
    h = x
    for layer in range(DEPTH):
        j = layer // 2
        hn = rms_norm(h, mix_norm[layer])
        if layer % 2 == 0:
            h = h + lru_dilated_mixer(hn, cos, sin, ab_w_in[j], lru_conv_w[j], lru_conv_b[j],
                                      lru_wa[j], lru_ba[j], lru_wx[j], lru_bx[j], lru_lambda[j],
                                      ab_w_out[j])
        else:
            h = h + swa_sink_mixer(hn, cos, sin, c_w_qkv[j], c_b_qkv[j], c_sinks[j],
                                   c_w_out[j], c_b_out[j])
        h = h + memory_cross_attention(rms_norm(h, xa_norm[layer]), rms_norm(mem, xa_mem_norm[layer]),
                                       xa_wq[layer], xa_wkv[layer], xa_wo[layer])
        h = h + swiglu(rms_norm(h, ffn_norm[layer]), ffn_w_gate_up[layer], ffn_w_down[layer])
    return rms_norm(h, final_norm)


_drawn_inputs = setup_inputs


def setup_inputs(seed=0):
    import zlib

    import numpy as np

    out = dict(_drawn_inputs(seed))
    spreads = {}
    factors = {'mix_norm': 4.425,
     'lru_ba': 8.0,
     'lru_bx': 8.0,
     'c_b_qkv': 6.196,
     'c_sinks': 24.403,
     'c_b_out': 18.15,
     'xa_norm': 8.0,
     'xa_mem_norm': 8.0,
     'ffn_norm': 2.81,
     'final_norm': 7.865}
    for name, (base, spread) in spreads.items():
        noise = np.random.default_rng([zlib.crc32(name.encode()), seed]).standard_normal(out[name].shape)
        drawn = base * np.exp(spread * noise) if base else spread * noise
        out[name] = __import__('jax').numpy.asarray(drawn.astype(out[name].dtype))
    for name, factor in factors.items():
        out[name] = (out[name] * factor).astype(out[name].dtype)
    return out
```

```python
import concourse.bass as bass
from concourse import mybir
from contextlib import ExitStack

F32 = mybir.dt.float32
F32R = mybir.dt.float32r
ALU = mybir.AluOpType
ACT = mybir.ActivationFunctionType
AX = mybir.AxisListType

P = 128
T = 512
D = 1024
DB = D // P
TB = T // P
M = 256
MB = M // P
LRU_HEADS = 4
B_HEADS = 8
C_HEADS = 16
HD = 64
XH = 4
D_FF = 2816
EPS = 1e-6
LRU_C = 8.0
CONV = 4
NEG = -1e30
BANK = 512
RAW = 4
SPLIT = 2
CHUNK = (12, 10)

STAGES = [("x_t", 2, 0), ("in_xy", 4, 4), ("mem_t0", 1, 0), ("gates", 4, 1), ("in_qkv", 3, 4),
          ("mem_k0", 1, 4), ("mem_v0", 1, 4), ("attn0", 2, 0), ("out0", 2, 6)]
for _l in (0, 1):
    if _l:
        STAGES += [("qkv_q", 2, 4), ("qkv_kv", 1, 2), ("mem_t1", 1, 0), ("mem_k1", 1, 4), ("mem_v1", 1, 4),
                   ("attn1", 2, 0), ("out1", 2, 4)]
    STAGES += [(f"xq{_l}", 1, 4), (f"xattn{_l}", 2, 0), (f"xo{_l}", 2, 2),
               (f"up{_l}0", CHUNK[0] // 2, 4), (f"down{_l}0", 2, CHUNK[0] // 2),
               (f"up{_l}1", CHUNK[1] // 2, 4), (f"down{_l}1", 2, CHUNK[1] // 2)]
STAGES.append(("final", 2, 0))
GROUP0, UNIT0, GROUPS = {}, {}, {}
_g = _u = 0
for _n, _ng, _nu in STAGES:
    GROUP0[_n], UNIT0[_n], GROUPS[_n] = _g, _u, _ng
    _g += _ng
    _u += _ng * _nu
UNITS = _u

NORMS = ("mix0", "xa0", "ffn0", "mix1", "xa1", "ffn1", "final")
NORM = {n: i for i, n in enumerate(NORMS)}
COL = {}
_c = 0
for _n, _w in [(f"g_{n}", DB) for n in NORMS] + [("g_mem0", DB), ("g_mem1", DB), ("conv_w", CONV * DB), ("conv_b", DB),
                                                ("ba", DB), ("bx", DB), ("lam", DB), ("b_qkv", 10), ("b_out", DB),
                                                ("sinks", C_HEADS), ("eps", 1)]:
    COL[_n] = _c
    _c += _w
NCOL = _c


def attention_plan(kind):
    if kind == "xattn":
        scores = [(i, 0, M, M * i) for i in range(TB)]
        return dict(width=TB * M, scores=scores, reduces=[(0, TB, M)], masks=[], probs=[(M * i, M) for i in range(TB)],
                    turns=[(M * i + P * j, BANK * j + P * i) for j in range(MB) for i in range(TB)],
                    t_width=MB * BANK, values=[(j, BANK * j, 0, T, j == 0) for j in range(MB)])
    if kind == "attn1":
        start = [2 * P * i + (P if i == 0 else 0) for i in range(TB)]
        scores = [(i, max(i - 1, 0) * P, P if i == 0 else 2 * P, start[i]) for i in range(TB)]
        blocks = [(0, 0)] + [(i, j) for i in range(1, TB) for j in (i - 1, i)]
        return dict(width=TB * 2 * P, scores=scores, reduces=[(P, 1, P), (2 * P, TB - 1, 2 * P)],
                    masks=[(P, (2 * TB - 1) * P, P)], probs=[(start[i], P if i == 0 else 2 * P) for i in range(TB)],
                    turns=[(2 * P * i + P * (j - i + 1), P * n) for n, (i, j) in enumerate(blocks)],
                    t_width=len(blocks) * P,
                    values=[(j, P * n, P * i, P, n == 0) for n, (i, j) in enumerate(blocks)])
    start = [0, P, BANK, 2 * BANK]
    t_start = [0, BANK, 2 * BANK, BANK + 3 * P]
    return dict(width=3 * BANK, scores=[(i, 0, P * (i + 1), start[i]) for i in range(TB)],
                reduces=[(start[i], 1, P * (i + 1)) for i in range(TB)],
                masks=[(start[i], P * (i + 1), (TB - 1 - i) * P) for i in range(TB)],
                probs=[(start[i], P * (i + 1)) for i in range(TB)],
                turns=[(start[i] + P * j, t_start[j] + P * (i - j)) for j in range(TB) for i in range(j, TB)],
                t_width=2 * BANK + 2 * P,
                values=[(j, t_start[j], P * j, T - P * j, j == 0) for j in range(TB)])


def trunk(nc, x, mem, w_in, w_gates, w_out0, w_qkv, w_out1, xa_wq, xa_wkv, xa_wo, w_gate_up, w_down,
          vectors, mask0, mask1, rope_cos, rope_sin, identity, out):
    ctx = ExitStack()
    with ctx:
        base = 16512
        top = [base]

        def at(name, shape, dt, offset):
            return nc.alloc_sbuf_tensor_at(name, shape, dt, offset=offset)

        def zone(nbytes):
            top[0] += nbytes
            return top[0] - nbytes

        z_h = zone(4 * DB * T)
        z_zh, z_zl = zone(4 * DB * T), zone(4 * DB * T)
        z_raw = zone(RAW * 4096)
        z_wh, z_wl = zone(SPLIT * 4096), zone(SPLIT * 4096)
        z_fh, z_fl = zone(4 * CHUNK[0] * T), zone(4 * CHUNK[0] * T)
        z_x, z_y = zone(4 * DB * T), zone(4 * DB * T)
        z_q, z_k, z_v = zone(8192), zone(8192), zone(8192)
        z_mk, z_mv = zone(4096), zone(4096)
        z_const = zone(0)

        h = at("h", [P, DB, T], F32, z_h)
        z_hi = at("z_hi", [P, DB, T], F32R, z_zh)
        z_lo = at("z_lo", [P, DB, T], F32R, z_zl)
        raw = at("raw", [P, RAW, 2, 512], F32, z_raw)
        w_hi = at("w_hi", [P, SPLIT, 2, 512], F32R, z_wh)
        w_lo = at("w_lo", [P, SPLIT, 2, 512], F32R, z_wl)
        f_hi = at("f_hi", [P, CHUNK[0], T], F32R, z_fh)
        f_lo = at("f_lo", [P, CHUNK[0], T], F32R, z_fl)
        lru_r = at("lru_r", [P, DB, T], F32, z_fh)
        lru_a = at("lru_a", [P, DB, T], F32, z_fl)
        mem_hi = f_hi[:, 8:12, :].rearrange("p a (b n) -> p (a b) n", n=M)
        mem_lo = f_lo[:, 8:12, :].rearrange("p a (b n) -> p (a b) n", n=M)
        xc = at("xc", [P, DB, T], F32, z_x)
        q1 = at("q1", [P, DB, T], F32, z_x)
        x_nat = at("x_nat", [P, TB, D], F32, z_y)
        yg = at("yg", [P, DB, T], F32, z_y)
        ff_g = at("ff_g", [P, 2, T], F32, z_y)
        ff_u = at("ff_u", [P, 2, T], F32, z_y + 4096)
        rope1 = [at(f"rope1_{i}", [P, T], F32, z_y + 2048 * i) for i in range(3)]
        mem_nat1 = at("mem_nat1", [P, MB, D], F32, z_y + 8192)
        mem_nat0 = at("mem_nat0", [P, MB, D], F32, z_q)
        q0 = at("q0", [P, 4, T], F32, z_q)
        qx = at("qx", [P, 4, T], F32, z_q)
        xpad = [at(f"xpad{i}", [P, T + CONV], F32, z_k + 2080 * i) for i in range(2)]
        y_in = at("y_in", [P, T], F32, z_k + 4160)
        k0 = at("k0", [P, 4, T], F32, z_k)
        k1 = at("k1", [P, 2, T], F32, z_k)
        m1 = at("m1", [P, 2 * TB * P], F32, z_k + 4096)
        rope0 = [at(f"rope0_{i}", [P, T], F32, z_v + 2048 * i) for i in range(3)]
        v0 = at("v0", [P, TB, 512], F32, z_v)
        k1_rot = at("k1_rot", [P, T], F32, z_v)
        v1_t = at("v1_t", [P, T], F32, z_v + 2048)
        v1 = at("v1", [P, TB, P], F32, z_v + 4096)
        mk = at("mk", [P, XH, M], F32, z_mk)
        mv = at("mv", [P, MB, 512], F32, z_mv)
        gate_i = at("gate_i", [P, 2, T], F32, z_mk)
        lru_d = at("lru_d", [P, 2, T], F32, z_mv)
        v0_t = at("v0_t", [P, 4, T], F32, z_zh + 18432)
        prob = [at(f"prob{i}", [P, 3 * BANK], F32, z_zh + 6144 * i) for i in range(3)]
        m0 = at("m0", [P, TB * P], F32, z_zh + 30720)
        prob_t = [at(f"prob_t{i}", [P, 3 * BANK], F32, z_zh + 18432 + 6144 * i) for i in range(2)]
        y_t = at("y_t", [P, DB, T], F32, z_zh)
        y_out = at("y_out", [P, TB, D], F32, z_zl)
        sq = at("sq", [P, 2, T], F32, z_const)
        acc = at("acc", [P, T], F32, z_const + 4096)
        rstd = at("rstd", [P, T], F32, z_const + 6144)
        ident = at("ident", [P, P], F32, z_const + 8192)
        ones = at("ones", [P, P], F32, z_const + 8704)
        vec = at("vec", [P, NCOL], F32, z_const + 9216)
        z_small = z_const + 9216 + (4 * NCOL + 31) // 32 * 32
        small = at("small", [P, 8 * 8], F32, z_small)
        stat = at("stat", [P, 3, 6, TB], F32, z_small + 256)
        cos_t = at("cos_t", [P, T], F32, z_small + 544)
        sin_t = at("sin_t", [P, T], F32, z_small + 2592)
        assert z_small + 4640 <= nc.sbuf_usable_end, (z_small + 4640, nc.sbuf_usable_end)

        ps = ctx.enter_context(nc.psum_tensor("ps", [P, 8, BANK], F32))
        flat = ps[:, :, :].rearrange("p b n -> p (b n)")

        def bank(group, m):
            return (group % 2) * 4 + m

        def sem(name):
            return ctx.enter_context(nc.semaphore(name))

        def v(name, m=0, n=1):
            return vec[:, COL[name] + m:COL[name] + m + n]

        s_ident, s_vec, s_x, s_rope, s_mask0, s_mask1 = [sem(n) for n in
                                                      ("s_ident", "s_vec", "s_x", "s_rope", "s_mask0", "s_mask1")]
        s_mem = [sem("s_mem0"), sem("s_mem1")]
        s_raw = [sem(f"s_raw{i}") for i in range(RAW)]
        s_begun = sem("s_weight_begun")
        s_hi = sem("s_weight_hi")
        s_split = sem("s_weight_split")
        s_used = sem("s_weight_used")
        s_free = [sem("s_banks_free0"), sem("s_banks_free1")]
        s_done = {n: sem(f"s_done_{n}") for n, _, _ in STAGES if n[:2] not in ("up", "do") and "attn" not in n}
        s_done |= {f"down{l}{c}": sem(f"s_done_down{l}{c}") for l in (0, 1) for c in (0, 1)}
        s_ff = sem("s_ff_tiles")
        s_ff_gate, s_ff_silu, s_ff_up = sem("s_ff_gate"), sem("s_ff_silu"), sem("s_ff_up")
        s_ff_prod, s_ff_hi, s_ff_lo = sem("s_ff_prod"), sem("s_ff_hi"), sem("s_ff_lo")
        s_h = sem("s_h")
        s_sq = sem("s_sq")
        s_acc = sem("s_acc")
        s_zh = sem("s_z_hi")
        s_zl = sem("s_z_lo")
        s_sum = sem("s_sum")
        s_rms = sem("s_rms")
        s_rstd = sem("s_rstd")
        s_dve, s_act = sem("s_dve_chain"), sem("s_act_chain")
        s_const = sem("s_const")
        s_xp, s_c0, s_xc = sem("s_x_scaled"), sem("s_conv_first"), sem("s_conv")
        s_xch, s_xcl = sem("s_conv_hi"), sem("s_conv_lo")
        s_y, s_yg = sem("s_y_scaled"), sem("s_gelu")
        s_sp_e, s_sp = sem("s_exp_lambda"), sem("s_softplus")
        s_gate, s_gx = sem("s_gate_i"), sem("s_gated_input")
        s_at, s_lq, s_ls = sem("s_decay"), sem("s_one_minus_a2"), sem("s_input_scale")
        s_rec, s_rech, s_recl = sem("s_rec"), sem("s_rec_hi"), sem("s_rec_lo")
        s_q0, s_v0t, s_v0p, s_v0 = sem("s_qk0"), sem("s_v0_t"), sem("s_v0_turned"), sem("s_v0")
        s_q1, s_v1p, s_v1, s_k1 = sem("s_qkv1"), sem("s_v1_turned"), sem("s_v1"), sem("s_k1")
        s_ms, s_mr, s_mn = [sem("s_ms0"), sem("s_ms1")], [sem("s_mr0"), sem("s_mr1")], [sem("s_mn0"), sem("s_mn1")]
        s_mh, s_ml = [sem("s_mh0"), sem("s_mh1")], [sem("s_ml0"), sem("s_ml1")]
        s_mkv = [sem("s_mkv0"), sem("s_mkv1")]
        s_xq = [sem("s_xq0"), sem("s_xq1")]
        s_fin, s_fin_o, s_out = sem("s_final_t"), sem("s_final_out"), sem("s_out")

        ATTN = {}
        for name, heads, plan, tiles in (("attn0", B_HEADS, "attn0", 4), ("xattn0", XH, "xattn", 4),
                                         ("attn1", C_HEADS, "attn1", 8), ("xattn1", XH, "xattn", 4)):
            a = dict(name=name, heads=heads, tiles=tiles, per=heads // tiles, **attention_plan(plan))
            a["s_bufs"] = 1 if plan == "attn0" else 2
            a["t_bank"] = 3 if plan == "attn0" else 4
            a["scale"] = P ** -0.5 if plan == "xattn" else HD ** -0.5
            a["sink"] = plan == "attn1"
            a["tile0"] = 8 if plan == "attn0" else 0
            for s in ("scores", "read", "max", "exp", "prob", "turned", "pt", "head", "o_hi", "o_lo"):
                a["s_" + s] = sem(f"s_{name}_{s}")
            ATTN[name] = a

        class Chain:
            def __init__(self, eng, s):
                self.eng, self.s, self.n = eng, s, 0

            def link(self, ins):
                self.n += 1
                ins.then_inc(self.s, 1)
                self.eng.wait_ge(self.s, self.n)

        def loop(eng, count, body):
            if count == 1:
                body(0)
            elif count > 1:
                with eng.Fori(0, count) as i:
                    body(i)

        def free_needed(group):
            return 4 * (group // 2)

        block = ctx.enter_context(nc.Block())

        @block.sync
        def _(sp):
            sp.dma_start(ident[:], identity).then_inc(s_ident, 16)
            for t in range(TB):
                sp.dma_start(x_nat[:, t, :], x[t * P:(t + 1) * P, :]).then_inc(s_x, 16)
            sp.dma_start(vec[:], vectors).then_inc(s_vec, 16)
            seen = [0]

            def unit(u, parts):
                u_static = seen[0]
                seen[0] += 1
                if u_static >= RAW:
                    sp.wait_ge(s_split, u - RAW + 1)
                for lo, hi, src in parts:
                    sp.dma_start(raw[:, u_static % RAW, :, lo:hi], src).then_inc(s_raw[u_static % RAW], 32 // len(parts))

            def rows(w, r0, col, n=512):
                return w[r0:r0 + 2 * P, bass.ds(col, n)].rearrange("(a p) n -> p a n", p=P)

            def stream(name, w, units, col0=0, first=0, count=None):
                n = GROUPS[name] if count is None else count
                u0 = UNIT0[name] + first * units

                def body(i):
                    keep = seen[0]
                    for j in range(units):
                        unit(u0 + units * i + j, [(0, 512, rows(w, 2 * P * j, (first + i) * 512 + col0))])
                    seen[0] = keep + units
                if units % RAW == 0:
                    loop(sp, n, body)
                    seen[0] = u0 + n * units
                else:
                    for i in range(n):
                        body(i)

            def ff(l, c):
                u0 = UNIT0[f"up{l}{c}"]
                f0 = sum(CHUNK[:c]) * P

                def body(i):
                    for j in range(4):
                        unit(u0 + 4 * i + j, [(0, 256, rows(w_gate_up[l], 2 * P * j, i * 256 + f0, 256)),
                                              (256, 512, rows(w_gate_up[l], 2 * P * j, i * 256 + f0 + D_FF, 256))])
                loop(sp, CHUNK[c] // 2, body)
                seen[0] = UNIT0[f"down{l}{c}"]
                stream(f"down{l}{c}", w_down[l][f0:f0 + CHUNK[c] * P, :], CHUNK[c] // 2)

            for j in range(4):
                unit(j, [(0, 512, rows(w_in, 2 * P * j, 0))])
            sp.dma_start(mem_nat0[:], mem.rearrange("(a p) n -> p a n", p=P)).then_inc(s_mem[0], 16)
            stream("in_xy", w_in, 4, first=1, count=3)
            sp.dma_start(cos_t[:], rope_cos).then_inc(s_rope, 16)
            sp.dma_start(sin_t[:], rope_sin).then_inc(s_rope, 16)
            for hd in range(LRU_HEADS):
                unit(UNIT0["gates"] + hd, [(0, 256, w_gates[0][hd].rearrange("(a p) n -> p a n", p=P)),
                                           (256, 512, w_gates[1][hd].rearrange("(a p) n -> p a n", p=P))])
            stream("in_qkv", w_in, 4, col0=2 * D)
            for l in (0, 1):
                if l:
                    stream("qkv_q", w_qkv, 4)
                    for j in range(2):
                        src = w_qkv[4 * P * j:4 * P * (j + 1), D:D + 256].rearrange("(a p) n -> p a n", p=P)
                        unit(UNIT0["qkv_kv"] + j, [(0, 256, src[:, 0:2, :]), (256, 512, src[:, 2:4, :])])
                    sp.wait_ge(s_recl, DB)
                    sp.dma_start(mem_nat1[:], mem.rearrange("(a p) n -> p a n", p=P)).then_inc(s_mem[1], 16)
                    sp.wait_ge(ATTN["attn0"]["s_scores"], B_HEADS)
                    sp.dma_start(m1[:], mask1).then_inc(s_mask1, 16)
                stream(f"mem_k{l}", xa_wkv[l], 4)
                stream(f"mem_v{l}", xa_wkv[l], 4, col0=512)
                if l == 0:
                    sp.wait_ge(s_done["in_qkv"], 12)
                    sp.dma_start(m0[:], mask0).then_inc(s_mask0, 16)
                stream(f"out{l}", (w_out0, w_out1)[l], (6, 4)[l])
                stream(f"xq{l}", xa_wq[l], 4)
                stream(f"xo{l}", xa_wo[l], 2)
                ff(l, 0)
                ff(l, 1)
            assert seen[0] == UNITS
            for c in range(4):
                sp.wait_ge(s_fin_o, 2 * (c + 1))
                sp.dma_start(out.rearrange("(t p) n -> p t n", p=P)[:, :, 256 * c:256 * (c + 1)],
                             y_out[:, :, 256 * c:256 * (c + 1)]).then_inc(s_out, 16)
            sp.wait_ge(s_out, 64)

        @block.gpsimd
        def _(pool):
            def split(u, j, peeled):
                slot, half = j % RAW, j % SPLIT
                pool.wait_ge(s_raw[slot], (u - j + RAW) * (32 // RAW) + (j - slot) * (32 // RAW))
                if not (peeled and j < SPLIT):
                    pool.wait_ge(s_used, u - SPLIT + 2)
                pool.sem_inc(s_begun, 1)
                pool.tensor_scalar(w_hi[:, half], raw[:, slot], 1.0, 1.0, ALU.mult, ALU.mult).then_inc(s_hi, 1)
                pool.wait_ge(s_hi, u + 1)
                pool.tensor_tensor(w_lo[:, half], raw[:, slot], w_hi[:, half].bitcast(F32),
                                   ALU.subtract).then_inc(s_split, 1)

            for j in range(RAW):
                split(j, j, True)

            def body(i):
                for j in range(RAW):
                    split(i * RAW + (RAW + j), j, False)
            loop(pool, UNITS // RAW - 1, body)
            for u in range(UNITS // RAW * RAW, UNITS):
                split(u, u % RAW, False)

        @block.tensor
        def _(pe):
            def product(o, half, kk, c0, c1, rhi, rlo, start, stop, unit_starts):
                whi, wlo = w_hi[:, half, kk, c0:c1], w_lo[:, half, kk, c0:c1]
                ins = pe.matmul(o, whi, rhi, start=start, stop=False)
                if unit_starts:
                    ins.then_inc(s_used, 1)
                pe.matmul(o, whi, rlo, start=False, stop=False)
                return pe.matmul(o, wlo, rhi, start=False, stop=stop)

            def group(g_static, g, u0_static, u0, units, rhs, done, n=T, before=None, hook=None):
                for j in range(units):
                    if before:
                        before(2 * j + 1)
                    if j == 0 and g_static >= 2:
                        pe.wait_ge(s_free[g_static % 2], 4 * (g_static // 2) + (g - g_static) * 2)
                    pe.wait_ge(s_split, u0 + j + 1)
                    half = (u0_static + j) % SPLIT
                    for m in range(4):
                        for kk in range(2):
                            k = 2 * j + kk
                            hi, lo = rhs(k)
                            ins = product(ps[:, bank(g_static, m), 0:n], half, kk, P * m, P * (m + 1), hi, lo,
                                          k == 0, k == 2 * units - 1, m == 0 and kk == 0)
                        if j == units - 1:
                            ins.then_inc(done, 1)
                    if hook and j == min(1, units - 1):
                        hook()

            def stage(name, units, rhs, done, ready=None, norm=None, n=T):
                g0, u0, ng = GROUP0[name], UNIT0[name], GROUPS[name]
                hook = (lambda: norm_sum(norm, g0 + 1)) if norm else None
                group(g0, g0, u0, u0, units, rhs, done, n, before=ready, hook=hook)
                if norm and ng > 1:
                    pe.wait_ge(s_rms, NORM[norm] + 1)
                rest, at_g, at_u = ng - 1, g0 + 1, u0 + units

                def body(i):
                    for s in range(2):
                        group(at_g + s, at_g + s + 2 * i, at_u + units * s, at_u + units * s + 2 * units * i,
                              units, rhs, done, n)
                if units % SPLIT == 0:
                    if rest // 2:
                        loop(pe, rest // 2, body)
                    if rest % 2:
                        group(at_g + rest - 1, at_g + rest - 1, at_u + units * (rest - 1),
                              at_u + units * (rest - 1), units, rhs, done, n)
                else:
                    for s in range(rest):
                        group(at_g + s, at_g + s, at_u + units * s, at_u + units * s, units, rhs, done, n)

            def norm_sum(norm, g):
                pe.wait_ge(s_acc, NORM[norm] + 1)
                pe.wait_ge(s_free[g % 2], free_needed(g))
                pe.matmul(ps[:, bank(g, 0), :], ones[:], acc[:], start=True, stop=True).then_inc(s_sum, 1)

            def z(k):
                return z_hi[:, k, :], z_lo[:, k, :]

            def f(k):
                return f_hi[:, k, :], f_lo[:, k, :]

            def z_ready(norm):
                return lambda k: pe.wait_ge(s_zl, NORM[norm] * DB + k + 1)

            def attention(a, q, key, value, ready, o_ready):
                g = GROUP0[a["name"]]
                for s in range(2):
                    pe.wait_ge(s_free[(g + s) % 2], free_needed(g + s))
                ready()

                def scores(n):
                    if n >= a["s_bufs"]:
                        pe.wait_ge(a["s_read"], n - a["s_bufs"] + 1)
                    b0 = 2 * BANK * (n % a["s_bufs"])
                    for i, k0_, nk, c in a["scores"]:
                        ins = pe.matmul(flat[:, b0 + c:b0 + c + nk], q(n)[:, i * P:(i + 1) * P],
                                        key(n)[:, k0_:k0_ + nk], start=True, stop=True)
                    ins.then_inc(a["s_scores"], 1)

                def turns(n):
                    pe.wait_ge(a["s_prob"], n + 1)
                    if n >= 1:
                        pe.wait_ge(a["s_pt"], n)
                    else:
                        o_ready()
                    t0 = a["t_bank"] * BANK
                    for src, dst in a["turns"]:
                        ins = pe.transpose(flat[:, t0 + dst:t0 + dst + P], prob[n % 3][:, src:src + P], ident[:])
                    ins.then_inc(a["s_turned"], 1)

                def values(n):
                    pe.wait_ge(a["s_pt"], n + 1)
                    tile = n // a["per"]
                    if n % a["per"] == 0 and tile >= 2:
                        pe.wait_ge(a["s_o_lo"], tile - 1)
                    rows = P // a["per"]
                    r0 = rows * (n % a["per"])
                    o = ps[r0:r0 + rows, 6 + tile % 2, :]
                    last = len(a["values"]) - 1
                    for x_, (j, src, q0_, nq, start) in enumerate(a["values"]):
                        ins = pe.matmul(o[:, q0_:q0_ + nq], value(n, j), prob_t[n % 2][:, src:src + nq],
                                        start=start, stop=x_ == last)
                    ins.then_inc(a["s_head"], 1)

                for n in range(a["heads"] + 3):
                    if n < a["heads"]:
                        scores(n)
                    if n >= 3:
                        values(n - 3)
                    if 2 <= n < a["heads"] + 2:
                        turns(n - 2)

            def turn_memory(l):
                name = f"mem_t{l}"
                g = GROUP0[name]
                src = (mem_nat0, mem_nat1)[l]
                pe.wait_ge(s_mn[l], MB)
                pe.wait_ge(s_free[g % 2], free_needed(g))
                for b in range(4):
                    for m in range(2 * b, 2 * b + 2):
                        for t in range(MB):
                            ins = pe.transpose(ps[:, bank(g, b), (m % 2) * M + t * P:(m % 2) * M + (t + 1) * P],
                                               src[:, t, m * P:(m + 1) * P], ident[:])
                    ins.then_inc(s_done[name], 1)

            def memory_kv(l):
                stage(f"mem_k{l}", 4, lambda k: (mem_hi[:, k, :], mem_lo[:, k, :]), s_done[f"mem_k{l}"],
                      ready=lambda k: pe.wait_ge(s_ml[l], k + 1), n=M)
                g, u0 = GROUP0[f"mem_v{l}"], UNIT0[f"mem_v{l}"]
                pe.wait_ge(s_free[g % 2], free_needed(g))
                for j in range(4):
                    pe.wait_ge(s_split, u0 + j + 1)
                    half = (u0 + j) % SPLIT
                    for t in range(MB):
                        o = ps[:, bank(g, t), :]
                        for kk in range(2):
                            k = 2 * j + kk
                            mh, ml = mem_hi[:, k, t * P:(t + 1) * P], mem_lo[:, k, t * P:(t + 1) * P]
                            ins = pe.matmul(o, mh, w_hi[:, half, kk, :], start=k == 0, stop=False)
                            if t == 0 and kk == 0:
                                ins.then_inc(s_used, 1)
                            pe.matmul(o, mh, w_lo[:, half, kk, :], start=False, stop=False)
                            ins = pe.matmul(o, ml, w_hi[:, half, kk, :], start=False, stop=k == DB - 1)
                        if j == 3:
                            ins.then_inc(s_done[f"mem_v{l}"], 1)

            pe.wait_ge(s_ident, 16)
            pe.wait_ge(s_x, 16 * TB)
            for m in range(DB):
                for t in range(TB):
                    ins = pe.transpose(ps[:, m, t * P:(t + 1) * P], x_nat[:, t, m * P:(m + 1) * P], ident[:])
                ins.then_inc(s_done["x_t"], 1)
            pe.wait_ge(s_const, 1)
            stage("in_xy", 4, z, s_done["in_xy"], ready=z_ready("mix0"), norm="mix0")
            turn_memory(0)
            for hd in range(LRU_HEADS):
                g, u0 = GROUP0["gates"] + hd, UNIT0["gates"] + hd
                group(g, g, u0, u0, 1, lambda k: f(2 * hd + k), s_done["gates"],
                      before=lambda k: pe.wait_ge(s_xcl, 2 * hd + k + 1))
            stage("in_qkv", 4, z, s_done["in_qkv"])
            memory_kv(0)

            a = ATTN["attn0"]

            def turn_v0():
                pe.wait_ge(s_v0t, 4)
                for j in range(TB):
                    for c in range(4):
                        ins = pe.transpose(ps[:, 4 + j, c * P:(c + 1) * P], v0_t[:, c, j * P:(j + 1) * P], ident[:])
                    ins.then_inc(s_v0p, 1)
                pe.wait_ge(s_q0, 8)

            attention(a, lambda n: q0[HD * (n % 2):HD * (n % 2) + HD, n // 2, :],
                      lambda n: k0[HD * (n % 2):HD * (n % 2) + HD, n // 2, :],
                      lambda n, j: v0[:, j, HD * n:HD * n + HD], turn_v0, lambda: pe.wait_ge(s_v0, 4))

            def mixer_ready(k):
                pe.wait_ge(s_recl, min(k + 1, DB))
                if k >= DB:
                    pe.wait_ge(a["s_o_lo"], k - DB + 1)
            stage("out0", 6, f, s_done["out0"], ready=mixer_ready)

            for l in (0, 1):
                if l:
                    stage("qkv_q", 4, z, s_done["qkv_q"], ready=z_ready("mix1"), norm="mix1")
                    g, u0 = GROUP0["qkv_kv"], UNIT0["qkv_kv"]
                    pe.wait_ge(s_free[g % 2], free_needed(g))
                    for j in range(2):
                        pe.wait_ge(s_split, u0 + j + 1)
                        half = (u0 + j) % SPLIT
                        for m in range(2):
                            for q_ in range(4):
                                k = 4 * j + q_
                                c0 = 256 * (q_ // 2) + P * m
                                ins = product(ps[:, bank(g, m), :], half, q_ % 2, c0, c0 + P, *z(k), k == 0, k == DB - 1,
                                              m == 0 and q_ == 0)
                            if j == 1:
                                ins.then_inc(s_done["qkv_kv"], 1)
                    turn_memory(1)
                    memory_kv(1)

                    def turn_v1():
                        pe.wait_ge(s_q1, 10)
                        for j in range(TB):
                            ins = pe.transpose(ps[:, 4, j * P:(j + 1) * P], v1_t[:, j * P:(j + 1) * P], ident[:])
                        ins.then_inc(s_v1p, 1)
                        pe.wait_ge(s_k1, 4)

                    a1 = ATTN["attn1"]
                    attention(a1, lambda n: q1[HD * (n % 2):HD * (n % 2) + HD, n // 2, :],
                              lambda n: k1[HD * (n % 2):HD * (n % 2) + HD, n // 8, :],
                              lambda n, j: v1[:, j, HD * (n // 8):HD * (n // 8) + HD], turn_v1,
                              lambda: pe.wait_ge(s_v1, 1))
                    stage("out1", 4, f, s_done["out1"], ready=lambda k: pe.wait_ge(a1["s_o_lo"], k + 1))

                stage(f"xq{l}", 4, z, s_done[f"xq{l}"], ready=z_ready(f"xa{l}"), norm=f"xa{l}")
                ax = ATTN[f"xattn{l}"]

                def x_ready():
                    pe.wait_ge(s_xq[l], 4)
                    pe.wait_ge(s_mkv[l], 6)
                attention(ax, lambda n: qx[:, n, :], lambda n: mk[:, n, :],
                          lambda n, j: mv[:, j, P * n:P * (n + 1)], x_ready, lambda: None)
                stage(f"xo{l}", 2, f, s_done[f"xo{l}"], ready=lambda k: pe.wait_ge(ax["s_o_lo"], k + 1))
                for c in range(2):
                    stage(f"up{l}{c}", 4, z, s_ff, ready=z_ready(f"ffn{l}") if c == 0 else None,
                          norm=f"ffn{l}" if c == 0 else None)
                    tiles = D_FF // P * l + sum(CHUNK[:c])
                    stage(f"down{l}{c}", CHUNK[c] // 2, f, s_done[f"down{l}{c}"],
                          ready=lambda k: pe.wait_ge(s_ff_lo, tiles + k + 1))

            g = GROUP0["final"]
            pe.wait_ge(s_free[(g + 1) % 2], free_needed(g + 1))
            norm_sum("final", g)
            for m in range(DB):
                pe.wait_ge(s_zl, NORM["final"] * DB + m + 1)
                for t in range(TB):
                    ins = pe.transpose(ps[:, m, t * P:(t + 1) * P], y_t[:, m, t * P:(t + 1) * P], ident[:])
                ins.then_inc(s_fin, 1)

        @block.vector
        def _(dve):
            chain = Chain(dve, s_dve)
            link = chain.link

            def residual(norm, done, first=False, bias=None, group0=0, norm_next=True):
                def low(m):
                    if norm != "final":
                        dve.wait_ge(s_zh, NORM[norm] * DB + m + 1)
                        dve.scalar_tensor_tensor(z_lo[:, m, :], h[:, m, :], v(f"g_{norm}", m), z_hi[:, m, :].bitcast(F32),
                                                 ALU.mult, ALU.subtract).then_inc(s_zl, 1)
                    dve.wait_ge(s_sq, NORM[norm] * DB + m + 1)
                    if m == 0:
                        link(dve.tensor_copy(acc[:], sq[:, 0, :]))
                    elif m < DB - 1:
                        link(dve.tensor_tensor(acc[:], acc[:], sq[:, m % 2, :], ALU.add))
                    else:
                        dve.tensor_tensor(acc[:], acc[:], sq[:, m % 2, :], ALU.add).then_inc(s_acc, 1)

                for m in range(DB):
                    dve.wait_ge(done, m + 1)
                    b = bank(group0 + m // 4, m % 4)
                    if first:
                        ins = dve.tensor_copy(h[:, m, :], ps[:, b, :])
                    elif bias:
                        ins = dve.scalar_tensor_tensor(h[:, m, :], ps[:, b, :], v(bias, m), h[:, m, :], ALU.add, ALU.add)
                    else:
                        ins = dve.tensor_tensor(h[:, m, :], ps[:, b, :], h[:, m, :], ALU.add)
                    link(ins)
                    dve.nop().then_inc(s_free[b // 4], 1)
                    if norm_next:
                        dve.nop().then_inc(s_h, 1)
                        if m >= 1:
                            low(m - 1)
                if norm_next:
                    low(DB - 1)

            def one_over_rms(norm):
                dve.wait_ge(s_rms, NORM[norm] + 1)
                dve.reciprocal(rstd[:], sq[:, 0, :]).then_inc(s_rstd, 1)
                dve.wait_ge(s_rstd, NORM[norm] + 1)

            def scaled(dst, g, m, done, count):
                dve.wait_ge(done, count)
                b = bank(g, m)
                link(dve.tensor_tensor(dst, ps[:, b, :], rstd[:], ALU.mult))
                dve.nop().then_inc(s_free[b // 4], 1)

            def rotate(dst, tmp, done_sem):
                swap = list(range(8, 16)) + list(range(8)) + list(range(16, 32))
                link(dve.stream_shuffle(tmp[1][:], tmp[0][:], swap))
                dve.tensor_tensor(tmp[2][:], tmp[0][:], cos_t[:], ALU.mult)
                link(dve.tensor_tensor(tmp[1][:], tmp[1][:], sin_t[:], ALU.mult))
                dve.tensor_tensor(dst, tmp[2][:], tmp[1][:], ALU.add).then_inc(done_sem, 1)

            def memory_norm(l):
                src = (mem_nat0, mem_nat1)[l]
                dve.wait_ge(s_mr[l], 1)
                link(dve.reciprocal(small[:, 2:4], small[:, 0:2]))
                for t in range(MB):
                    dve.tensor_scalar(src[:, t, :], src[:, t, :], small[:, 2 + t:3 + t], None,
                                      ALU.mult).then_inc(s_mn[l], 1)

            def memory_low(l):
                g = GROUP0[f"mem_t{l}"]
                for m in range(DB):
                    dve.wait_ge(s_mh[l], m // 2 * 2 + 2)
                    b = bank(g, m // 2)
                    ins = dve.scalar_tensor_tensor(mem_lo[:, m, :], ps[:, b, (m % 2) * M:(m % 2 + 1) * M],
                                                   v(f"g_mem{l}", m), mem_hi[:, m, :].bitcast(F32), ALU.mult,
                                                   ALU.subtract)
                    ins.then_inc(s_ml[l], 1)
                    if m % 2:
                        dve.wait_ge(s_ml[l], m + 1)
                        dve.nop().then_inc(s_free[b // 4], 1)

            def memory_kv(l):
                g = GROUP0[f"mem_k{l}"]
                for m in range(4):
                    dve.wait_ge(s_done[f"mem_k{l}"], m + 1)
                    dve.tensor_copy(mk[:, m, :], ps[:, bank(g, m), 0:M]).then_inc(s_mkv[l], 1)
                    dve.wait_ge(s_mkv[l], m + 1)
                    dve.nop().then_inc(s_free[g % 2], 1)
                g = GROUP0[f"mem_v{l}"]
                for t in range(MB):
                    dve.wait_ge(s_done[f"mem_v{l}"], t + 1)
                    dve.tensor_copy(mv[:, t, :], ps[:, bank(g, t), :]).then_inc(s_mkv[l], 1)
                    dve.wait_ge(s_mkv[l], 5 + t)
                    dve.nop().then_inc(s_free[g % 2], 2)

            def attention(a, before_prob=None):
                H = a["heads"]

                def maxima(n):
                    st = stat[:, n % 3]
                    dve.wait_ge(a["s_scores"], n + 1)
                    b0 = 2 * BANK * (n % a["s_bufs"])
                    src, s0 = flat, b0
                    if a["masks"]:
                        if n >= 3:
                            dve.wait_ge(a["s_turned"], n - 2)
                        mask = m0 if a["name"] == "attn0" else m1
                        for c, w, mc in a["masks"]:
                            ins = dve.scalar_tensor_tensor(prob[n % 3][:, c:c + w], flat[:, b0 + c:b0 + c + w], a["scale"],
                                                           mask[:, mc:mc + w], ALU.mult, ALU.add)
                        ins.then_inc(a["s_read"], 1)
                        dve.wait_ge(a["s_read"], n + 1)
                        src, s0 = prob[n % 3], 0
                    tile = 0
                    for c, k, w in a["reduces"]:
                        ins = dve.tensor_reduce(st[:, 0, tile:tile + k],
                                                src[:, s0 + c:s0 + c + k * w].rearrange("p (k w) -> p k w", w=w),
                                                AX.X, ALU.max)
                        tile += k
                    link(ins)
                    if a["sink"]:
                        link(dve.tensor_scalar(st[:, 0, :], st[:, 0, :], v("sinks", n), None, ALU.max))
                    factor = -1.0 if a["masks"] else -a["scale"]
                    dve.tensor_scalar(st[:, 1, :], st[:, 0, :], factor, None, ALU.mult).then_inc(a["s_max"], 1)

                def normalise(n):
                    st = stat[:, n % 3]
                    dve.wait_ge(a["s_exp"], n + 1)
                    if a["sink"]:
                        link(dve.tensor_tensor(st[:, 2, :], st[:, 2, :], st[:, 3, :], ALU.add))
                    link(dve.reciprocal(st[:, 4, :], st[:, 2, :]))
                    for i, (c, w) in enumerate(a["probs"]):
                        ins = dve.tensor_scalar(prob[n % 3][:, c:c + w], prob[n % 3][:, c:c + w], st[:, 4, i:i + 1], None,
                                                ALU.mult)
                    ins.then_inc(a["s_prob"], 1)

                def output(tile):
                    dve.wait_ge(a["s_o_hi"], tile + 1)
                    k = a["tile0"] + tile
                    dve.tensor_tensor(f_lo[:, k, :], ps[:, 6 + tile % 2, :], f_hi[:, k, :].bitcast(F32),
                                      ALU.subtract).then_inc(a["s_o_lo"], 1)

                for n in range(H + 4):
                    if n < H:
                        maxima(n)
                    if 1 <= n <= H:
                        normalise(n - 1)
                    if n >= 4 and (n - 4) % a["per"] == a["per"] - 1:
                        output((n - 4) // a["per"])
                dve.wait_ge(a["s_o_lo"], a["tiles"])
                dve.nop().then_inc(s_free[0], 4)
                dve.nop().then_inc(s_free[1], 4)

            dve.memset(ones[:], 1.0).then_inc(s_const, 1)
            for b in range(2):
                link(dve.memset(xpad[b][:, 0:CONV - 1], 0.0))
            dve.wait_ge(s_vec, 16)
            lam, S = v("lam", 0, DB), [small[:, 8 * i:8 * i + 8] for i in range(8)]
            link(dve.scalar_tensor_tensor(S[1], lam, -1.0, lam, ALU.mult, ALU.max))
            link(dve.tensor_scalar(S[1], S[1], -1.0, None, ALU.mult))
            dve.nop().then_inc(s_sp_e, 1)

            residual("mix0", s_done["x_t"], first=True)

            dve.wait_ge(s_sp_e, 2)
            link(dve.tensor_scalar(S[3], S[2], 2.0, None, ALU.add))
            link(dve.reciprocal(S[3], S[3]))
            link(dve.tensor_tensor(S[3], S[2], S[3], ALU.mult))
            link(dve.tensor_tensor(S[4], S[3], S[3], ALU.mult))
            link(dve.tensor_scalar(S[5], S[4], 1.0 / 17.0, None, ALU.mult))
            for odd in (15, 13, 11, 9, 7, 5, 3):
                link(dve.scalar_tensor_tensor(S[5], S[5], 1.0 / odd, S[4], ALU.add, ALU.mult))
            link(dve.scalar_tensor_tensor(S[5], S[5], 1.0, S[3], ALU.add, ALU.mult))
            link(dve.tensor_scalar(S[6], lam, -1.0, 0.0, ALU.mult, ALU.max))
            link(dve.scalar_tensor_tensor(S[6], S[5], 2.0, S[6], ALU.mult, ALU.add))
            link(dve.tensor_scalar(S[7], S[6], LRU_C, None, ALU.mult))
            dve.tensor_scalar(S[6], S[6], -LRU_C, None, ALU.mult).then_inc(s_sp, 1)

            one_over_rms("mix0")
            g0 = GROUP0["in_xy"]

            def conv(m):
                dve.wait_ge(s_c0, m + 1)
                for tap in range(1, CONV):
                    ins = dve.scalar_tensor_tensor(xc[:, m, :], xpad[m % 2][:, tap:tap + T],
                                                   v("conv_w", tap * DB + m), xc[:, m, :], ALU.mult, ALU.add)
                    if tap < CONV - 1:
                        link(ins)
                ins.then_inc(s_xc, 1)

            def conv_low(m):
                dve.wait_ge(s_xch, m + 1)
                dve.tensor_tensor(f_lo[:, m, :], xc[:, m, :], f_hi[:, m, :].bitcast(F32), ALU.subtract).then_inc(s_xcl, 1)

            for m in range(DB + 2):
                if m < DB:
                    if m >= 2:
                        dve.wait_ge(s_xc, m - 1)
                    scaled(xpad[m % 2][:, CONV - 1:CONV - 1 + T], g0 + m // 4, m % 4, s_done["in_xy"], m + 1)
                    dve.nop().then_inc(s_xp, 1)
                if 1 <= m <= DB:
                    conv(m - 1)
                if m >= 2:
                    conv_low(m - 2)
            for m in range(DB):
                if m:
                    dve.wait_ge(s_yg, m)
                scaled(y_in[:], g0 + 2 + m // 4, m % 4, s_done["in_xy"], DB + m + 1)
                dve.nop().then_inc(s_y, 1)
            memory_norm(0)
            memory_low(0)

            for m in range(DB):
                dve.wait_ge(s_gate, m + 1)
                dve.tensor_tensor(xc[:, m, :], gate_i[:, m % 2, :], xc[:, m, :], ALU.mult).then_inc(s_gx, 1)

            def decay(m):
                dve.wait_ge(s_at, m + 1)
                link(dve.tensor_scalar(lru_d[:, m % 2, :], lru_r[:, m, :], 1.0, None, ALU.add))
                link(dve.reciprocal(lru_d[:, m % 2, :], lru_d[:, m % 2, :]))
                dve.tensor_tensor(lru_r[:, m, :], lru_r[:, m, :], lru_d[:, m % 2, :], ALU.mult).then_inc(s_lq, 1)

            def recur(m):
                dve.wait_ge(s_ls, m + 1)
                link(dve.tensor_tensor(lru_r[:, m, :], lru_r[:, m, :], xc[:, m, :], ALU.mult))
                link(dve.tensor_tensor_scan(xc[:, m, :], lru_a[:, m, :], lru_r[:, m, :], 0.0, ALU.mult, ALU.add))
                dve.tensor_tensor(xc[:, m, :], xc[:, m, :], yg[:, m, :], ALU.mult).then_inc(s_rec, 1)

            def rec_low(m):
                dve.wait_ge(s_rech, m + 1)
                dve.tensor_tensor(f_lo[:, m, :], xc[:, m, :], f_hi[:, m, :].bitcast(F32), ALU.subtract).then_inc(s_recl, 1)

            for m in range(DB):
                decay(m)
            g0 = GROUP0["in_qkv"]
            dve.wait_ge(s_rope, 32)

            def qk_tile(t):
                scaled(rope0[0][:], g0 + t // 4, t % 4, s_done["in_qkv"], t + 1)
                rotate(q0[:, t, :] if t < 4 else k0[:, t - 4, :], rope0, s_q0)

            for t in range(4):
                qk_tile(t)
            for m in range(4):
                recur(m)
                if m:
                    rec_low(m - 1)
            for t in range(4, 8):
                qk_tile(t)
            for m in range(4, DB):
                recur(m)
                rec_low(m - 1)
            rec_low(DB - 1)
            dve.wait_ge(s_done["in_qkv"], 12)
            for t in range(4):
                b = bank(g0 + 2, t)
                link(dve.tensor_tensor(v0_t[:, t, :], ps[:, b, :], rstd[:], ALU.mult))
                dve.nop().then_inc(s_free[b // 4], 1)
            dve.nop().then_inc(s_v0t, 4)
            memory_kv(0)
            for j in range(TB):
                dve.wait_ge(s_v0p, j + 1)
                dve.tensor_copy(v0[:, j, :], ps[:, 4 + j, :]).then_inc(s_v0, 1)
            dve.wait_ge(s_mask0, 16)
            attention(ATTN["attn0"])
            residual("xa0", s_done["out0"], group0=GROUP0["out0"])

            for l in (0, 1):
                if l:
                    one_over_rms("mix1")
                    for t in range(10):
                        name = "qkv_q" if t < 8 else "qkv_kv"
                        tt = t if t < 8 else t - 8
                        g = GROUP0[name] + tt // 4
                        b = bank(g, tt % 4)
                        tmp = rope1[0][:] if t < 9 else v1_t[:]
                        dve.wait_ge(s_done[name], tt + 1)
                        link(dve.tensor_tensor(tmp, ps[:, b, :], rstd[:], ALU.mult))
                        dve.nop().then_inc(s_free[b // 4], 1 if t < 8 else 2)
                        ins = dve.tensor_scalar(tmp, tmp, v("b_qkv", t), None, ALU.add)
                        if t == 9:
                            ins.then_inc(s_q1, 1)
                        else:
                            link(ins)
                            rotate(q1[:, t, :] if t < 8 else k1_rot[:], rope1, s_q1)
                    dve.wait_ge(s_q1, 10)
                    for kv in range(2):
                        for half in range(2):
                            dve.tensor_copy(k1[HD * half:HD * half + HD, kv, :],
                                            k1_rot[HD * kv:HD * kv + HD, :]).then_inc(s_k1, 1)
                    memory_norm(1)
                    memory_low(1)
                    memory_kv(1)
                    dve.wait_ge(s_v1p, 1)
                    dve.tensor_copy(v1[:, :, :].rearrange("p a n -> p (a n)"), ps[:, 4, :]).then_inc(s_v1, 1)
                    dve.wait_ge(s_mask1, 16)
                    attention(ATTN["attn1"])
                    residual("xa1", s_done["out1"], bias="b_out", group0=GROUP0["out1"])
                one_over_rms(f"xa{l}")
                for t in range(4):
                    scaled(qx[:, t, :], GROUP0[f"xq{l}"], t, s_done[f"xq{l}"], t + 1)
                    dve.nop().then_inc(s_xq[l], 1)
                attention(ATTN[f"xattn{l}"])
                residual(f"ffn{l}", s_done[f"xo{l}"], group0=GROUP0[f"xo{l}"])
                one_over_rms(f"ffn{l}")
                for c in range(2):
                    g0 = GROUP0[f"up{l}{c}"]
                    n0 = (D_FF // P * l + sum(CHUNK[:c])) // 2

                    def ff_group(i, s, g_static):
                        n = n0 + 2 * i + s
                        b0 = (g_static % 2) * 4
                        for p in range(2):
                            dve.wait_ge(s_ff, 4 * n + p + 1)
                            dve.tensor_tensor(ff_g[:, p, :], ps[:, b0 + p, :], rstd[:], ALU.mult).then_inc(s_ff_gate, 1)
                        for p in range(2):
                            dve.wait_ge(s_ff, 4 * n + p + 3)
                            dve.tensor_tensor(ff_u[:, p, :], ps[:, b0 + 2 + p, :], rstd[:], ALU.mult).then_inc(s_ff_up, 1)
                        dve.wait_ge(s_ff_gate, 2 * n + 2)
                        dve.wait_ge(s_ff_up, 2 * n + 2)
                        dve.nop().then_inc(s_free[g_static % 2], 4)
                        for p in range(2):
                            dve.wait_ge(s_ff_silu, 2 * n + p + 1)
                            dve.tensor_tensor(ff_u[:, p, :], ff_g[:, p, :], ff_u[:, p, :], ALU.mult).then_inc(s_ff_prod, 1)
                        for p in range(2):
                            tile = bass.ds(4 * i + (2 * s + p), 1)
                            dve.wait_ge(s_ff_hi, 2 * n + p + 1)
                            dve.tensor_tensor(f_lo[:, tile, :], ff_u[:, p:p + 1, :], f_hi[:, tile, :].bitcast(F32),
                                              ALU.subtract).then_inc(s_ff_lo, 1)
                        dve.wait_ge(s_ff_lo, 2 * n + 2)

                    groups = CHUNK[c] // 2

                    def body(i):
                        for s in range(2):
                            ff_group(i, s, g0 + s)
                    loop(dve, groups // 2, body)
                    if groups % 2:
                        ff_group(groups // 2, 0, g0)
                    nxt = ("mix1", "final")[l]
                    residual(nxt, s_done[f"down{l}{c}"], group0=GROUP0[f"down{l}{c}"], norm_next=c == 1)

            one_over_rms("final")
            for m in range(DB):
                dve.scalar_tensor_tensor(y_t[:, m, :], h[:, m, :], v("g_final", m), rstd[:], ALU.mult,
                                         ALU.mult).then_inc(s_zl, 1)
            for m in range(1, DB, 2):
                dve.wait_ge(s_fin, m + 1)
                dve.wait_ge(s_fin_o, m)
                dve.tensor_copy(y_out[:, :, m * P:(m + 1) * P],
                                ps[:, m, :].rearrange("p (t n) -> p t n", t=TB)).then_inc(s_fin_o, 1)

        @block.scalar
        def _(act):
            def residual(norm):
                for m in range(DB):
                    act.wait_ge(s_h, NORM[norm] * DB + m + 1)
                    if norm != "final":
                        act.activation(z_hi[:, m, :], h[:, m, :], ACT.Identity, scale=v(f"g_{norm}", m)).then_inc(s_zh, 1)
                    if m >= 2:
                        if norm != "final":
                            act.wait_ge(s_zl, NORM[norm] * DB + m)
                        else:
                            act.wait_ge(s_h, NORM[norm] * DB + m + 1)
                    act.activation(sq[:, m % 2, :], h[:, m, :], ACT.Square).then_inc(s_sq, 1)
                act.wait_ge(s_sum, NORM[norm] + 1)
                act.activation(sq[:, 0, :], ps[:, rms_bank[norm], :], ACT.Sqrt, bias=v("eps"), scale=1.0 / D).then_inc(s_rms, 1)

            rms_bank = {"mix0": bank(GROUP0["in_xy"] + 1, 0), "mix1": bank(GROUP0["qkv_q"] + 1, 0),
                        "final": bank(GROUP0["final"], 0)}
            for l in (0, 1):
                rms_bank[f"xa{l}"] = bank(GROUP0[f"xq{l}"] + 1, 0)
                rms_bank[f"ffn{l}"] = bank(GROUP0[f"up{l}0"] + 1, 0)

            def memory_norm(l):
                src, scratch = (mem_nat0, mem_nat1)[l], (mk, mk)[l]
                act.wait_ge(s_mem[l], 16)
                for t in range(MB):
                    for half in range(2):
                        act.activation(mk[:, 2 * half:2 * half + 2, :].rearrange("p a n -> p (a n)"),
                                       src[:, t, 512 * half:512 * half + 512], ACT.Square,
                                       accum_out=small[:, 4 + 2 * t + half:5 + 2 * t + half]).then_inc(s_ms[l], 1)
                        act.wait_ge(s_ms[l], 2 * t + half + 1)
                act.activation(small[:, 0:2], small[:, 4:8].rearrange("p (t a) -> p t a", a=2)[:, :, 0], ACT.Identity).then_inc(s_ms[l], 1)
                act.wait_ge(s_ms[l], 5)
                for t in range(MB):
                    act.activation(small[:, t:t + 1], small[:, 5 + 2 * t:6 + 2 * t], ACT.Identity, bias=small[:, t:t + 1]).then_inc(s_ms[l], 1)
                act.wait_ge(s_ms[l], 7)
                act.activation(small[:, 0:2], small[:, 0:2], ACT.Sqrt, bias=v("eps"), scale=1.0 / D).then_inc(s_mr[l], 1)

            def memory_high(l):
                g = GROUP0[f"mem_t{l}"]
                for m in range(DB):
                    act.wait_ge(s_done[f"mem_t{l}"], m // 2 + 1)
                    act.activation(mem_hi[:, m, :], ps[:, bank(g, m // 2), (m % 2) * M:(m % 2 + 1) * M], ACT.Identity,
                                   scale=v(f"g_mem{l}", m)).then_inc(s_mh[l], 1)

            def attention(a):
                H = a["heads"]

                def exps(n):
                    st = stat[:, n % 3]
                    act.wait_ge(a["s_max"], n + 1)
                    if a["masks"]:
                        src, s0, scale = prob[n % 3], 0, 1.0
                    else:
                        if n >= 3:
                            act.wait_ge(a["s_turned"], n - 2)
                        src, s0, scale = flat, 2 * BANK * (n % a["s_bufs"]), a["scale"]
                    if a["sink"]:
                        for i in range(TB):
                            act.activation(st[:, 3, i:i + 1], v("sinks", n), ACT.Exp, bias=st[:, 1, i:i + 1])
                    for i, (c, w) in enumerate(a["probs"]):
                        ins = act.activation(prob[n % 3][:, c:c + w], src[:, s0 + c:s0 + c + w], ACT.Exp,
                                             bias=st[:, 1, i:i + 1], scale=scale, accum_out=st[:, 2, i:i + 1])
                    ins.then_inc(a["s_exp"], 1)
                    if not a["masks"]:
                        act.wait_ge(a["s_exp"], n + 1)
                        act.nop().then_inc(a["s_read"], 1)

                def turned(n):
                    act.wait_ge(a["s_turned"], n + 1)
                    if n >= 2:
                        act.wait_ge(a["s_head"], n - 1)
                    t0 = a["t_bank"] * BANK
                    for c in range(0, a["t_width"], BANK):
                        w = min(BANK, a["t_width"] - c)
                        ins = act.activation(prob_t[n % 2][:, c:c + w], flat[:, t0 + c:t0 + c + w], ACT.Copy)
                    ins.then_inc(a["s_pt"], 1)

                def output(tile):
                    act.wait_ge(a["s_head"], a["per"] * (tile + 1))
                    act.activation(f_hi[:, a["tile0"] + tile, :], ps[:, 6 + tile % 2, :], ACT.Copy).then_inc(a["s_o_hi"], 1)

                for n in range(H + 4):
                    if n < H:
                        exps(n)
                    if 2 <= n < H + 2:
                        turned(n - 2)
                    if n >= 4 and (n - 4) % a["per"] == a["per"] - 1:
                        output((n - 4) // a["per"])

            act.wait_ge(s_vec, 16)
            act.wait_ge(s_sp_e, 1)
            act.activation(small[:, 16:24], small[:, 8:16], ACT.Exp).then_inc(s_sp_e, 1)
            residual("mix0")
            for m in range(DB + 1):
                if m < DB:
                    act.wait_ge(s_xp, m + 1)
                    act.activation(xc[:, m, :], xpad[m % 2][:, 0:T], ACT.Identity, bias=v("conv_b", m),
                                   scale=v("conv_w", m)).then_inc(s_c0, 1)
                if m >= 1:
                    act.wait_ge(s_xc, m)
                    act.activation(f_hi[:, m - 1, :], xc[:, m - 1, :], ACT.Copy).then_inc(s_xch, 1)
            for m in range(DB):
                act.wait_ge(s_y, m + 1)
                act.activation(yg[:, m, :], y_in[:], ACT.Gelu_apprx_tanh).then_inc(s_yg, 1)
            act.wait_ge(s_sp, 1)
            memory_norm(0)
            memory_high(0)
            for hd in range(LRU_HEADS):
                g = GROUP0["gates"] + hd
                act.wait_ge(s_done["gates"], 4 * (hd + 1))
                for p in range(2):
                    m = 2 * hd + p
                    act.activation(lru_r[:, m, :], ps[:, bank(g, p), :], ACT.Sigmoid, bias=v("ba", m)).then_inc(s_act, 1)
                    if m >= 2:
                        act.wait_ge(s_gx, m - 1)
                    act.activation(gate_i[:, p, :], ps[:, bank(g, 2 + p), :], ACT.Sigmoid, bias=v("bx", m)).then_inc(s_gate, 1)
                act.wait_ge(s_gate, 2 * hd + 2)
                act.wait_ge(s_act, 2 * hd + 2)
                act.nop().then_inc(s_free[g % 2], 4)
            for m in range(DB):
                act.activation(lru_a[:, m, :], lru_r[:, m, :], ACT.Exp, scale=small[:, 48:56][:, m:m + 1])
                act.activation(lru_r[:, m, :], lru_r[:, m, :], ACT.Tanh, scale=small[:, 56:64][:, m:m + 1]).then_inc(s_at, 1)
            for m in range(DB):
                act.wait_ge(s_lq, m + 1)
                act.activation(lru_r[:, m, :], lru_r[:, m, :], ACT.Sqrt, scale=2.0).then_inc(s_ls, 1)
            for m in range(DB):
                act.wait_ge(s_rec, m + 1)
                act.activation(f_hi[:, m, :], xc[:, m, :], ACT.Copy).then_inc(s_rech, 1)
            attention(ATTN["attn0"])
            residual("xa0")
            for l in (0, 1):
                if l:
                    memory_norm(1)
                    memory_high(1)
                    attention(ATTN["attn1"])
                    residual("xa1")
                attention(ATTN[f"xattn{l}"])
                residual(f"ffn{l}")
                for c in range(2):
                    n0 = (D_FF // P * l + sum(CHUNK[:c])) // 2

                    def ff_group(i, s):
                        n = n0 + 2 * i + s
                        for p in range(2):
                            act.wait_ge(s_ff_gate, 2 * n + p + 1)
                            act.activation(ff_g[:, p, :], ff_g[:, p, :], ACT.Silu).then_inc(s_ff_silu, 1)
                        for p in range(2):
                            act.wait_ge(s_ff_prod, 2 * n + p + 1)
                            act.activation(f_hi[:, bass.ds(4 * i + (2 * s + p), 1), :], ff_u[:, p:p + 1, :],
                                           ACT.Copy).then_inc(s_ff_hi, 1)

                    groups = CHUNK[c] // 2

                    def body(i):
                        for s in range(2):
                            ff_group(i, s)
                    loop(act, groups // 2, body)
                    if groups % 2:
                        ff_group(groups // 2, 0)
                residual(("mix1", "final")[l])
            for m in range(0, DB, 2):
                act.wait_ge(s_fin, m + 1)
                if m:
                    act.wait_ge(s_fin_o, m)
                act.activation(y_out[:, :, m * P:(m + 1) * P], ps[:, m, :].rearrange("p (t n) -> p t n", t=TB),
                               ACT.Copy).then_inc(s_fin_o, 1)


def tables():
    import math
    import numpy as np

    q, k = np.arange(P)[:, None], np.arange(P)[None, :]

    def dist(blocks):
        return q - k + P * blocks
    strip = []
    for blocks in (3, 2, 1, 0):
        d = dist(blocks)
        count = (d <= 128).astype(int) + (d % 4 == 0) + (d % 16 == 0)
        strip.append(np.where((d >= 0) & (count > 0), np.log(np.maximum(count, 1)), NEG))
    mask0 = np.concatenate(strip, axis=1).astype(np.float32)
    pair = np.concatenate([np.where((dist(b) >= 0) & (dist(b) <= 127), 0.0, NEG) for b in (1, 0)], axis=1)
    mask1 = np.tile(pair, (1, TB)).astype(np.float32)
    rot = HD // 4
    inv = np.float32(500000.0) ** (-np.arange(0, rot, 2, dtype=np.float32) / np.float32(rot))
    ang = np.arange(T, dtype=np.float32)[:, None] * inv.astype(np.float32)[None, :]
    cos, sin = np.cos(ang).T, np.sin(ang).T
    cos_t, sin_t = np.ones((P, T), np.float32), np.zeros((P, T), np.float32)
    for head in (0, HD):
        for half in range(2):
            r = head + half * rot // 2
            cos_t[r:r + rot // 2] = cos
            sin_t[r:r + rot // 2] = sin if half else -sin
    return dict(mask0=mask0, mask1=mask1, rope_cos=cos_t, rope_sin=sin_t, identity=np.eye(P, dtype=np.float32))


def kernel(**inputs):
    import numpy as np
    import concourse.bacc as bacc
    from concourse.bass_utils import run_bass_kernel_spmd as run

    a = {k: np.asarray(w) for k, w in inputs.items()}

    def cols(w):
        return w.reshape(-1, P).T

    packed = [cols(a["mix_norm"][0]), cols(a["xa_norm"][0]), cols(a["ffn_norm"][0]), cols(a["mix_norm"][1]),
              cols(a["xa_norm"][1]), cols(a["ffn_norm"][1]), cols(a["final_norm"]), cols(a["xa_mem_norm"][0]),
              cols(a["xa_mem_norm"][1]), cols(a["lru_conv_w"][0].reshape(-1)), cols(a["lru_conv_b"][0]),
              cols(a["lru_ba"][0].reshape(-1)), cols(a["lru_bx"][0].reshape(-1)), cols(a["lru_lambda"][0]),
              cols(a["c_b_qkv"][0]), cols(a["c_b_out"][0]), np.broadcast_to(a["c_sinks"][0], (P, C_HEADS)),
              np.full((P, 1), EPS, np.float32)]
    arrays = dict(
        x=a["x"][0], mem=a["mem"][0], w_in=a["ab_w_in"][0], w_gates=np.stack([a["lru_wa"][0], a["lru_wx"][0]]),
        w_out0=a["ab_w_out"][0], w_qkv=a["c_w_qkv"][0], w_out1=a["c_w_out"][0], xa_wq=a["xa_wq"], xa_wkv=a["xa_wkv"],
        xa_wo=a["xa_wo"], w_gate_up=a["ffn_w_gate_up"], w_down=a["ffn_w_down"],
        vectors=np.concatenate(packed, axis=1), **tables())
    arrays = {k: np.ascontiguousarray(w) for k, w in arrays.items()}
    nc = bacc.Bacc("TRN2", target_bir_lowering=False, num_devices=1)
    args = {k: nc.dram_tensor(f"in_{k}", w.shape, mybir.dt.from_np(w.dtype), kind="ExternalInput").ap()
            for k, w in arrays.items()}
    out = nc.dram_tensor("out", (T, D), F32, kind="ExternalOutput").ap()
    trunk(nc, out=out, **args)
    r = run(nc, [{f"in_{k}": w for k, w in arrays.items()}], core_ids=[0])
    return np.asarray(r.results[0]["out"]).reshape(1, T, D)
```

```python
import concourse.bass as bass
from concourse import mybir
from contextlib import ExitStack

F32 = mybir.dt.float32
F32R = mybir.dt.float32r
ALU = mybir.AluOpType
ACT = mybir.ActivationFunctionType
AX = mybir.AxisListType

P = 128
T = 512
D = 1024
DB = D // P
TB = T // P
M = 256
MB = M // P
LRU_HEADS = 4
B_HEADS = 8
C_HEADS = 16
HD = 64
XH = 4
D_FF = 2816
EPS = 1e-6
LRU_C = 8.0
CONV = 4
NEG = -1e30
BANK = 512
RAW = 4
SPLIT = 2
CHUNK = (12, 10)

STAGES = [("x_t", 2, 0), ("in_xy", 4, 4), ("gates", 4, 1), ("mem_t0", 1, 0), ("in_qkv", 3, 4),
          ("attn0", 2, 2), ("out0", 2, 6)]
for _l in (0, 1):
    if _l:
        STAGES += [("qkv_q0", 1, 4), ("qkv_kv", 1, 2), ("mem_t1", 1, 0), ("qkv_q1", 1, 4), ("attn1", 2, 2), ("out1", 2, 4)]
    STAGES += [(f"xq{_l}", 1, 4), (f"xattn{_l}", 2, 2), (f"xo{_l}", 2, 2),
               (f"up{_l}0", CHUNK[0] // 2, 4), (f"down{_l}0", 2, CHUNK[0] // 2),
               (f"up{_l}1", CHUNK[1] // 2, 4), (f"down{_l}1", 2, CHUNK[1] // 2)]
STAGES.append(("final", 2, 0))
GROUP0, UNIT0, GROUPS = {}, {}, {}
_g = _u = 0
for _n, _ng, _nu in STAGES:
    GROUP0[_n], UNIT0[_n], GROUPS[_n] = _g, _u, _ng
    _g += _ng
    _u += _ng * _nu
UNITS = _u

NORMS = ("mix0", "xa0", "ffn0", "mix1", "xa1", "ffn1", "final")
NORM = {n: i for i, n in enumerate(NORMS)}
COL = {}
_c = 0
for _n, _w in [(f"g_{n}", DB) for n in NORMS] + [("g_mem0", DB), ("g_mem1", DB), ("conv_w", CONV * DB), ("conv_b", DB),
                                                ("ba", DB), ("bx", DB), ("lam", DB), ("b_qkv", 10), ("b_out", DB),
                                                ("sinks", C_HEADS), ("eps", 1)]:
    COL[_n] = _c
    _c += _w
NCOL = _c


def attention_plan(kind):
    if kind == "xattn":
        scores = [(i, 0, M, M * i) for i in range(TB)]
        return dict(width=TB * M, scores=scores, reduces=[(0, TB, M)], masks=[], probs=[(M * i, M) for i in range(TB)],
                    turns=[(M * i + P * j, BANK * j + P * i) for j in range(MB) for i in range(TB)],
                    t_width=MB * BANK, values=[(j, BANK * j, 0, T, j == 0) for j in range(MB)])
    if kind == "attn1":
        start = [2 * P * i + (P if i == 0 else 0) for i in range(TB)]
        scores = [(i, max(i - 1, 0) * P, P if i == 0 else 2 * P, start[i]) for i in range(TB)]
        blocks = [(0, 0)] + [(i, j) for i in range(1, TB) for j in (i - 1, i)]
        return dict(width=TB * 2 * P, scores=scores, reduces=[(P, 1, P), (2 * P, TB - 1, 2 * P)],
                    masks=[(P, (2 * TB - 1) * P, P)], probs=[(start[i], P if i == 0 else 2 * P) for i in range(TB)],
                    turns=[(2 * P * i + P * (j - i + 1), P * n) for n, (i, j) in enumerate(blocks)],
                    t_width=len(blocks) * P,
                    values=[(j, P * n, P * i, P, n == 0) for n, (i, j) in enumerate(blocks)])
    start = [0, P, BANK, 2 * BANK]
    t_start = [0, BANK, 2 * BANK, BANK + 3 * P]
    return dict(width=3 * BANK, scores=[(i, 0, P * (i + 1), start[i]) for i in range(TB)],
                reduces=[(start[i], 1, P * (i + 1)) for i in range(TB)],
                masks=[(start[i], P * (i + 1), (TB - 1 - i) * P) for i in range(TB)],
                probs=[(start[i], P * (i + 1)) for i in range(TB)],
                turns=[(start[i] + P * j, t_start[j] + P * (i - j)) for j in range(TB) for i in range(j, TB)],
                t_width=2 * BANK + 2 * P,
                values=[(j, t_start[j], P * j, T - P * j, j == 0) for j in range(TB)])


def trunk(nc, x, mem, w_in, w_gates, w_out0, w_qkv, w_out1, xa_wq, xa_wkv, xa_wo, w_gate_up, w_down,
          vectors, mask0, mask1, rope_cos, rope_sin, identity, out):
    ctx = ExitStack()
    with ctx:
        base = 16512
        top = [base]

        def at(name, shape, dt, offset):
            return nc.alloc_sbuf_tensor_at(name, shape, dt, offset=offset)

        def zone(nbytes):
            top[0] += nbytes
            return top[0] - nbytes

        z_h = zone(4 * DB * T)
        z_zh, z_zl = zone(4 * DB * T), zone(4 * DB * T)
        z_raw = zone(RAW * 4096)
        z_wh, z_wl = zone(SPLIT * 4096), zone(SPLIT * 4096)
        z_fh, z_fl = zone(4 * CHUNK[0] * T), zone(4 * CHUNK[0] * T)
        z_x, z_y = zone(4 * DB * T), zone(4 * DB * T)
        z_q, z_k, z_v = zone(8192), zone(8192), zone(8192)
        z_mk, z_mv = zone(4096), zone(4096)
        z_const = zone(0)

        h = at("h", [P, DB, T], F32, z_h)
        z_hi = at("z_hi", [P, DB, T], F32R, z_zh)
        z_lo = at("z_lo", [P, DB, T], F32R, z_zl)
        raw = at("raw", [P, RAW, 2, 512], F32, z_raw)
        w_hi = at("w_hi", [P, SPLIT, 2, 512], F32R, z_wh)
        w_lo = at("w_lo", [P, SPLIT, 2, 512], F32R, z_wl)
        f_hi = at("f_hi", [P, CHUNK[0], T], F32R, z_fh)
        f_lo = at("f_lo", [P, CHUNK[0], T], F32R, z_fl)
        lru_r = at("lru_r", [P, DB, T], F32, z_fh)
        lru_a = at("lru_a", [P, DB, T], F32, z_fl)
        mem_hi = f_hi[:, 8:12, :].rearrange("p a (b n) -> p (a b) n", n=M)
        mem_lo = f_lo[:, 8:12, :].rearrange("p a (b n) -> p (a b) n", n=M)
        mem2_hi = at("mem2_hi", [P, DB, M], F32R, z_x)
        mem2_lo = at("mem2_lo", [P, DB, M], F32R, z_x + 8192)
        xc = at("xc", [P, DB, T], F32, z_x)
        q1 = at("q1", [P, DB, T], F32, z_x)
        x_nat = at("x_nat", [P, TB, D], F32, z_y)
        yg = at("yg", [P, DB, T], F32, z_y)
        ff_g = at("ff_g", [P, 2, T], F32, z_y)
        ff_u = at("ff_u", [P, 2, T], F32, z_y + 4096)
        rope1 = [at(f"rope1_{i}", [P, T], F32, z_y + 2048 * i) for i in range(2)]
        k1_in = at("k1_in", [P, T], F32, z_y + 4096)
        mem_nat1 = at("mem_nat1", [P, MB, D], F32, z_y + 8192)
        mem_nat0 = at("mem_nat0", [P, MB, D], F32, z_q)
        q0 = at("q0", [P, 4, T], F32, z_q)
        qx = at("qx", [P, 4, T], F32, z_q)
        xpad = [at(f"xpad{i}", [P, T + CONV], F32, z_k + 2080 * i) for i in range(2)]
        k0 = at("k0", [P, 4, T], F32, z_k)
        k1 = at("k1", [P, 2, T], F32, z_k)
        m1 = at("m1", [P, 2 * TB * P], F32, z_k + 4096)
        rope0 = [at(f"rope0_{i}", [P, T], F32, z_v + 2048 * i) for i in range(3)]
        v0 = at("v0", [P, TB, 512], F32, z_v)
        k1_rot = at("k1_rot", [P, T], F32, z_v)
        v1_t = at("v1_t", [P, T], F32, z_v + 2048)
        v1 = at("v1", [P, TB, P], F32, z_v + 4096)
        mk = at("mk", [P, XH, M], F32, z_mk)
        mv = at("mv", [P, MB, 512], F32, z_mv)
        gate_i = at("gate_i", [P, 2, T], F32, z_mk)
        lru_d = at("lru_d", [P, 2, T], F32, z_mv)
        v0_t = at("v0_t", [P, 4, T], F32, z_zh + 18432)
        prob = [at(f"prob{i}", [P, 3 * BANK], F32, z_zh + 6144 * i) for i in range(3)]
        m0 = at("m0", [P, TB * P], F32, z_zh + 30720)
        prob_t = [at(f"prob_t{i}", [P, 3 * BANK], F32, z_zh + 18432 + 6144 * i) for i in range(2)]
        y_t = at("y_t", [P, DB, T], F32, z_zh)
        y_out = at("y_out", [P, TB, D], F32, z_zl)
        sq = at("sq", [P, 2, T], F32, z_const)
        acc = at("acc", [P, T], F32, z_const + 4096)
        rstd = at("rstd", [P, T], F32, z_const + 6144)
        ident = at("ident", [P, P], F32, z_const + 8192)
        ones = at("ones", [P, P], F32, z_const + 8704)
        vec = at("vec", [P, NCOL], F32, z_const + 9216)
        z_small = z_const + 9216 + (4 * NCOL + 31) // 32 * 32
        small = at("small", [P, 8 * 8], F32, z_small)
        stat = at("stat", [P, 3, 6, TB], F32, z_small + 256)
        cos_t = at("cos_t", [P, T], F32, z_small + 544)
        sin_t = at("sin_t", [P, T], F32, z_small + 2592)
        assert z_small + 4640 <= nc.sbuf_usable_end, (z_small + 4640, nc.sbuf_usable_end)

        ps = ctx.enter_context(nc.psum_tensor("ps", [P, 8, BANK], F32))
        flat = ps[:, :, :].rearrange("p b n -> p (b n)")

        def bank(group, m):
            return (group % 2) * 4 + m

        def sem(name):
            return ctx.enter_context(nc.semaphore(name))

        def v(name, m=0, n=1):
            return vec[:, COL[name] + m:COL[name] + m + n]

        s_ident, s_vec, s_x, s_rope, s_mask0, s_mask1 = [sem(n) for n in
                                                      ("s_ident", "s_vec", "s_x", "s_rope", "s_mask0", "s_mask1")]
        s_mem = [sem("s_mem0"), sem("s_mem1")]
        s_raw = [sem(f"s_raw{i}") for i in range(RAW)]
        s_begun = sem("s_weight_begun")
        s_hi = sem("s_weight_hi")
        s_split = sem("s_weight_split")
        s_used = sem("s_weight_used")
        s_free = [sem("s_banks_free0"), sem("s_banks_free1")]
        s_done = {n: sem(f"s_done_{n}") for n, _, _ in STAGES if n[:2] not in ("up", "do") and "attn" not in n}
        s_done |= {f"down{l}{c}": sem(f"s_done_down{l}{c}") for l in (0, 1) for c in (0, 1)}
        s_ff = sem("s_ff_tiles")
        s_ff_gate, s_ff_silu, s_ff_up = sem("s_ff_gate"), sem("s_ff_silu"), sem("s_ff_up")
        s_ff_prod, s_ff_hi, s_ff_lo = sem("s_ff_prod"), sem("s_ff_hi"), sem("s_ff_lo")
        s_h = sem("s_h")
        s_sq = sem("s_sq")
        s_acc = sem("s_acc")
        s_zh = sem("s_z_hi")
        s_zl = sem("s_z_lo")
        s_sum = sem("s_sum")
        s_rms = sem("s_rms")
        s_rstd = sem("s_rstd")
        s_dve, s_act = sem("s_dve_chain"), sem("s_act_chain")
        s_const = sem("s_const")
        s_xp, s_c0, s_xc = sem("s_x_scaled"), sem("s_conv_first"), sem("s_conv")
        s_xch, s_xcl = sem("s_conv_hi"), sem("s_conv_lo")
        s_y, s_yg = sem("s_y_scaled"), sem("s_gelu")
        s_sp_e, s_sp = sem("s_exp_lambda"), sem("s_softplus")
        s_gate, s_gx = sem("s_gate_i"), sem("s_gated_input")
        s_at, s_lq, s_ls = sem("s_decay"), sem("s_one_minus_a2"), sem("s_input_scale")
        s_rec, s_rech, s_recl = sem("s_rec"), sem("s_rec_hi"), sem("s_rec_lo")
        s_q0, s_v0t, s_v0p, s_v0 = sem("s_qk0"), sem("s_v0_t"), sem("s_v0_turned"), sem("s_v0")
        s_qkv1, s_qkv1b, s_q1 = sem("s_qkv1"), sem("s_qkv1_biased"), sem("s_qk1_rotated")
        s_v1p, s_v1, s_k1 = sem("s_v1_turned"), sem("s_v1"), sem("s_k1")
        s_ms, s_mr, s_mn = [sem("s_ms0"), sem("s_ms1")], [sem("s_mr0"), sem("s_mr1")], [sem("s_mn0"), sem("s_mn1")]
        s_mem2 = sem("s_mem_copied")
        s_mh, s_ml = [sem("s_mh0"), sem("s_mh1")], [sem("s_ml0"), sem("s_ml1")]
        s_xq = [sem("s_xq0"), sem("s_xq1")]
        s_fin, s_fin_o, s_out = sem("s_final_t"), sem("s_final_out"), sem("s_out")

        ATTN = {}
        for name, heads, plan, tiles in (("attn0", B_HEADS, "attn0", 4), ("xattn0", XH, "xattn", 4),
                                         ("attn1", C_HEADS, "attn1", 8), ("xattn1", XH, "xattn", 4)):
            a = dict(name=name, heads=heads, tiles=tiles, per=heads // tiles, **attention_plan(plan))
            a["bank"] = lambda i, g=GROUP0[name]: (i + 4 * (g % 2)) % 8
            a["s_bufs"] = 1 if plan == "attn0" else 2
            a["o_banks"] = [a["bank"](i) for i in ((3, 7) if plan == "attn0" else (6, 7))]
            a["scale"] = P ** -0.5 if plan == "xattn" else HD ** -0.5
            a["sink"] = plan == "attn1"
            a["t_dve"] = (a["t_width"] - 1) // BANK * BANK
            a["tile0"] = 8 if plan == "attn0" else 0
            for s in ("scores", "read", "max", "exp", "rden", "prob", "turned", "pt", "head", "o_hi", "o_lo",
                      "filler", "filled"):
                a["s_" + s] = sem(f"s_{name}_{s}")
            ATTN[name] = a

        class Chain:
            def __init__(self, eng, s):
                self.eng, self.s, self.n = eng, s, 0

            def link(self, ins):
                self.n += 1
                ins.then_inc(self.s, 1)
                self.eng.wait_ge(self.s, self.n)

        def loop(eng, count, body):
            if count == 1:
                body(0)
            elif count > 1:
                with eng.Fori(0, count) as i:
                    body(i)

        def free_needed(group):
            return 4 * (group // 2)

        block = ctx.enter_context(nc.Block())

        @block.sync
        def _(sp):
            sp.dma_start(ident[:], identity).then_inc(s_ident, 16)
            for t in range(TB):
                sp.dma_start(x_nat[:, t, :], x[t * P:(t + 1) * P, :]).then_inc(s_x, 16)
            sp.dma_start(vec[:], vectors).then_inc(s_vec, 16)
            seen = [0]

            def unit(u, parts):
                u_static = seen[0]
                seen[0] += 1
                if u_static >= RAW:
                    sp.wait_ge(s_split, u - RAW + 1)
                for lo, hi, src in parts:
                    sp.dma_start(raw[:, u_static % RAW, :, lo:hi], src).then_inc(s_raw[u_static % RAW], 32 // len(parts))

            def rows(w, r0, col, n=512):
                return w[r0:r0 + 2 * P, bass.ds(col, n)].rearrange("(a p) n -> p a n", p=P)

            def stream(name, w, units, col0=0, first=0, count=None):
                n = GROUPS[name] if count is None else count
                u0 = UNIT0[name] + first * units

                def body(i):
                    keep = seen[0]
                    for j in range(units):
                        unit(u0 + units * i + j, [(0, 512, rows(w, 2 * P * j, (first + i) * 512 + col0))])
                    seen[0] = keep + units
                if units % RAW == 0:
                    loop(sp, n, body)
                    seen[0] = u0 + n * units
                else:
                    for i in range(n):
                        body(i)

            def ff(l, c):
                u0 = UNIT0[f"up{l}{c}"]
                f0 = sum(CHUNK[:c]) * P

                def body(i):
                    for j in range(4):
                        unit(u0 + 4 * i + j, [(0, 256, rows(w_gate_up[l], 2 * P * j, i * 256 + f0, 256)),
                                              (256, 512, rows(w_gate_up[l], 2 * P * j, i * 256 + f0 + D_FF, 256))])
                loop(sp, CHUNK[c] // 2, body)
                seen[0] = UNIT0[f"down{l}{c}"]
                stream(f"down{l}{c}", w_down[l][f0:f0 + CHUNK[c] * P, :], CHUNK[c] // 2)

            for j in range(4):
                unit(j, [(0, 512, rows(w_in, 2 * P * j, 0))])
            sp.dma_start(mem_nat0[:], mem.rearrange("(a p) n -> p a n", p=P)).then_inc(s_mem[0], 16)
            for i, col in ((1, D), (2, 512), (3, D + 512)):
                for j in range(4):
                    unit(UNIT0["in_xy"] + 4 * i + j, [(0, 512, rows(w_in, 2 * P * j, col))])
            sp.dma_start(cos_t[:], rope_cos).then_inc(s_rope, 16)
            sp.dma_start(sin_t[:], rope_sin).then_inc(s_rope, 16)
            for hd in range(LRU_HEADS):
                unit(UNIT0["gates"] + hd, [(0, 256, w_gates[0][hd].rearrange("(a p) n -> p a n", p=P)),
                                           (256, 512, w_gates[1][hd].rearrange("(a p) n -> p a n", p=P))])
            stream("in_qkv", w_in, 4, col0=2 * D)
            for l in (0, 1):
                if l:
                    stream("qkv_q0", w_qkv, 4)
                    for j in range(2):
                        src = w_qkv[4 * P * j:4 * P * (j + 1), D:D + 256].rearrange("(a p) n -> p a n", p=P)
                        unit(UNIT0["qkv_kv"] + j, [(0, 256, src[:, 0:2, :]), (256, 512, src[:, 2:4, :])])
                    stream("qkv_q1", w_qkv, 4, col0=512)
                    sp.wait_ge(ATTN["attn0"]["s_scores"], B_HEADS)
                    sp.dma_start(m1[:], mask1).then_inc(s_mask1, 16)
                stream(f"attn{l}", xa_wkv[l], 4, count=1)
                if l == 0:
                    sp.wait_ge(s_done["in_qkv"], 12)
                    sp.dma_start(m0[:], mask0).then_inc(s_mask0, 16)
                stream(f"out{l}", (w_out0, w_out1)[l], (6, 4)[l])
                stream(f"xq{l}", xa_wq[l], 4)
                if l == 0:
                    sp.wait_ge(s_recl, DB)
                    sp.dma_start(mem_nat1[:], mem.rearrange("(a p) n -> p a n", p=P)).then_inc(s_mem[1], 16)
                stream(f"xattn{l}", xa_wkv[l], 4, col0=512, count=1)
                stream(f"xo{l}", xa_wo[l], 2)
                ff(l, 0)
                ff(l, 1)
            assert seen[0] == UNITS
            for c in range(4):
                sp.wait_ge(s_fin_o, 2 * (c + 1))
                sp.dma_start(out.rearrange("(t p) n -> p t n", p=P)[:, :, 256 * c:256 * (c + 1)],
                             y_out[:, :, 256 * c:256 * (c + 1)]).then_inc(s_out, 16)
            sp.wait_ge(s_out, 64)

        @block.gpsimd
        def _(pool):
            def split(u, j, empty=False):
                half = j % SPLIT
                pool.wait_ge(s_raw[j], (u - j + RAW) * (32 // RAW))
                if not empty:
                    pool.wait_ge(s_used, u - SPLIT + 2)
                pool.sem_inc(s_begun, 1)
                pool.tensor_scalar(w_hi[:, half], raw[:, j], 1.0, 1.0, ALU.mult, ALU.mult).then_inc(s_hi, 1)
                pool.wait_ge(s_hi, u + 1)
                pool.tensor_tensor(w_lo[:, half], raw[:, j], w_hi[:, half].bitcast(F32),
                                   ALU.subtract).then_inc(s_split, 1)

            def split_all(u0, u1):
                while u0 % RAW and u0 < u1:
                    split(u0, u0 % RAW)
                    u0 += 1

                def body(i):
                    for j in range(RAW):
                        split(i * RAW + (u0 + j), j)
                loop(pool, (u1 - u0) // RAW, body)
                for u in range(u0 + (u1 - u0) // RAW * RAW, u1):
                    split(u, u % RAW)

            def normalise(a, n):
                pool.wait_ge(a["s_rden"], n + 1)
                for i, (c, w) in enumerate(a["probs"]):
                    ins = pool.tensor_scalar(prob[n % 3][:, c:c + w], prob[n % 3][:, c:c + w],
                                             stat[:, n % 3, 4, i:i + 1], 1.0, ALU.mult, ALU.mult)
                ins.then_inc(a["s_prob"], 1)

            split(0, 0, empty=True)
            split(1, 1, empty=True)
            at_unit = SPLIT
            for name in ("attn0", "xattn0", "attn1", "xattn1"):
                last = UNIT0[name] + 4
                split_all(at_unit, last)
                normalise(ATTN[name], 0)
                split(last, last % RAW)
                for n in range(1, ATTN[name]["heads"]):
                    normalise(ATTN[name], n)
                at_unit = last + 1
            split_all(at_unit, UNITS)

        @block.tensor
        def _(pe):
            def product(o, half, kk, c0, c1, rhi, rlo, start, stop, unit_starts):
                whi, wlo = w_hi[:, half, kk, c0:c1], w_lo[:, half, kk, c0:c1]
                ins = pe.matmul(o, whi, rhi, start=start, stop=False)
                if unit_starts:
                    ins.then_inc(s_used, 1)
                pe.matmul(o, whi, rlo, start=False, stop=False)
                return pe.matmul(o, wlo, rhi, start=False, stop=stop)

            def group(g_static, g, u0_static, u0, units, rhs, done, n=T, before=None, hook=None, first=0, last=None):
                for j in range(first, units if last is None else last):
                    if before:
                        before(2 * j + 1)
                    if j == 0 and g_static >= 2:
                        pe.wait_ge(s_free[g_static % 2], 4 * (g_static // 2) + (g - g_static) * 2)
                    pe.wait_ge(s_split, u0 + j + 1)
                    half = (u0_static + j) % SPLIT
                    for m in range(4):
                        for kk in range(2):
                            k = 2 * j + kk
                            hi, lo = rhs(k)
                            ins = product(ps[:, bank(g_static, m), 0:n], half, kk, P * m, P * (m + 1), hi, lo,
                                          k == 0, k == 2 * units - 1, m == 0 and kk == 0)
                        if j == units - 1:
                            ins.then_inc(done, 1)
                    if hook and j == min(1, units - 1):
                        hook()

            def stage(name, units, rhs, done, ready=None, norm=None, first=0):
                g0, u0, ng = GROUP0[name], UNIT0[name], GROUPS[name]
                hook = (lambda: norm_sum(norm, g0 + 1)) if norm else None
                group(g0, g0, u0, u0, units, rhs, done, before=ready, hook=hook, first=first)
                if norm and ng > 1:
                    pe.wait_ge(s_rms, NORM[norm] + 1)
                rest, at_g, at_u = ng - 1, g0 + 1, u0 + units

                def body(i):
                    for s in range(2):
                        group(at_g + s, at_g + s + 2 * i, at_u + units * s, at_u + units * s + 2 * units * i,
                              units, rhs, done)
                if units % SPLIT == 0:
                    if rest // 2:
                        loop(pe, rest // 2, body)
                    if rest % 2:
                        group(at_g + rest - 1, at_g + rest - 1, at_u + units * (rest - 1),
                              at_u + units * (rest - 1), units, rhs, done)
                else:
                    for s in range(rest):
                        group(at_g + s, at_g + s, at_u + units * s, at_u + units * s, units, rhs, done)

            def ahead(name, units, rhs, done, ready):
                g0, u0 = GROUP0[name], UNIT0[name]
                return lambda j: group(g0, g0, u0, u0, units, rhs, done, before=ready, first=j, last=j + 1)

            def norm_sum(norm, g):
                pe.wait_ge(s_acc, NORM[norm] + 1)
                pe.wait_ge(s_free[g % 2], free_needed(g))
                pe.matmul(ps[:, bank(g, 0), :], ones[:], acc[:], start=True, stop=True).then_inc(s_sum, 1)

            def z(k):
                return z_hi[:, k, :], z_lo[:, k, :]

            def f(k):
                return f_hi[:, k, :], f_lo[:, k, :]

            def z_ready(norm):
                return lambda k: pe.wait_ge(s_zl, NORM[norm] * DB + k + 1)

            def attention(a, q, key, value, ready, extra, next_unit, tail):
                g = GROUP0[a["name"]]
                H = a["heads"]
                for s in range(2):
                    pe.wait_ge(s_free[(g + s) % 2], free_needed(g + s))
                ready()

                def scores(n):
                    if a["name"] == "attn1" and n % 2 == 0:
                        pe.wait_ge(s_q1, 2 + n // 2)
                    if n >= a["s_bufs"]:
                        pe.wait_ge(a["s_read"], n - a["s_bufs"] + 1)
                    b0 = BANK * (a["bank"](0) + 2 * (n % a["s_bufs"]))
                    for i, k0_, nk, c in a["scores"]:
                        ins = pe.matmul(flat[:, b0 + c:b0 + c + nk], q(n)[:, i * P:(i + 1) * P],
                                        key(n)[:, k0_:k0_ + nk], start=True, stop=True)
                    ins.then_inc(a["s_scores"], 1)

                def turns(n):
                    pe.wait_ge(a["s_prob"], n + 1)
                    if n >= 1:
                        pe.wait_ge(a["s_pt"], 2 * n)
                    else:
                        pe.wait_ge(a["s_filled"], 2)
                    t0 = a["bank"](4) * BANK
                    for src, dst in a["turns"]:
                        ins = pe.transpose(flat[:, t0 + dst:t0 + dst + P], prob[n % 3][:, src:src + P], ident[:])
                    ins.then_inc(a["s_turned"], 1)

                def values(n):
                    pe.wait_ge(a["s_pt"], 2 * n + 2)
                    tile = n // a["per"]
                    if n % a["per"] == 0 and tile >= 2:
                        pe.wait_ge(a["s_o_lo"], tile - 1)
                    rows = P // a["per"]
                    r0 = rows * (n % a["per"])
                    o = ps[r0:r0 + rows, a["o_banks"][tile % 2], :]
                    last = len(a["values"]) - 1
                    for x_, (j, src, q0_, nq, start) in enumerate(a["values"]):
                        ins = pe.matmul(o[:, q0_:q0_ + nq], value(n, j), prob_t[n % 2][:, src:src + nq],
                                        start=start, stop=x_ == last)
                    ins.then_inc(a["s_head"], 1)

                for n in range(H + 3):
                    if n < H:
                        scores(n)
                    if n == a["s_bufs"] - 1:
                        extra()
                    if n >= 3:
                        values(n - 3)
                    if 2 <= n < H + 2:
                        turns(n - 2)
                    if n in tail:
                        next_unit(tail.index(n))

            def turn_memory(l):
                name = f"mem_t{l}"
                g = GROUP0[name]
                src = (mem_nat0, mem_nat1)[l]
                pe.wait_ge(s_mn[l], MB)
                pe.wait_ge(s_free[g % 2], free_needed(g))
                for b in range(4):
                    for m in range(2 * b, 2 * b + 2):
                        for t in range(MB):
                            ins = pe.transpose(ps[:, bank(g, b), (m % 2) * M + t * P:(m % 2) * M + (t + 1) * P],
                                               src[:, t, m * P:(m + 1) * P], ident[:])
                    ins.then_inc(s_done[name], 1)

            def memory_keys(l):
                a, u0 = ATTN[f"attn{l}"], UNIT0[f"attn{l}"]
                pe.wait_ge(s_ml[l], DB)
                for j in range(4):
                    pe.wait_ge(s_split, u0 + j + 1)
                    half = (u0 + j) % SPLIT
                    for m in range(4):
                        o = ps[:, a["bank"](4 + m // 2), (m % 2) * M:(m % 2 + 1) * M]
                        for kk in range(2):
                            k = 2 * j + kk
                            mh, ml = mem_hi[:, k, :], mem_lo[:, k, :]
                            whi, wlo = w_hi[:, half, kk, P * m:P * (m + 1)], w_lo[:, half, kk, P * m:P * (m + 1)]
                            ins = pe.matmul(o, whi, mh, start=k == 0 and m % 2 == 0, stop=False, skip_group_check=True)
                            if m == 0 and kk == 0:
                                ins.then_inc(s_used, 1)
                            pe.matmul(o, whi, ml, start=False, stop=False, skip_group_check=True)
                            ins = pe.matmul(o, wlo, mh, start=False, stop=k == DB - 1, skip_group_check=True)
                        if j == 3 and m % 2:
                            ins.then_inc(a["s_filler"], 1)

            def memory_values(l):
                a, u0 = ATTN[f"xattn{l}"], UNIT0[f"xattn{l}"]
                mem_h, mem_l = ((mem2_hi, mem2_lo), (mem_hi, mem_lo))[l]
                for j in range(4):
                    pe.wait_ge(s_split, u0 + j + 1)
                    half = (u0 + j) % SPLIT
                    for t in range(MB):
                        o = ps[:, a["bank"](4 + t), :]
                        for kk in range(2):
                            k = 2 * j + kk
                            mh, ml = mem_h[:, k, t * P:(t + 1) * P], mem_l[:, k, t * P:(t + 1) * P]
                            ins = pe.matmul(o, mh, w_hi[:, half, kk, :], start=k == 0, stop=False)
                            if t == 0 and kk == 0:
                                ins.then_inc(s_used, 1)
                            pe.matmul(o, mh, w_lo[:, half, kk, :], start=False, stop=False)
                            ins = pe.matmul(o, ml, w_hi[:, half, kk, :], start=False, stop=k == DB - 1)
                        if j == 3:
                            ins.then_inc(a["s_filler"], 1)

            pe.wait_ge(s_ident, 16)
            pe.wait_ge(s_x, 16 * TB)
            for m in range(DB):
                for t in range(TB):
                    ins = pe.transpose(ps[:, m, t * P:(t + 1) * P], x_nat[:, t, m * P:(m + 1) * P], ident[:])
                ins.then_inc(s_done["x_t"], 1)
            pe.wait_ge(s_const, 1)
            stage("in_xy", 4, z, s_done["in_xy"], ready=z_ready("mix0"), norm="mix0")
            for hd in range(LRU_HEADS):
                g, u0 = GROUP0["gates"] + hd, UNIT0["gates"] + hd
                group(g, g, u0, u0, 1, lambda k: f(2 * hd + k), s_done["gates"],
                      before=lambda k: pe.wait_ge(s_xcl, 2 * hd + k + 1))
            turn_memory(0)
            stage("in_qkv", 4, z, s_done["in_qkv"])

            a = ATTN["attn0"]

            def fill0():
                pe.wait_ge(s_v0t, 4)
                for j in range(TB):
                    for c in range(4):
                        ins = pe.transpose(ps[:, a["bank"](4 + j), c * P:(c + 1) * P],
                                           v0_t[:, c, j * P:(j + 1) * P], ident[:])
                    ins.then_inc(s_v0p, 1)
                pe.wait_ge(s_v0, 4)
                memory_keys(0)

            def mixer_ready(k):
                pe.wait_ge(s_recl, min(k + 1, DB))
                if k >= DB:
                    pe.wait_ge(a["s_o_lo"], k - DB + 1)
            out0 = ("out0", 6, f, s_done["out0"], mixer_ready)

            attention(a, lambda n: q0[HD * (n % 2):HD * (n % 2) + HD, n // 2, :],
                      lambda n: k0[HD * (n % 2):HD * (n % 2) + HD, n // 2, :],
                      lambda n, j: v0[:, j, HD * n:HD * n + HD], lambda: pe.wait_ge(s_q0, 8), fill0, ahead(*out0), (8, 9))
            stage(*out0, first=2)

            for l in (0, 1):
                if l:
                    stage("qkv_q0", 4, z, s_done["qkv_q0"], ready=z_ready("mix1"), norm="mix1")
                    pe.wait_ge(s_rms, NORM["mix1"] + 1)
                    g, u0 = GROUP0["qkv_kv"], UNIT0["qkv_kv"]
                    pe.wait_ge(s_free[g % 2], free_needed(g))
                    for j in range(2):
                        pe.wait_ge(s_split, u0 + j + 1)
                        half = (u0 + j) % SPLIT
                        for m in range(2):
                            for q_ in range(4):
                                k = 4 * j + q_
                                c0 = 256 * (q_ // 2) + P * m
                                ins = product(ps[:, bank(g, m), :], half, q_ % 2, c0, c0 + P, *z(k), k == 0, k == DB - 1,
                                              m == 0 and q_ == 0)
                            if j == 1:
                                ins.then_inc(s_done["qkv_kv"], 1)
                    turn_memory(1)
                    stage("qkv_q1", 4, z, s_done["qkv_q1"])
                    a1 = ATTN["attn1"]

                    def fill1():
                        pe.wait_ge(s_qkv1b, 6)
                        for j in range(TB):
                            ins = pe.transpose(ps[:, a1["bank"](6), j * P:(j + 1) * P], v1_t[:, j * P:(j + 1) * P], ident[:])
                        ins.then_inc(s_v1p, 1)
                        memory_keys(1)
                        pe.wait_ge(s_v1, 1)

                    def rotated():
                        pe.wait_ge(s_k1, 4)
                    out1 = ("out1", 4, f, s_done["out1"], lambda k: pe.wait_ge(a1["s_o_lo"], k + 1))
                    attention(a1, lambda n: q1[HD * (n % 2):HD * (n % 2) + HD, n // 2, :],
                              lambda n: k1[HD * (n % 2):HD * (n % 2) + HD, n // 8, :],
                              lambda n, j: v1[:, j, HD * (n // 8):HD * (n // 8) + HD], rotated, fill1,
                              ahead(*out1), (16, 17))
                    stage(*out1, first=2)

                stage(f"xq{l}", 4, z, s_done[f"xq{l}"], ready=z_ready(f"xa{l}"), norm=f"xa{l}")
                ax = ATTN[f"xattn{l}"]

                xo = (f"xo{l}", 2, f, s_done[f"xo{l}"], lambda k: pe.wait_ge(ax["s_o_lo"], k + 1))
                attention(ax, lambda n: qx[:, n, :], lambda n: mk[:, n, :],
                          lambda n, j: mv[:, j, P * n:P * (n + 1)], lambda: pe.wait_ge(s_xq[l], 4),
                          lambda: memory_values(l), ahead(*xo), (5,))
                stage(*xo, first=1)
                for c in range(2):
                    stage(f"up{l}{c}", 4, z, s_ff, ready=z_ready(f"ffn{l}") if c == 0 else None,
                          norm=f"ffn{l}" if c == 0 else None)
                    tiles = D_FF // P * l + sum(CHUNK[:c])
                    stage(f"down{l}{c}", CHUNK[c] // 2, f, s_done[f"down{l}{c}"],
                          ready=lambda k: pe.wait_ge(s_ff_lo, tiles + k + 1))

            g = GROUP0["final"]
            pe.wait_ge(s_free[(g + 1) % 2], free_needed(g + 1))
            norm_sum("final", g)
            for m in range(DB):
                pe.wait_ge(s_zl, NORM["final"] * DB + m + 1)
                for t in range(TB):
                    ins = pe.transpose(ps[:, m, t * P:(t + 1) * P], y_t[:, m, t * P:(t + 1) * P], ident[:])
                ins.then_inc(s_fin, 1)

        @block.vector
        def _(dve):
            chain = Chain(dve, s_dve)
            link = chain.link

            def residual(norm, done, first=False, bias=None, group0=0, norm_next=True):
                def low(m):
                    if norm != "final":
                        dve.wait_ge(s_zh, NORM[norm] * DB + m + 1)
                        dve.scalar_tensor_tensor(z_lo[:, m, :], h[:, m, :], v(f"g_{norm}", m), z_hi[:, m, :].bitcast(F32),
                                                 ALU.mult, ALU.subtract).then_inc(s_zl, 1)
                    dve.wait_ge(s_sq, NORM[norm] * DB + m + 1)
                    if m == 0:
                        link(dve.tensor_copy(acc[:], sq[:, 0, :]))
                    elif m < DB - 1:
                        link(dve.tensor_tensor(acc[:], acc[:], sq[:, m % 2, :], ALU.add))
                    else:
                        dve.tensor_tensor(acc[:], acc[:], sq[:, m % 2, :], ALU.add).then_inc(s_acc, 1)

                for m in range(DB):
                    dve.wait_ge(done, m + 1)
                    b = bank(group0 + m // 4, m % 4)
                    if first:
                        ins = dve.tensor_copy(h[:, m, :], ps[:, b, :])
                    elif bias:
                        ins = dve.scalar_tensor_tensor(h[:, m, :], ps[:, b, :], v(bias, m), h[:, m, :], ALU.add, ALU.add)
                    else:
                        ins = dve.tensor_tensor(h[:, m, :], ps[:, b, :], h[:, m, :], ALU.add)
                    link(ins)
                    dve.nop().then_inc(s_free[b // 4], 1)
                    if norm_next:
                        dve.nop().then_inc(s_h, 1)
                        if m >= 1:
                            low(m - 1)
                if norm_next:
                    low(DB - 1)

            def one_over_rms(norm):
                dve.wait_ge(s_rms, NORM[norm] + 1)
                dve.reciprocal(rstd[:], sq[:, 0, :]).then_inc(s_rstd, 1)
                dve.wait_ge(s_rstd, NORM[norm] + 1)

            def scaled(dst, g, m, done, count, free=1):
                dve.wait_ge(done, count)
                b = bank(g, m)
                link(dve.tensor_tensor(dst, ps[:, b, :], rstd[:], ALU.mult))
                dve.nop().then_inc(s_free[b // 4], free)

            def rotate(dst, src, tmp, done_sem):
                swap = list(range(8, 16)) + list(range(8)) + list(range(16, 32))
                link(dve.stream_shuffle(tmp[0][:], src, swap))
                dve.tensor_tensor(tmp[1][:], src, cos_t[:], ALU.mult)
                link(dve.tensor_tensor(tmp[0][:], tmp[0][:], sin_t[:], ALU.mult))
                dve.tensor_tensor(dst, tmp[1][:], tmp[0][:], ALU.add).then_inc(done_sem, 1)

            def memory_norm(l):
                src = (mem_nat0, mem_nat1)[l]
                dve.wait_ge(s_mr[l], 1)
                link(dve.reciprocal(small[:, 2:4], small[:, 0:2]))
                for t in range(MB):
                    dve.tensor_scalar(src[:, t, :], src[:, t, :], small[:, 2 + t:3 + t], None,
                                      ALU.mult).then_inc(s_mn[l], 1)

            def memory_low(l):
                g = GROUP0[f"mem_t{l}"]
                for m in range(DB):
                    dve.wait_ge(s_mh[l], m // 2 * 2 + 2)
                    b = bank(g, m // 2)
                    ins = dve.scalar_tensor_tensor(mem_lo[:, m, :], ps[:, b, (m % 2) * M:(m % 2 + 1) * M],
                                                   v(f"g_mem{l}", m), mem_hi[:, m, :].bitcast(F32), ALU.mult,
                                                   ALU.subtract)
                    ins.then_inc(s_ml[l], 1)
                    if m % 2:
                        dve.wait_ge(s_ml[l], m + 1)
                        dve.nop().then_inc(s_free[b // 4], 1)

            def attention(a, extra=None):
                H = a["heads"]
                dst = (mk[:, :, :] if a["masks"] else mv[:, :, :]).rearrange("p a n -> p (a n)")

                def maxima(n):
                    st = stat[:, n % 3]
                    dve.wait_ge(a["s_scores"], n + 1)
                    b0 = BANK * (a["bank"](0) + 2 * (n % a["s_bufs"]))
                    src, s0 = flat, b0
                    if a["masks"]:
                        if n >= 3:
                            dve.wait_ge(a["s_turned"], n - 2)
                        mask = m0 if a["name"] == "attn0" else m1
                        for c, w, mc in a["masks"]:
                            ins = dve.scalar_tensor_tensor(prob[n % 3][:, c:c + w], flat[:, b0 + c:b0 + c + w], a["scale"],
                                                           mask[:, mc:mc + w], ALU.mult, ALU.add)
                        ins.then_inc(a["s_read"], 1)
                        dve.wait_ge(a["s_read"], n + 1)
                        src, s0 = prob[n % 3], 0
                    tile = 0
                    for c, k, w in a["reduces"]:
                        ins = dve.tensor_reduce(st[:, 0, tile:tile + k],
                                                src[:, s0 + c:s0 + c + k * w].rearrange("p (k w) -> p k w", w=w),
                                                AX.X, ALU.max)
                        tile += k
                    link(ins)
                    if a["sink"]:
                        link(dve.tensor_scalar(st[:, 0, :], st[:, 0, :], v("sinks", n), None, ALU.max))
                    factor = -1.0 if a["masks"] else -a["scale"]
                    dve.tensor_scalar(st[:, 1, :], st[:, 0, :], factor, None, ALU.mult).then_inc(a["s_max"], 1)

                def denominator(n):
                    st = stat[:, n % 3]
                    dve.wait_ge(a["s_exp"], n + 1)
                    if a["sink"]:
                        link(dve.tensor_tensor(st[:, 2, :], st[:, 2, :], st[:, 3, :], ALU.add))
                    dve.reciprocal(st[:, 4, :], st[:, 2, :]).then_inc(a["s_rden"], 1)

                def turned(n):
                    dve.wait_ge(a["s_turned"], n + 1)
                    if n >= 2:
                        dve.wait_ge(a["s_head"], n - 1)
                    t0, c, w = a["bank"](4) * BANK, a["t_dve"], a["t_width"] - a["t_dve"]
                    dve.tensor_copy(prob_t[n % 2][:, c:c + w], flat[:, t0 + c:t0 + c + w]).then_inc(a["s_pt"], 1)

                def output(tile):
                    dve.wait_ge(a["s_o_hi"], tile + 1)
                    k = a["tile0"] + tile
                    dve.tensor_tensor(f_lo[:, k, :], ps[:, a["o_banks"][tile % 2], :], f_hi[:, k, :].bitcast(F32),
                                      ALU.subtract).then_inc(a["s_o_lo"], 1)

                for n in range(H + 4):
                    if n < H:
                        maxima(n)
                    if n == H - 1 and a["masks"] and a["tiles"] != 4:
                        dve.nop().then_inc(s_free[GROUP0[a["name"]] % 2], 4)
                    if 1 <= n <= H:
                        denominator(n - 1)
                    if n == 0 and a["name"] == "attn0":
                        for d_, s_ in ((mem2_hi, mem_hi), (mem2_lo, mem_lo)):
                            dve.tensor_copy(d_[:], s_).then_inc(s_mem2, 1)
                    if n == a["s_bufs"] - 1:
                        if extra:
                            extra()
                        for b in range(2):
                            dve.wait_ge(a["s_filler"], b + 1)
                            dve.tensor_copy(dst[:, BANK * b:BANK * (b + 1)],
                                            ps[:, a["bank"](4 + b), :]).then_inc(a["s_filled"], 1)
                    if n >= 4 and (n - 4) % a["per"] == a["per"] - 1:
                        tile = (n - 4) // a["per"]
                        output(tile)
                        if a["name"] == "attn0" and tile == 2:
                            dve.wait_ge(a["s_o_lo"], 3)
                            dve.nop().then_inc(s_free[GROUP0[a["name"]] % 2], 4)
                    if 2 <= n < H + 2:
                        turned(n - 2)
                dve.wait_ge(a["s_o_lo"], a["tiles"])
                dve.nop().then_inc(s_free[(GROUP0[a["name"]] + 1) % 2], 4)

            dve.memset(ones[:], 1.0).then_inc(s_const, 1)
            for b in range(2):
                link(dve.memset(xpad[b][:, 0:CONV - 1], 0.0))
            dve.wait_ge(s_vec, 16)
            lam, S = v("lam", 0, DB), [small[:, 8 * i:8 * i + 8] for i in range(8)]
            link(dve.scalar_tensor_tensor(S[1], lam, -1.0, lam, ALU.mult, ALU.max))
            link(dve.tensor_scalar(S[1], S[1], -1.0, None, ALU.mult))
            dve.nop().then_inc(s_sp_e, 1)

            residual("mix0", s_done["x_t"], first=True)

            dve.wait_ge(s_sp_e, 2)
            link(dve.tensor_scalar(S[3], S[2], 2.0, None, ALU.add))
            link(dve.reciprocal(S[3], S[3]))
            link(dve.tensor_tensor(S[3], S[2], S[3], ALU.mult))
            link(dve.tensor_tensor(S[4], S[3], S[3], ALU.mult))
            link(dve.tensor_scalar(S[5], S[4], 1.0 / 17.0, None, ALU.mult))
            for odd in (15, 13, 11, 9, 7, 5, 3):
                link(dve.scalar_tensor_tensor(S[5], S[5], 1.0 / odd, S[4], ALU.add, ALU.mult))
            link(dve.scalar_tensor_tensor(S[5], S[5], 1.0, S[3], ALU.add, ALU.mult))
            link(dve.tensor_scalar(S[6], lam, -1.0, 0.0, ALU.mult, ALU.max))
            link(dve.scalar_tensor_tensor(S[6], S[5], 2.0, S[6], ALU.mult, ALU.add))
            link(dve.tensor_scalar(S[7], S[6], LRU_C, None, ALU.mult))
            dve.tensor_scalar(S[6], S[6], -LRU_C, None, ALU.mult).then_inc(s_sp, 1)

            one_over_rms("mix0")
            g0 = GROUP0["in_xy"]

            def conv(m):
                dve.wait_ge(s_c0, m + 1)
                for tap in range(1, CONV):
                    ins = dve.scalar_tensor_tensor(xc[:, m, :], xpad[m % 2][:, tap:tap + T],
                                                   v("conv_w", tap * DB + m), xc[:, m, :], ALU.mult, ALU.add)
                    if tap < CONV - 1:
                        link(ins)
                ins.then_inc(s_xc, 1)

            def conv_low(m):
                dve.wait_ge(s_xch, m + 1)
                dve.tensor_tensor(f_lo[:, m, :], xc[:, m, :], f_hi[:, m, :].bitcast(F32), ALU.subtract).then_inc(s_xcl, 1)

            def in_tile(m, y):
                return g0 + 2 * (m // 4) + y, m % 4, s_done["in_xy"], 8 * (m // 4) + 4 * y + m % 4 + 1

            for m0_ in (0, 4):
                for i in range(6):
                    m = m0_ + i
                    if i < 4:
                        if m >= 2:
                            dve.wait_ge(s_xc, m - 1)
                        scaled(xpad[m % 2][:, CONV - 1:CONV - 1 + T], *in_tile(m, 0))
                        dve.nop().then_inc(s_xp, 1)
                    if 1 <= i <= 4:
                        conv(m - 1)
                    if i >= 2:
                        conv_low(m - 2)
                if m0_ == 0:
                    memory_norm(0)
                for m in range(m0_, m0_ + 4):
                    scaled(yg[:, m, :], *in_tile(m, 1))
                    dve.nop().then_inc(s_y, 1)

            for m in range(DB):
                dve.wait_ge(s_gate, m + 1)
                dve.tensor_tensor(xc[:, m, :], gate_i[:, m % 2, :], xc[:, m, :], ALU.mult).then_inc(s_gx, 1)

            def decay(m):
                dve.wait_ge(s_at, m + 1)
                link(dve.tensor_scalar(lru_d[:, m % 2, :], lru_r[:, m, :], 1.0, None, ALU.add))
                link(dve.reciprocal(lru_d[:, m % 2, :], lru_d[:, m % 2, :]))
                dve.tensor_tensor(lru_r[:, m, :], lru_r[:, m, :], lru_d[:, m % 2, :], ALU.mult).then_inc(s_lq, 1)

            def recur(m):
                dve.wait_ge(s_ls, m + 1)
                link(dve.tensor_tensor(lru_r[:, m, :], lru_r[:, m, :], xc[:, m, :], ALU.mult))
                link(dve.tensor_tensor_scan(xc[:, m, :], lru_a[:, m, :], lru_r[:, m, :], 0.0, ALU.mult, ALU.add))
                dve.wait_ge(s_yg, m + 1)
                dve.tensor_tensor(xc[:, m, :], xc[:, m, :], yg[:, m, :], ALU.mult).then_inc(s_rec, 1)

            def rec_low(m):
                dve.wait_ge(s_rech, m + 1)
                dve.tensor_tensor(f_lo[:, m, :], xc[:, m, :], f_hi[:, m, :].bitcast(F32), ALU.subtract).then_inc(s_recl, 1)

            memory_low(0)
            for m in range(DB):
                decay(m)
            g0 = GROUP0["in_qkv"]
            dve.wait_ge(s_rope, 32)

            def qk_tile(t):
                scaled(rope0[0][:], g0 + t // 4, t % 4, s_done["in_qkv"], t + 1)
                rotate(q0[:, t, :] if t < 4 else k0[:, t - 4, :], rope0[0][:], rope0[1:], s_q0)

            for t in range(4):
                qk_tile(t)
            for m in range(4):
                recur(m)
                if m:
                    rec_low(m - 1)
            for t in range(4, 8):
                qk_tile(t)
            for m in range(4, DB):
                recur(m)
                rec_low(m - 1)
            rec_low(DB - 1)
            dve.wait_ge(s_done["in_qkv"], 12)
            for t in range(4):
                b = bank(g0 + 2, t)
                link(dve.tensor_tensor(v0_t[:, t, :], ps[:, b, :], rstd[:], ALU.mult))
                dve.nop().then_inc(s_free[b // 4], 1)
            dve.nop().then_inc(s_v0t, 4)
            dve.wait_ge(s_mask0, 16)
            attention(ATTN["attn0"])
            residual("xa0", s_done["out0"], group0=GROUP0["out0"])

            for l in (0, 1):
                if l:
                    one_over_rms("mix1")

                    def qkv1(dst, done, group, m, t, free=1):
                        scaled(dst, GROUP0[group], m, done, m + 1, free)
                        dve.nop().then_inc(s_qkv1, 1)

                    def rotate_q(t):
                        dve.wait_ge(s_qkv1b, t + (1 if t < 4 else 3))
                        dve.wait_ge(s_q1, t + 1)
                        rotate(q1[:, t, :], q1[:, t, :], rope1, s_q1)

                    for t in range(4):
                        qkv1(q1[:, t, :], s_done["qkv_q0"], "qkv_q0", t, t)
                    qkv1(k1_in[:], s_done["qkv_kv"], "qkv_kv", 0, 8, 2)
                    qkv1(v1_t[:], s_done["qkv_kv"], "qkv_kv", 1, 9, 2)
                    dve.wait_ge(s_qkv1b, 5)
                    rotate(k1_rot[:], k1_in[:], rope1, s_q1)
                    dve.wait_ge(s_q1, 1)
                    for kv in range(2):
                        for half in range(2):
                            dve.tensor_copy(k1[HD * half:HD * half + HD, kv, :],
                                            k1_rot[HD * kv:HD * kv + HD, :]).then_inc(s_k1, 1)
                    memory_low(1)
                    for t in range(4):
                        rotate_q(t)
                    for t in range(4, 8):
                        qkv1(q1[:, t, :], s_done["qkv_q1"], "qkv_q1", t - 4, t)
                    dve.wait_ge(s_mask1, 16)
                    attention(ATTN["attn1"], lambda: [rotate_q(t) for t in range(4, 8)])
                    residual("xa1", s_done["out1"], bias="b_out", group0=GROUP0["out1"])
                one_over_rms(f"xa{l}")
                for t in range(4):
                    scaled(qx[:, t, :], GROUP0[f"xq{l}"], t, s_done[f"xq{l}"], t + 1)
                    dve.nop().then_inc(s_xq[l], 1)
                attention(ATTN[f"xattn{l}"])
                residual(f"ffn{l}", s_done[f"xo{l}"], group0=GROUP0[f"xo{l}"])
                one_over_rms(f"ffn{l}")
                if l == 0:
                    memory_norm(1)
                for c in range(2):
                    g0 = GROUP0[f"up{l}{c}"]
                    n0 = (D_FF // P * l + sum(CHUNK[:c])) // 2

                    def ff_group(i, s, g_static):
                        n = n0 + 2 * i + s
                        b0 = (g_static % 2) * 4
                        for p in range(2):
                            dve.wait_ge(s_ff, 4 * n + p + 1)
                            dve.tensor_tensor(ff_g[:, p, :], ps[:, b0 + p, :], rstd[:], ALU.mult).then_inc(s_ff_gate, 1)
                        for p in range(2):
                            dve.wait_ge(s_ff, 4 * n + p + 3)
                            dve.tensor_tensor(ff_u[:, p, :], ps[:, b0 + 2 + p, :], rstd[:], ALU.mult).then_inc(s_ff_up, 1)
                        dve.wait_ge(s_ff_gate, 2 * n + 2)
                        dve.wait_ge(s_ff_up, 2 * n + 2)
                        dve.nop().then_inc(s_free[g_static % 2], 4)
                        for p in range(2):
                            dve.wait_ge(s_ff_silu, 2 * n + p + 1)
                            dve.tensor_tensor(ff_u[:, p, :], ff_g[:, p, :], ff_u[:, p, :], ALU.mult).then_inc(s_ff_prod, 1)
                        for p in range(2):
                            tile = bass.ds(4 * i + (2 * s + p), 1)
                            dve.wait_ge(s_ff_hi, 2 * n + p + 1)
                            dve.tensor_tensor(f_lo[:, tile, :], ff_u[:, p:p + 1, :], f_hi[:, tile, :].bitcast(F32),
                                              ALU.subtract).then_inc(s_ff_lo, 1)
                        dve.wait_ge(s_ff_lo, 2 * n + 2)

                    groups = CHUNK[c] // 2

                    def body(i):
                        for s in range(2):
                            ff_group(i, s, g0 + s)
                    loop(dve, groups // 2, body)
                    if groups % 2:
                        ff_group(groups // 2, 0, g0)
                    nxt = ("mix1", "final")[l]
                    residual(nxt, s_done[f"down{l}{c}"], group0=GROUP0[f"down{l}{c}"], norm_next=c == 1)

            one_over_rms("final")
            for m in range(DB):
                dve.scalar_tensor_tensor(y_t[:, m, :], h[:, m, :], v("g_final", m), rstd[:], ALU.mult,
                                         ALU.mult).then_inc(s_zl, 1)
            for m in range(1, DB, 2):
                dve.wait_ge(s_fin, m + 1)
                dve.wait_ge(s_fin_o, m)
                dve.tensor_copy(y_out[:, :, m * P:(m + 1) * P],
                                ps[:, m, :].rearrange("p (t n) -> p t n", t=TB)).then_inc(s_fin_o, 1)

        @block.scalar
        def _(act):
            def residual(norm):
                for m in range(DB):
                    act.wait_ge(s_h, NORM[norm] * DB + m + 1)
                    if norm != "final":
                        act.activation(z_hi[:, m, :], h[:, m, :], ACT.Identity, scale=v(f"g_{norm}", m)).then_inc(s_zh, 1)
                    if m >= 2:
                        if norm != "final":
                            act.wait_ge(s_zl, NORM[norm] * DB + m)
                        else:
                            act.wait_ge(s_h, NORM[norm] * DB + m + 1)
                    act.activation(sq[:, m % 2, :], h[:, m, :], ACT.Square).then_inc(s_sq, 1)
                act.wait_ge(s_sum, NORM[norm] + 1)
                act.activation(sq[:, 0, :], ps[:, rms_bank[norm], :], ACT.Sqrt, bias=v("eps"), scale=1.0 / D).then_inc(s_rms, 1)

            rms_bank = {"mix0": bank(GROUP0["in_xy"] + 1, 0), "mix1": bank(GROUP0["qkv_q0"] + 1, 0),
                        "final": bank(GROUP0["final"], 0)}
            for l in (0, 1):
                rms_bank[f"xa{l}"] = bank(GROUP0[f"xq{l}"] + 1, 0)
                rms_bank[f"ffn{l}"] = bank(GROUP0[f"up{l}0"] + 1, 0)

            def memory_norm(l):
                src, scratch = (mem_nat0, mem_nat1)[l], (mk, mk)[l]
                act.wait_ge(s_mem[l], 16)
                for t in range(MB):
                    for half in range(2):
                        act.activation(mk[:, 2 * half:2 * half + 2, :].rearrange("p a n -> p (a n)"),
                                       src[:, t, 512 * half:512 * half + 512], ACT.Square,
                                       accum_out=small[:, 4 + 2 * t + half:5 + 2 * t + half]).then_inc(s_ms[l], 1)
                        act.wait_ge(s_ms[l], 2 * t + half + 1)
                act.activation(small[:, 0:2], small[:, 4:8].rearrange("p (t a) -> p t a", a=2)[:, :, 0], ACT.Identity).then_inc(s_ms[l], 1)
                act.wait_ge(s_ms[l], 5)
                for t in range(MB):
                    act.activation(small[:, t:t + 1], small[:, 5 + 2 * t:6 + 2 * t], ACT.Identity, bias=small[:, t:t + 1]).then_inc(s_ms[l], 1)
                act.wait_ge(s_ms[l], 7)
                act.activation(small[:, 0:2], small[:, 0:2], ACT.Sqrt, bias=v("eps"), scale=1.0 / D).then_inc(s_mr[l], 1)

            def memory_high(l):
                g = GROUP0[f"mem_t{l}"]
                for m in range(DB):
                    act.wait_ge(s_done[f"mem_t{l}"], m // 2 + 1)
                    act.activation(mem_hi[:, m, :], ps[:, bank(g, m // 2), (m % 2) * M:(m % 2 + 1) * M], ACT.Identity,
                                   scale=v(f"g_mem{l}", m)).then_inc(s_mh[l], 1)

            def attention(a):
                H = a["heads"]

                def exps(n):
                    st = stat[:, n % 3]
                    act.wait_ge(a["s_max"], n + 1)
                    if a["masks"]:
                        src, s0, scale = prob[n % 3], 0, 1.0
                    else:
                        if n >= 3:
                            act.wait_ge(a["s_turned"], n - 2)
                        src, s0, scale = flat, BANK * (a["bank"](0) + 2 * (n % a["s_bufs"])), a["scale"]
                    if a["sink"]:
                        act.activation(st[:, 3, :], st[:, 1, :], ACT.Exp, bias=v("sinks", n))
                    for i, (c, w) in enumerate(a["probs"]):
                        ins = act.activation(prob[n % 3][:, c:c + w], src[:, s0 + c:s0 + c + w], ACT.Exp,
                                             bias=st[:, 1, i:i + 1], scale=scale, accum_out=st[:, 2, i:i + 1])
                    ins.then_inc(a["s_exp"], 1)
                    if not a["masks"]:
                        act.wait_ge(a["s_exp"], n + 1)
                        act.nop().then_inc(a["s_read"], 1)

                def turned(n):
                    act.wait_ge(a["s_turned"], n + 1)
                    if n >= 2:
                        act.wait_ge(a["s_head"], n - 1)
                    t0 = a["bank"](4) * BANK
                    for c in range(0, a["t_dve"], BANK):
                        w = min(BANK, a["t_dve"] - c)
                        ins = act.activation(prob_t[n % 2][:, c:c + w], flat[:, t0 + c:t0 + c + w], ACT.Copy)
                    ins.then_inc(a["s_pt"], 1)

                def output(tile):
                    act.wait_ge(a["s_head"], a["per"] * (tile + 1))
                    if a["name"] == "attn0" and tile == 0:
                        act.wait_ge(s_mem2, 2)
                    act.activation(f_hi[:, a["tile0"] + tile, :], ps[:, a["o_banks"][tile % 2], :], ACT.Copy).then_inc(a["s_o_hi"], 1)

                for n in range(H + 4):
                    if n >= 4 and (n - 4) % a["per"] == a["per"] - 1:
                        output((n - 4) // a["per"])
                    if 2 <= n < H + 2:
                        turned(n - 2)
                    if n < H:
                        exps(n)
                    if n == H - 1 and not a["masks"]:
                        act.nop().then_inc(s_free[GROUP0[a["name"]] % 2], 4)

            act.wait_ge(s_vec, 16)
            act.wait_ge(s_sp_e, 1)
            act.activation(small[:, 16:24], small[:, 8:16], ACT.Exp).then_inc(s_sp_e, 1)
            residual("mix0")
            for m0_ in (0, 4):
                if m0_ == 0:
                    memory_norm(0)
                for i in range(5):
                    m = m0_ + i
                    if i < 4:
                        act.wait_ge(s_xp, m + 1)
                        act.activation(xc[:, m, :], xpad[m % 2][:, 0:T], ACT.Identity, bias=v("conv_b", m),
                                       scale=v("conv_w", m)).then_inc(s_c0, 1)
                    if i >= 1:
                        act.wait_ge(s_xc, m)
                        act.activation(f_hi[:, m - 1, :], xc[:, m - 1, :], ACT.Copy).then_inc(s_xch, 1)
                for m in range(m0_, m0_ + 4):
                    act.wait_ge(s_y, m + 1)
                    act.activation(yg[:, m, :], yg[:, m, :], ACT.Gelu_apprx_tanh).then_inc(s_yg, 1)
            act.wait_ge(s_sp, 1)
            for hd in range(LRU_HEADS):
                g = GROUP0["gates"] + hd
                act.wait_ge(s_done["gates"], 4 * (hd + 1))
                for p in range(2):
                    m = 2 * hd + p
                    act.activation(lru_r[:, m, :], ps[:, bank(g, p), :], ACT.Sigmoid, bias=v("ba", m)).then_inc(s_act, 1)
                    if m >= 2:
                        act.wait_ge(s_gx, m - 1)
                    act.activation(gate_i[:, p, :], ps[:, bank(g, 2 + p), :], ACT.Sigmoid, bias=v("bx", m)).then_inc(s_gate, 1)
                act.wait_ge(s_gate, 2 * hd + 2)
                act.wait_ge(s_act, 2 * hd + 2)
                act.nop().then_inc(s_free[g % 2], 4)
            memory_high(0)
            for m in range(DB):
                act.activation(lru_a[:, m, :], lru_r[:, m, :], ACT.Exp, scale=small[:, 48:56][:, m:m + 1])
                act.activation(lru_r[:, m, :], lru_r[:, m, :], ACT.Tanh, scale=small[:, 56:64][:, m:m + 1]).then_inc(s_at, 1)
            for m in range(DB):
                act.wait_ge(s_lq, m + 1)
                act.activation(lru_r[:, m, :], lru_r[:, m, :], ACT.Sqrt, scale=2.0).then_inc(s_ls, 1)
            for m in range(DB):
                act.wait_ge(s_rec, m + 1)
                act.activation(f_hi[:, m, :], xc[:, m, :], ACT.Copy).then_inc(s_rech, 1)
            for j in range(TB):
                act.wait_ge(s_v0p, j + 1)
                act.activation(v0[:, j, :], ps[:, ATTN["attn0"]["bank"](4 + j), :], ACT.Copy).then_inc(s_v0, 1)
            attention(ATTN["attn0"])
            residual("xa0")
            for l in (0, 1):
                if l:
                    def bias(t, n, x_):
                        act.wait_ge(s_qkv1, n)
                        act.activation(x_, x_, ACT.Identity, bias=v("b_qkv", t)).then_inc(s_qkv1b, 1)
                    for t in range(4):
                        bias(t, t + 1, q1[:, t, :])
                    bias(8, 5, k1_in[:])
                    bias(9, 6, v1_t[:])
                    memory_high(1)
                    for t in range(4, 8):
                        bias(t, t + 3, q1[:, t, :])
                    act.wait_ge(s_v1p, 1)
                    act.activation(v1[:, :, :].rearrange("p a n -> p (a n)"), ps[:, ATTN["attn1"]["bank"](6), :],
                                   ACT.Copy).then_inc(s_v1, 1)
                    attention(ATTN["attn1"])
                    residual("xa1")
                attention(ATTN[f"xattn{l}"])
                residual(f"ffn{l}")
                if l == 0:
                    memory_norm(1)
                for c in range(2):
                    n0 = (D_FF // P * l + sum(CHUNK[:c])) // 2

                    def ff_group(i, s):
                        n = n0 + 2 * i + s
                        for p in range(2):
                            act.wait_ge(s_ff_gate, 2 * n + p + 1)
                            act.activation(ff_g[:, p, :], ff_g[:, p, :], ACT.Silu).then_inc(s_ff_silu, 1)
                        for p in range(2):
                            act.wait_ge(s_ff_prod, 2 * n + p + 1)
                            act.activation(f_hi[:, bass.ds(4 * i + (2 * s + p), 1), :], ff_u[:, p:p + 1, :],
                                           ACT.Copy).then_inc(s_ff_hi, 1)

                    groups = CHUNK[c] // 2

                    def body(i):
                        for s in range(2):
                            ff_group(i, s)
                    loop(act, groups // 2, body)
                    if groups % 2:
                        ff_group(groups // 2, 0)
                residual(("mix1", "final")[l])
            for m in range(0, DB, 2):
                act.wait_ge(s_fin, m + 1)
                if m:
                    act.wait_ge(s_fin_o, m)
                act.activation(y_out[:, :, m * P:(m + 1) * P], ps[:, m, :].rearrange("p (t n) -> p t n", t=TB),
                               ACT.Copy).then_inc(s_fin_o, 1)


def tables():
    import math
    import numpy as np

    q, k = np.arange(P)[:, None], np.arange(P)[None, :]

    def dist(blocks):
        return q - k + P * blocks
    strip = []
    for blocks in (3, 2, 1, 0):
        d = dist(blocks)
        count = (d <= 128).astype(int) + (d % 4 == 0) + (d % 16 == 0)
        strip.append(np.where((d >= 0) & (count > 0), np.log(np.maximum(count, 1)), NEG))
    mask0 = np.concatenate(strip, axis=1).astype(np.float32)
    pair = np.concatenate([np.where((dist(b) >= 0) & (dist(b) <= 127), 0.0, NEG) for b in (1, 0)], axis=1)
    mask1 = np.tile(pair, (1, TB)).astype(np.float32)
    rot = HD // 4
    inv = np.float32(500000.0) ** (-np.arange(0, rot, 2, dtype=np.float32) / np.float32(rot))
    ang = np.arange(T, dtype=np.float32)[:, None] * inv.astype(np.float32)[None, :]
    cos, sin = np.cos(ang).T, np.sin(ang).T
    cos_t, sin_t = np.ones((P, T), np.float32), np.zeros((P, T), np.float32)
    for head in (0, HD):
        for half in range(2):
            r = head + half * rot // 2
            cos_t[r:r + rot // 2] = cos
            sin_t[r:r + rot // 2] = sin if half else -sin
    return dict(mask0=mask0, mask1=mask1, rope_cos=cos_t, rope_sin=sin_t, identity=np.eye(P, dtype=np.float32))


def kernel(**inputs):
    import numpy as np
    import concourse.bacc as bacc
    from concourse.bass_utils import run_bass_kernel_spmd as run

    a = {k: np.asarray(w) for k, w in inputs.items()}

    def cols(w):
        return w.reshape(-1, P).T

    packed = [cols(a["mix_norm"][0]), cols(a["xa_norm"][0]), cols(a["ffn_norm"][0]), cols(a["mix_norm"][1]),
              cols(a["xa_norm"][1]), cols(a["ffn_norm"][1]), cols(a["final_norm"]), cols(a["xa_mem_norm"][0]),
              cols(a["xa_mem_norm"][1]), cols(a["lru_conv_w"][0].reshape(-1)), cols(a["lru_conv_b"][0]),
              cols(a["lru_ba"][0].reshape(-1)), cols(a["lru_bx"][0].reshape(-1)), cols(a["lru_lambda"][0]),
              cols(a["c_b_qkv"][0]), cols(a["c_b_out"][0]), np.broadcast_to(a["c_sinks"][0], (P, C_HEADS)),
              np.full((P, 1), EPS, np.float32)]
    arrays = dict(
        x=a["x"][0], mem=a["mem"][0], w_in=a["ab_w_in"][0], w_gates=np.stack([a["lru_wa"][0], a["lru_wx"][0]]),
        w_out0=a["ab_w_out"][0], w_qkv=a["c_w_qkv"][0], w_out1=a["c_w_out"][0], xa_wq=a["xa_wq"], xa_wkv=a["xa_wkv"],
        xa_wo=a["xa_wo"], w_gate_up=a["ffn_w_gate_up"], w_down=a["ffn_w_down"],
        vectors=np.concatenate(packed, axis=1), **tables())
    arrays = {k: np.ascontiguousarray(w) for k, w in arrays.items()}
    nc = bacc.Bacc("TRN2", target_bir_lowering=False, num_devices=1)
    args = {k: nc.dram_tensor(f"in_{k}", w.shape, mybir.dt.from_np(w.dtype), kind="ExternalInput").ap()
            for k, w in arrays.items()}
    out = nc.dram_tensor("out", (T, D), F32, kind="ExternalOutput").ap()
    trunk(nc, out=out, **args)
    r = run(nc, [{f"in_{k}": w for k, w in arrays.items()}], core_ids=[0])
    return np.asarray(r.results[0]["out"]).reshape(1, T, D)
```

```python
import concourse.bass as bass
from concourse import mybir
from contextlib import ExitStack

F32 = mybir.dt.float32
F32R = mybir.dt.float32r
ALU = mybir.AluOpType
ACT = mybir.ActivationFunctionType
AX = mybir.AxisListType

P = 128
T = 512
D = 1024
DB = D // P
TB = T // P
M = 256
MB = M // P
LRU_HEADS = 4
B_HEADS = 8
C_HEADS = 16
HD = 64
XH = 4
D_FF = 2816
EPS = 1e-6
LRU_C = 8.0
CONV = 4
NEG = -1e30
BANK = 512
RAW = 4
SPLIT = 2
CHUNK = (12, 10)

STAGES = [("x_t", 2, 0), ("in_xy", 4, 4), ("gates", 4, 1), ("mem_t0", 1, 0), ("in_qkv", 3, 4),
          ("attn0", 2, 2), ("out0", 2, 6)]
for _l in (0, 1):
    if _l:
        STAGES += [("qkv_q0", 1, 4), ("qkv_q1", 1, 4), ("mem_t1", 1, 0), ("qkv_kv", 1, 2), ("attn1", 2, 2), ("out1", 2, 4)]
    STAGES += [(f"xq{_l}", 1, 4), (f"xattn{_l}", 2, 2), (f"xo{_l}", 2, 2),
               (f"up{_l}0", CHUNK[0] // 2, 4), (f"down{_l}0", 2, CHUNK[0] // 2),
               (f"up{_l}1", CHUNK[1] // 2, 4), (f"down{_l}1", 2, CHUNK[1] // 2)]
STAGES.append(("final", 2, 0))
GROUP0, UNIT0, GROUPS = {}, {}, {}
_g = _u = 0
for _n, _ng, _nu in STAGES:
    GROUP0[_n], UNIT0[_n], GROUPS[_n] = _g, _u, _ng
    _g += _ng
    _u += _ng * _nu
UNITS = _u

OUT_ORDER = (1, 2, 3, 0)
NORMS = ("mix0", "xa0", "ffn0", "mix1", "xa1", "ffn1", "final")
NORM = {n: i for i, n in enumerate(NORMS)}
COL = {}
_c = 0
for _n, _w in [(f"g_{n}", DB) for n in NORMS] + [("g_mem0", DB), ("g_mem1", DB), ("conv_w", CONV * DB), ("conv_b", DB),
                                                ("ba", DB), ("bx", DB), ("lam", DB), ("b_qkv", 10), ("b_out", DB),
                                                ("sinks", C_HEADS), ("eps", 1)]:
    COL[_n] = _c
    _c += _w
NCOL = _c


def attention_plan(kind):
    if kind == "xattn":
        scores = [(i, 0, M, M * i) for i in range(TB)]
        return dict(width=TB * M, scores=scores, reduces=[(0, TB, M)], masks=[], probs=[(M * i, M) for i in range(TB)],
                    turns=[(M * i + P * j, BANK * j + P * i) for j in range(MB) for i in range(TB)],
                    t_width=MB * BANK, values=[(j, BANK * j, 0, T, j == 0) for j in range(MB)])
    if kind == "attn1":
        start = [2 * P * i + (P if i == 0 else 0) for i in range(TB)]
        scores = [(i, max(i - 1, 0) * P, P if i == 0 else 2 * P, start[i]) for i in range(TB)]
        blocks = [(0, 0)] + [(i, j) for i in range(1, TB) for j in (i - 1, i)]
        return dict(width=TB * 2 * P, scores=scores, reduces=[(P, 1, P), (2 * P, TB - 1, 2 * P)],
                    masks=[(P, (2 * TB - 1) * P, P)], probs=[(start[i], P if i == 0 else 2 * P) for i in range(TB)],
                    turns=[(2 * P * i + P * (j - i + 1), P * n) for n, (i, j) in enumerate(blocks)],
                    t_width=len(blocks) * P,
                    values=[(j, P * n, P * i, P, n == 0) for n, (i, j) in enumerate(blocks)])
    start = [0, P, BANK, 2 * BANK]
    t_start = [0, BANK, 2 * BANK, BANK + 3 * P]
    return dict(width=3 * BANK, scores=[(i, 0, P * (i + 1), start[i]) for i in range(TB)],
                reduces=[(start[i], 1, P * (i + 1)) for i in range(TB)],
                masks=[(start[i], P * (i + 1), (TB - 1 - i) * P) for i in range(TB)],
                probs=[(start[i], P * (i + 1)) for i in range(TB)],
                turns=[(start[i] + P * j, t_start[j] + P * (i - j)) for j in range(TB) for i in range(j, TB)],
                t_width=2 * BANK + 2 * P,
                values=[(j, t_start[j], P * j, T - P * j, j == 0) for j in range(TB)])


def trunk(nc, x, mem, w_in, w_gates, w_out0, w_qkv, w_out1, xa_wq, xa_wkv, xa_wo, w_gate_up, w_down,
          vectors, mask0, mask1, rope_cos, rope_sin, identity, out):
    ctx = ExitStack()
    with ctx:
        base = 16512
        top = [base]

        def at(name, shape, dt, offset):
            return nc.alloc_sbuf_tensor_at(name, shape, dt, offset=offset)

        def zone(nbytes):
            top[0] += nbytes
            return top[0] - nbytes

        z_h = zone(4 * DB * T)
        z_zh, z_zl = zone(4 * DB * T), zone(4 * DB * T)
        z_raw = zone(RAW * 4096)
        z_wh, z_wl = zone(SPLIT * 4096), zone(SPLIT * 4096)
        z_fh, z_fl = zone(4 * CHUNK[0] * T), zone(4 * CHUNK[0] * T)
        z_x, z_y = zone(4 * DB * T), zone(4 * DB * T)
        z_q, z_k, z_v = zone(8192), zone(8192), zone(8192)
        z_mk, z_mv = zone(4096), zone(4096)
        z_const = zone(0)

        h = at("h", [P, DB, T], F32, z_h)
        z_hi = at("z_hi", [P, DB, T], F32R, z_zh)
        z_lo = at("z_lo", [P, DB, T], F32R, z_zl)
        raw = at("raw", [P, RAW, 2, 512], F32, z_raw)
        w_hi = at("w_hi", [P, SPLIT, 2, 512], F32R, z_wh)
        w_lo = at("w_lo", [P, SPLIT, 2, 512], F32R, z_wl)
        f_hi = at("f_hi", [P, CHUNK[0], T], F32R, z_fh)
        f_lo = at("f_lo", [P, CHUNK[0], T], F32R, z_fl)
        lru_r = at("lru_r", [P, DB, T], F32, z_fh)
        lru_a = at("lru_a", [P, DB, T], F32, z_fl)
        mem_hi = f_hi[:, 8:12, :].rearrange("p a (b n) -> p (a b) n", n=M)
        mem_lo = f_lo[:, 8:12, :].rearrange("p a (b n) -> p (a b) n", n=M)
        mem2_lo = at("mem2_lo", [P, DB, M], F32R, z_x)
        xc = at("xc", [P, DB, T], F32, z_x)
        q1 = at("q1", [P, DB, T], F32, z_x)
        x_nat = at("x_nat", [P, TB, D], F32, z_y)
        yg = at("yg", [P, DB, T], F32, z_y)
        mem2_hi = at("mem2_hi", [P, DB, M], F32R, z_y)
        ff_g = at("ff_g", [P, 2, T], F32, z_y)
        ff_u = at("ff_u", [P, 2, T], F32, z_y + 4096)
        rope1 = [at(f"rope1_{i}", [P, T], F32, z_y + 2048 * i) for i in range(2)]
        k1_in = at("k1_in", [P, T], F32, z_y + 4096)
        mem_nat1 = at("mem_nat1", [P, MB, D], F32, z_y + 8192)
        mem_nat0 = at("mem_nat0", [P, MB, D], F32, z_q)
        q0 = at("q0", [P, 4, T], F32, z_q)
        qx = at("qx", [P, 4, T], F32, z_q)
        xpad = [at(f"xpad{i}", [P, T + CONV], F32, z_k + 2080 * i) for i in range(2)]
        k0 = at("k0", [P, 4, T], F32, z_k)
        k1 = at("k1", [P, 2, T], F32, z_k)
        m1 = at("m1", [P, 2 * TB * P], F32, z_k + 4096)
        rope0 = [at(f"rope0_{i}", [P, T], F32, z_v + 2048 * i) for i in range(3)]
        v0 = at("v0", [P, TB, 512], F32, z_v)
        k1_rot = at("k1_rot", [P, T], F32, z_v)
        v1_t = at("v1_t", [P, T], F32, z_v + 2048)
        v1 = at("v1", [P, TB, P], F32, z_v + 4096)
        mk = at("mk", [P, XH, M], F32, z_mk)
        mv = at("mv", [P, MB, 512], F32, z_mv)
        gate_i = at("gate_i", [P, 2, T], F32, z_mk)
        lru_d = at("lru_d", [P, 2, T], F32, z_mv)
        v0_t = at("v0_t", [P, 4, T], F32, z_x)
        prob = [at(f"prob{i}", [P, 3 * BANK], F32, z_zh + 6144 * i) for i in range(3)]
        m0 = at("m0", [P, TB * P], F32, z_zh + 30720)
        prob_t = [at(f"prob_t{i}", [P, 3 * BANK], F32, z_zh + 18432 + 6144 * i) for i in range(2)]
        y_t = at("y_t", [P, DB, T], F32, z_zh)
        y_out = at("y_out", [P, TB, D], F32, z_zl)
        sq = at("sq", [P, 2, T], F32, z_const)
        acc = at("acc", [P, T], F32, z_const + 4096)
        rstd = at("rstd", [P, T], F32, z_const + 6144)
        ident = at("ident", [P, P], F32, z_const + 8192)
        ones = at("ones", [P, P], F32, z_const + 8704)
        vec = at("vec", [P, NCOL], F32, z_const + 9216)
        z_small = z_const + 9216 + (4 * NCOL + 31) // 32 * 32
        small = at("small", [P, 8 * 8], F32, z_small)
        neg_sinks = at("neg_sinks", [P, C_HEADS], F32, z_small + 32)
        root = at("root", [P, 1], F32, z_small + 4640)
        stat = at("stat", [P, 3, 6, TB], F32, z_small + 256)
        cos_t = at("cos_t", [P, T], F32, z_small + 544)
        sin_t = at("sin_t", [P, T], F32, z_small + 2592)
        assert z_small + 4644 <= nc.sbuf_usable_end, (z_small + 4640, nc.sbuf_usable_end)

        ps = ctx.enter_context(nc.psum_tensor("ps", [P, 8, BANK], F32))
        flat = ps[:, :, :].rearrange("p b n -> p (b n)")

        def bank(group, m):
            return (group % 2) * 4 + m

        def sem(name):
            return ctx.enter_context(nc.semaphore(name))

        def v(name, m=0, n=1):
            return vec[:, COL[name] + m:COL[name] + m + n]

        s_ident, s_vec, s_rope, s_mask0, s_mask1 = [sem(n) for n in
                                                    ("s_ident", "s_vec", "s_rope", "s_mask0", "s_mask1")]
        s_x = [sem("s_x_left"), sem("s_x_right")]
        s_mem = [sem("s_mem0"), sem("s_mem1")]
        s_raw = [sem(f"s_raw{i}") for i in range(RAW)]
        s_begun = sem("s_weight_begun")
        s_hi = sem("s_weight_hi")
        s_split = sem("s_weight_split")
        s_used = sem("s_weight_used")
        s_free = [sem("s_banks_free0"), sem("s_banks_free1")]
        s_done = {n: sem(f"s_done_{n}") for n, _, _ in STAGES if n[:2] not in ("up", "do") and "attn" not in n}
        s_done |= {f"down{l}{c}": sem(f"s_done_down{l}{c}") for l in (0, 1) for c in (0, 1)}
        s_ff = sem("s_ff_tiles")
        s_ff_gate, s_ff_silu, s_ff_up = sem("s_ff_gate"), sem("s_ff_silu"), sem("s_ff_up")
        s_ff_prod, s_ff_hi, s_ff_lo = sem("s_ff_prod"), sem("s_ff_hi"), sem("s_ff_lo")
        s_h = sem("s_h")
        s_sq = sem("s_sq")
        s_acc = sem("s_acc")
        s_zh = sem("s_z_hi")
        s_zl = sem("s_z_lo")
        s_sum = sem("s_sum")
        s_rms = sem("s_rms")
        s_rstd = sem("s_rstd")
        s_dve, s_act = sem("s_dve_chain"), sem("s_act_chain")
        s_const = sem("s_const")
        s_xp, s_c0, s_xc = sem("s_x_scaled"), sem("s_conv_first"), sem("s_conv")
        s_xch, s_xcl = sem("s_conv_hi"), sem("s_conv_lo")
        s_y, s_yg = sem("s_y_scaled"), sem("s_gelu")
        s_sp_e, s_sp = sem("s_exp_lambda"), sem("s_softplus")
        s_gate, s_gx = sem("s_gate_i"), sem("s_gated_input")
        s_at, s_lq, s_ls = sem("s_decay"), sem("s_one_minus_a2"), sem("s_input_scale")
        s_rec, s_rech, s_recl = sem("s_rec"), sem("s_rec_hi"), sem("s_rec_lo")
        s_q0, s_v0t, s_v0p, s_v0 = sem("s_qk0"), sem("s_v0_t"), sem("s_v0_turned"), sem("s_v0")
        s_qkv1, s_qkv1b, s_q1 = sem("s_qkv1"), sem("s_qkv1_biased"), sem("s_qk1_rotated")
        s_v1p, s_v1, s_k1 = sem("s_v1_turned"), sem("s_v1"), sem("s_k1")
        s_ms, s_mr, s_mn = [sem("s_ms0"), sem("s_ms1")], [sem("s_mr0"), sem("s_mr1")], [sem("s_mn0"), sem("s_mn1")]
        s_mem2 = sem("s_mem_copied")
        s_mh, s_ml = [sem("s_mh0"), sem("s_mh1")], [sem("s_ml0"), sem("s_ml1")]
        s_xq = [sem("s_xq0"), sem("s_xq1")]
        s_fin, s_fin_o = [sem("s_final_t0"), sem("s_final_t1")], [sem("s_final_out0"), sem("s_final_out1")]
        s_out = sem("s_out")

        ATTN = {}
        for name, heads, plan, tiles in (("attn0", B_HEADS, "attn0", 4), ("xattn0", XH, "xattn", 4),
                                         ("attn1", C_HEADS, "attn1", 8), ("xattn1", XH, "xattn", 4)):
            a = dict(name=name, heads=heads, tiles=tiles, per=heads // tiles, **attention_plan(plan))
            a["bank"] = lambda i, g=GROUP0[name]: (i + 4 * (g % 2)) % 8
            a["s_bufs"] = 1 if plan == "attn0" else 2
            a["o_banks"] = [a["bank"](i) for i in ((3, 7) if plan == "attn0" else (6, 7))]
            a["scale"] = P ** -0.5 if plan == "xattn" else HD ** -0.5
            a["dve_splits"] = 2 if plan == "xattn" else 0
            a["turned_first"] = plan == "xattn"
            a["sink"] = plan == "attn1"
            a["t_dve"] = a["t_width"] if plan == "attn0" else (a["t_width"] - 1) // BANK * BANK
            a["copies"] = 1 if plan == "attn0" else 2
            a["tile0"] = 8 if plan == "attn0" else 0
            a["output_at"] = {}
            for tile in range(tiles):
                n = a["per"] * (tile + 1) - 1
                a["output_at"][n + (4 if n + 4 < heads else 3)] = tile
            for s in ("scores", "read", "max", "exp", "rden", "prob", "turned", "pt", "head", "o_hi", "o_lo",
                      "filler", "filled"):
                a["s_" + s] = sem(f"s_{name}_{s}")
            ATTN[name] = a

        class Chain:
            def __init__(self, eng, s):
                self.eng, self.s, self.n = eng, s, 0

            def link(self, ins):
                self.n += 1
                ins.then_inc(self.s, 1)
                self.eng.wait_ge(self.s, self.n)

        def loop(eng, count, body):
            if count == 1:
                body(0)
            elif count > 1:
                with eng.Fori(0, count) as i:
                    body(i)

        def free_needed(group):
            return 4 * (group // 2)

        block = ctx.enter_context(nc.Block())

        @block.sync
        def _(sp):
            sp.dma_start(ident[:], identity).then_inc(s_ident, 16)
            sp.dma_start(vec[:], vectors).then_inc(s_vec, 16)

            def load_x(half):
                c = slice(half * D // 2, (half + 1) * D // 2)
                for t in range(TB):
                    sp.dma_start(x_nat[:, t, c], x[t * P:(t + 1) * P, c]).then_inc(s_x[half], 16)
            seen = [0]

            def unit(u, parts):
                u_static = seen[0]
                seen[0] += 1
                if u_static >= RAW:
                    sp.wait_ge(s_split, u - RAW + 1)
                for lo, hi, src in parts:
                    sp.dma_start(raw[:, u_static % RAW, :, lo:hi], src).then_inc(s_raw[u_static % RAW], 32 // len(parts))

            def rows(w, r0, col, n=512):
                return w[r0:r0 + 2 * P, bass.ds(col, n)].rearrange("(a p) n -> p a n", p=P)

            def stream(name, w, units, col0=0, first=0, count=None):
                n = GROUPS[name] if count is None else count
                u0 = UNIT0[name] + first * units

                def body(i):
                    keep = seen[0]
                    for j in range(units):
                        unit(u0 + units * i + j, [(0, 512, rows(w, 2 * P * j, (first + i) * 512 + col0))])
                    seen[0] = keep + units
                if units % RAW == 0:
                    loop(sp, n, body)
                    seen[0] = u0 + n * units
                else:
                    for i in range(n):
                        body(i)

            def ff(l, c):
                u0 = UNIT0[f"up{l}{c}"]
                f0 = sum(CHUNK[:c]) * P

                def body(i):
                    for j in range(4):
                        unit(u0 + 4 * i + j, [(0, 256, rows(w_gate_up[l], 2 * P * j, i * 256 + f0, 256)),
                                              (256, 512, rows(w_gate_up[l], 2 * P * j, i * 256 + f0 + D_FF, 256))])
                loop(sp, CHUNK[c] // 2, body)
                seen[0] = UNIT0[f"down{l}{c}"]
                stream(f"down{l}{c}", w_down[l][f0:f0 + CHUNK[c] * P, :], CHUNK[c] // 2)

            load_x(0)
            for j in range(4):
                unit(j, [(0, 512, rows(w_in, 2 * P * j, 0))])
                if j == 0:
                    load_x(1)
            sp.dma_start(mem_nat0[:], mem.rearrange("(a p) n -> p a n", p=P)).then_inc(s_mem[0], 16)
            for i, col in ((1, D), (2, 512), (3, D + 512)):
                for j in range(4):
                    unit(UNIT0["in_xy"] + 4 * i + j, [(0, 512, rows(w_in, 2 * P * j, col))])
            sp.dma_start(cos_t[:], rope_cos).then_inc(s_rope, 16)
            sp.dma_start(sin_t[:], rope_sin).then_inc(s_rope, 16)
            for hd in range(LRU_HEADS):
                unit(UNIT0["gates"] + hd, [(0, 256, w_gates[0][hd].rearrange("(a p) n -> p a n", p=P)),
                                           (256, 512, w_gates[1][hd].rearrange("(a p) n -> p a n", p=P))])
            stream("in_qkv", w_in, 4, col0=2 * D)
            for l in (0, 1):
                if l:
                    stream("qkv_q0", w_qkv, 4)
                    stream("qkv_q1", w_qkv, 4, col0=512)
                    for j in range(2):
                        src = w_qkv[4 * P * j:4 * P * (j + 1), D:D + 256].rearrange("(a p) n -> p a n", p=P)
                        unit(UNIT0["qkv_kv"] + j, [(0, 256, src[:, 0:2, :]), (256, 512, src[:, 2:4, :])])
                    sp.wait_ge(ATTN["attn0"]["s_scores"], B_HEADS)
                    sp.dma_start(m1[:], mask1).then_inc(s_mask1, 16)
                stream(f"attn{l}", xa_wkv[l], 4, count=1)
                if l == 0:
                    sp.wait_ge(s_done["in_qkv"], 12)
                    sp.dma_start(m0[:], mask0).then_inc(s_mask0, 16)
                stream(f"out{l}", (w_out0, w_out1)[l], (6, 4)[l])
                stream(f"xq{l}", xa_wq[l], 4)
                if l == 0:
                    sp.wait_ge(s_recl, DB)
                    sp.dma_start(mem_nat1[:], mem.rearrange("(a p) n -> p a n", p=P)).then_inc(s_mem[1], 16)
                stream(f"xattn{l}", xa_wkv[l], 4, col0=512, count=1)
                stream(f"xo{l}", xa_wo[l], 2)
                ff(l, 0)
                ff(l, 1)
            assert seen[0] == UNITS
            for i, t in enumerate(OUT_ORDER):
                for half in range(2):
                    sp.wait_ge(s_fin_o[half], i + 1)
                sp.dma_start(out[t * P:(t + 1) * P, :], y_out[:, t, :]).then_inc(s_out, 16)
            sp.wait_ge(s_out, 64)

        @block.gpsimd
        def _(pool):
            def split(u, j, empty=False):
                half = j % SPLIT
                pool.wait_ge(s_raw[j], (u - j + RAW) * (32 // RAW))
                if not empty:
                    pool.wait_ge(s_used, u - SPLIT + 2)
                pool.sem_inc(s_begun, 1)
                pool.tensor_scalar(w_hi[:, half], raw[:, j], 1.0, 1.0, ALU.mult, ALU.mult).then_inc(s_hi, 1)
                pool.wait_ge(s_hi, u + 1)
                pool.tensor_tensor(w_lo[:, half], raw[:, j], w_hi[:, half].bitcast(F32),
                                   ALU.subtract).then_inc(s_split, 1)

            def split_all(u0, u1):
                while u0 % RAW and u0 < u1:
                    split(u0, u0 % RAW)
                    u0 += 1

                def body(i):
                    for j in range(RAW):
                        split(i * RAW + (u0 + j), j)
                loop(pool, (u1 - u0) // RAW, body)
                for u in range(u0 + (u1 - u0) // RAW * RAW, u1):
                    split(u, u % RAW)

            def normalise(a, n):
                pool.wait_ge(a["s_rden"], n + 1)
                for i, (c, w) in enumerate(a["probs"]):
                    ins = pool.tensor_scalar(prob[n % 3][:, c:c + w], prob[n % 3][:, c:c + w],
                                             stat[:, n % 3, 4, i:i + 1], 1.0, ALU.mult, ALU.mult)
                ins.then_inc(a["s_prob"], 1)

            split(0, 0, empty=True)
            split(1, 1, empty=True)
            at_unit = SPLIT
            for name in ("attn0", "xattn0", "attn1", "xattn1"):
                last = UNIT0[name] + 4
                split_all(at_unit, last - ATTN[name]["dve_splits"])
                for n in range(ATTN[name]["heads"]):
                    normalise(ATTN[name], n)
                    if n == 0:
                        split(last, last % RAW)
                    if n == (ATTN[name]["heads"] - 1 if name[0] == "x" else 1):
                        split(last + 1, (last + 1) % RAW)
                at_unit = last + SPLIT
            split_all(at_unit, UNITS)

        @block.tensor
        def _(pe):
            def product(o, half, kk, c0, c1, rhi, rlo, start, stop, unit_starts):
                whi, wlo = w_hi[:, half, kk, c0:c1], w_lo[:, half, kk, c0:c1]
                ins = pe.matmul(o, whi, rhi, start=start, stop=False)
                if unit_starts:
                    ins.then_inc(s_used, 1)
                pe.matmul(o, whi, rlo, start=False, stop=False)
                return pe.matmul(o, wlo, rhi, start=False, stop=stop)

            def group(g_static, g, u0_static, u0, units, rhs, done, n=T, before=None, hook=None, first=0, last=None,
                      attention_told=False, only=False):
                for j in range(first, units if last is None else last):
                    rows_first = before and not (only and j == units - 1)
                    order = [(m, kk) for kk in range(2) for m in range(4)] if rows_first else [
                        (m, kk) for m in range(4) for kk in range(2)]
                    if j == 0:
                        if g_static >= 2:
                            pe.wait_ge(s_free[g_static % 2], 4 * (g_static // 2) + (g - g_static) * 2)
                    pe.wait_ge(s_split, u0 + j + 1)
                    half = (u0_static + j) % SPLIT
                    for x_, (m, kk) in enumerate(order):
                        k = 2 * j + kk
                        if before and m == 0:
                            before(k)
                        if hook and j == min(2, units - 1) and x_ == 4:
                            hook()
                        hi, lo = rhs(k)
                        ins = product(ps[:, bank(g_static, m), 0:n], half, kk, P * m, P * (m + 1), hi, lo,
                                      k == 0, k == 2 * units - 1, x_ == 0 and not (attention_told and j == 0))
                        if j == units - 1 and kk == 1:
                            ins.then_inc(done, 1)

            def stage(name, units, rhs, done, ready=None, norm=None, first=0):
                g0, u0, ng = GROUP0[name], UNIT0[name], GROUPS[name]
                hook = (lambda: norm_sum(norm, g0 + 1)) if norm else None
                group(g0, g0, u0, u0, units, rhs, done, before=ready, hook=hook, first=first, only=ng == 1)
                if norm and ng > 1:
                    pe.wait_ge(s_rms, NORM[norm] + 1)
                rest, at_g, at_u = ng - 1, g0 + 1, u0 + units

                def body(i):
                    for s in range(2):
                        group(at_g + s, at_g + s + 2 * i, at_u + units * s, at_u + units * s + 2 * units * i,
                              units, rhs, done)
                if units % SPLIT == 0:
                    if rest // 2:
                        loop(pe, rest // 2, body)
                    if rest % 2:
                        group(at_g + rest - 1, at_g + rest - 1, at_u + units * (rest - 1),
                              at_u + units * (rest - 1), units, rhs, done)
                else:
                    for s in range(rest):
                        group(at_g + s, at_g + s, at_u + units * s, at_u + units * s, units, rhs, done)

            def ahead(name, units, rhs, done, ready):
                g0, u0 = GROUP0[name], UNIT0[name]
                return lambda j: group(g0, g0, u0, u0, units, rhs, done, before=ready, first=j, last=j + 1,
                                       attention_told=True)

            def norm_sum(norm, g):
                pe.wait_ge(s_acc, NORM[norm] + 1)
                pe.wait_ge(s_free[g % 2], free_needed(g))
                pe.matmul(ps[:, bank(g, 3), :], ones[:], acc[:], start=True, stop=True).then_inc(s_sum, 1)

            def z(k):
                return z_hi[:, k, :], z_lo[:, k, :]

            def f(k):
                return f_hi[:, k, :], f_lo[:, k, :]

            def z_ready(norm):
                return lambda k: pe.wait_ge(s_zl, NORM[norm] * DB + k + 1)

            def attention(a, q, key, value, ready, extra, next_unit, tail):
                g = GROUP0[a["name"]]
                H = a["heads"]
                pe.wait_ge(s_free[g % 2], free_needed(g))

                def scores(n):
                    ready(n)
                    if n >= a["s_bufs"]:
                        pe.wait_ge(a["s_read"], n - a["s_bufs"] + 1)
                    b0 = BANK * (a["bank"](0) + 2 * (n % a["s_bufs"]))
                    for i, k0_, nk, c in a["scores"]:
                        ins = pe.matmul(flat[:, b0 + c:b0 + c + nk], q(n)[:, i * P:(i + 1) * P],
                                        key(n)[:, k0_:k0_ + nk], start=True, stop=True)
                        if n == 0 and i == 0 and a["name"] != "attn1":
                            ins.then_inc(s_used, 1)
                    ins.then_inc(a["s_scores"], 1)

                def turns(n):
                    pe.wait_ge(a["s_prob"], n + 1)
                    if n >= 1:
                        pe.wait_ge(a["s_pt"], a["copies"] * n)
                    elif a["name"] == "attn0":
                        pe.wait_ge(s_v0, TB)
                    elif a["name"] == "attn1":
                        pe.wait_ge(s_v1, 1)
                    t0 = a["bank"](4) * BANK
                    for src, dst in a["turns"]:
                        ins = pe.transpose(flat[:, t0 + dst:t0 + dst + P], prob[n % 3][:, src:src + P], ident[:])
                        if n == 0 and (src, dst) == a["turns"][0]:
                            ins.then_inc(s_used, 1)
                    ins.then_inc(a["s_turned"], 1)

                def values(n):
                    pe.wait_ge(a["s_pt"], a["copies"] * (n + 1))
                    tile = n // a["per"]
                    if n == 0:
                        pe.wait_ge(a["s_filled"], 2)
                    if n % a["per"] == 0 and tile >= 2:
                        pe.wait_ge(a["s_o_lo"], tile - 1)
                    rows = P // a["per"]
                    r0 = rows * (n % a["per"])
                    o = ps[r0:r0 + rows, a["o_banks"][tile % 2], :]
                    last = len(a["values"]) - 1
                    for x_, (j, src, q0_, nq, start) in enumerate(a["values"]):
                        ins = pe.matmul(o[:, q0_:q0_ + nq], value(n, j), prob_t[n % 2][:, src:src + nq],
                                        start=start, stop=x_ == last)
                    ins.then_inc(a["s_head"], 1)

                for n in range(H + 3):
                    if n < H:
                        scores(n)
                    if n in extra:
                        pe.wait_ge(s_free[(g + 1) % 2], free_needed(g + 1))
                        extra[n]()
                    if n >= 3:
                        values(n - 3)
                    if 2 <= n < H + 2:
                        turns(n - 2)
                    if n in tail:
                        next_unit(tail.index(n))

            def turn_memory(l):
                name = f"mem_t{l}"
                g = GROUP0[name]
                src = (mem_nat0, mem_nat1)[l]
                pe.wait_ge(s_mn[l], MB)
                pe.wait_ge(s_free[g % 2], free_needed(g))
                for b in range(4):
                    for m in range(2 * b, 2 * b + 2):
                        for t in range(MB):
                            ins = pe.transpose(ps[:, bank(g, b), (m % 2) * M + t * P:(m % 2) * M + (t + 1) * P],
                                               src[:, t, m * P:(m + 1) * P], ident[:])
                    ins.then_inc(s_done[name], 1)

            def memory_keys(l, units):
                a, u0 = ATTN[f"attn{l}"], UNIT0[f"attn{l}"]
                pe.wait_ge(s_ml[l], DB)
                for j in units:
                    pe.wait_ge(s_split, u0 + j + 1)
                    half = (u0 + j) % SPLIT
                    for m in range(4):
                        if l == 0 and j == 0 and m == 0:
                            pe.wait_ge(s_v0, 1)
                        o = ps[:, a["o_banks"][m // 2], (m % 2) * M:(m % 2 + 1) * M]
                        for kk in range(2):
                            k = 2 * j + kk
                            mh, ml = mem_hi[:, k, :], mem_lo[:, k, :]
                            whi, wlo = w_hi[:, half, kk, P * m:P * (m + 1)], w_lo[:, half, kk, P * m:P * (m + 1)]
                            ins = pe.matmul(o, whi, mh, start=k == 0 and m % 2 == 0, stop=False, skip_group_check=True)
                            if (j or l) and m == 0 and kk == 0:
                                ins.then_inc(s_used, 1)
                            pe.matmul(o, whi, ml, start=False, stop=False, skip_group_check=True)
                            ins = pe.matmul(o, wlo, mh, start=False, stop=k == DB - 1, skip_group_check=True)
                        if j == 3 and m % 2:
                            ins.then_inc(a["s_filler"], 1)

            def memory_values(l):
                a, u0 = ATTN[f"xattn{l}"], UNIT0[f"xattn{l}"]
                mem_h, mem_l = ((mem2_hi, mem2_lo), (mem_hi, mem_lo))[l]
                for j in range(4):
                    pe.wait_ge(s_split, u0 + j + 1)
                    half = (u0 + j) % SPLIT
                    for t in range(MB):
                        o = ps[:, a["o_banks"][t], :]
                        for kk in range(2):
                            k = 2 * j + kk
                            mh, ml = mem_h[:, k, t * P:(t + 1) * P], mem_l[:, k, t * P:(t + 1) * P]
                            ins = pe.matmul(o, mh, w_hi[:, half, kk, :], start=k == 0, stop=False)
                            if j and t == 0 and kk == 0:
                                ins.then_inc(s_used, 1)
                            pe.matmul(o, mh, w_lo[:, half, kk, :], start=False, stop=False)
                            ins = pe.matmul(o, ml, w_hi[:, half, kk, :], start=False, stop=k == DB - 1)
                        if j == 3:
                            ins.then_inc(a["s_filler"], 1)

            pe.wait_ge(s_ident, 16)
            def turn_x(half):
                pe.wait_ge(s_x[half], 16 * TB)
                for m in range(4 * half, 4 * half + 4):
                    for t in range(TB):
                        ins = pe.transpose(ps[:, m, t * P:(t + 1) * P], x_nat[:, t, m * P:(m + 1) * P], ident[:])
                    ins.then_inc(s_done["x_t"], 1)

            def first_ready(k):
                if k == 2:
                    turn_x(1)
                z_ready("mix0")(k)
            turn_x(0)
            pe.wait_ge(s_const, 1)
            stage("in_xy", 4, z, s_done["in_xy"], ready=first_ready, norm="mix0")
            for hd in range(LRU_HEADS):
                g, u0 = GROUP0["gates"] + hd, UNIT0["gates"] + hd
                group(g, g, u0, u0, 1, lambda k: f(2 * hd + k), s_done["gates"],
                      before=lambda k: pe.wait_ge(s_xcl, 2 * hd + k + 1))
            turn_memory(0)
            stage("in_qkv", 4, z, s_done["in_qkv"])

            a = ATTN["attn0"]

            def fill0():
                pe.wait_ge(s_v0t, 4)
                for j in range(TB):
                    for c in range(4):
                        ins = pe.transpose(ps[:, a["bank"](3 + j), c * P:(c + 1) * P],
                                           v0_t[:, c, j * P:(j + 1) * P], ident[:])
                    ins.then_inc(s_v0p, 1)
                memory_keys(0, (0, 1))

            def mixer_ready(k):
                pe.wait_ge(s_recl, min(k + 1, DB))
                if k >= DB:
                    pe.wait_ge(a["s_o_lo"], k - DB + 1)
            out0 = ("out0", 6, f, s_done["out0"], mixer_ready)

            attention(a, lambda n: q0[HD * (n % 2):HD * (n % 2) + HD, n // 2, :],
                      lambda n: k0[HD * (n % 2):HD * (n % 2) + HD, n // 2, :],
                      lambda n, j: v0[:, j, HD * n:HD * n + HD], lambda n: pe.wait_ge(s_q0, 5 + n // 2),
                      {0: fill0, 1: lambda: memory_keys(0, (2, 3))}, ahead(*out0), (8, 9))
            stage(*out0, first=2)

            for l in (0, 1):
                if l:
                    stage("qkv_q0", 4, z, s_done["qkv_q0"], ready=z_ready("mix1"), norm="mix1")
                    pe.wait_ge(s_rms, NORM["mix1"] + 1)
                    stage("qkv_q1", 4, z, s_done["qkv_q1"])
                    turn_memory(1)
                    g, u0 = GROUP0["qkv_kv"], UNIT0["qkv_kv"]
                    pe.wait_ge(s_free[g % 2], free_needed(g))
                    for j in range(2):
                        pe.wait_ge(s_split, u0 + j + 1)
                        half = (u0 + j) % SPLIT
                        for m in range(2):
                            for q_ in range(4):
                                k = 4 * j + q_
                                c0 = 256 * (q_ // 2) + P * m
                                ins = product(ps[:, bank(g, m), :], half, q_ % 2, c0, c0 + P, *z(k), k == 0, k == DB - 1,
                                              m == 0 and q_ == 0)
                            if j == 1:
                                ins.then_inc(s_done["qkv_kv"], 1)
                    memory_keys(1, (0, 1))
                    a1 = ATTN["attn1"]

                    def fill1():
                        pe.wait_ge(s_qkv1b, 10)
                        for j in range(TB):
                            ins = pe.transpose(ps[:, a1["bank"](4), j * P:(j + 1) * P], v1_t[:, j * P:(j + 1) * P], ident[:])
                        ins.then_inc(s_v1p, 1)
                        memory_keys(1, (2, 3))

                    def rotated(n):
                        if n == 0:
                            pe.wait_ge(s_k1, 4)
                        if n % 2 == 0 and n // 2 > 4:
                            pe.wait_ge(s_q1, 2 + n // 2)
                    out1 = ("out1", 4, f, s_done["out1"], lambda k: pe.wait_ge(a1["s_o_lo"], k + 1))
                    attention(a1, lambda n: q1[HD * (n % 2):HD * (n % 2) + HD, n // 2, :],
                              lambda n: k1[HD * (n % 2):HD * (n % 2) + HD, n // 8, :],
                              lambda n, j: v1[:, j, HD * (n // 8):HD * (n // 8) + HD], rotated, {1: fill1},
                              ahead(*out1), (16, 17))
                    stage(*out1, first=2)

                stage(f"xq{l}", 4, z, s_done[f"xq{l}"], ready=z_ready(f"xa{l}"), norm=f"xa{l}")
                ax = ATTN[f"xattn{l}"]

                xo = (f"xo{l}", 2, f, s_done[f"xo{l}"], lambda k: pe.wait_ge(ax["s_o_lo"], k + 1))
                attention(ax, lambda n: qx[:, n, :], lambda n: mk[:, n, :],
                          lambda n, j: mv[:, j, P * n:P * (n + 1)], lambda n: pe.wait_ge(s_xq[l], n + 1),
                          {1: lambda: memory_values(l)}, ahead(*xo), (5,))
                stage(*xo, first=1)
                for c in range(2):
                    stage(f"up{l}{c}", 4, z, s_ff, ready=z_ready(f"ffn{l}") if c == 0 else None,
                          norm=f"ffn{l}" if c == 0 else None)
                    tiles = D_FF // P * l + sum(CHUNK[:c])
                    stage(f"down{l}{c}", CHUNK[c] // 2, f, s_done[f"down{l}{c}"],
                          ready=lambda k: pe.wait_ge(s_ff_lo, tiles + k + 1))

            g = GROUP0["final"]

            def turn_out(g, half, tiles):
                for t in tiles:
                    for m in range(4 * half, 4 * half + 4):
                        ins = pe.transpose(ps[:, bank(g, t), (m % 4) * P:(m % 4 + 1) * P], y_t[:, m, t * P:(t + 1) * P],
                                           ident[:])
                    ins.then_inc(s_fin[half], 1)

            pe.wait_ge(s_free[g % 2], free_needed(g))
            pe.wait_ge(s_zh, NORM["final"] * DB + 4)
            turn_out(g, 0, OUT_ORDER)
            pe.wait_ge(s_free[(g + 1) % 2], free_needed(g + 1))
            pe.wait_ge(s_acc, NORM["final"] + 1)
            for t in range(TB):
                ins = pe.matmul(ps[:, bank(g + 1, 0), t:t + 1], acc[:, t * P:(t + 1) * P], ones[:, 0:1],
                                start=True, stop=True)
            ins.then_inc(s_sum, 1)
            pe.wait_ge(s_zh, NORM["final"] * DB + DB)
            turn_out(g + 1, 1, OUT_ORDER[:3])
            pe.wait_ge(s_rms, NORM["final"] + 1)
            turn_out(g + 1, 1, OUT_ORDER[3:])

        @block.vector
        def _(dve):
            chain = Chain(dve, s_dve)
            link = chain.link

            def residual(norm, done, bias=None, group0=0, norm_next=True):
                def low(m):
                    if norm != "final":
                        dve.wait_ge(s_zh, NORM[norm] * DB + m + 1)
                        dve.scalar_tensor_tensor(z_lo[:, m, :], h[:, m, :], v(f"g_{norm}", m), z_hi[:, m, :].bitcast(F32),
                                                 ALU.mult, ALU.subtract).then_inc(s_zl, 1)
                    dve.wait_ge(s_sq, NORM[norm] * DB + m + 1)
                    if m == 0:
                        ins = dve.tensor_copy(acc[:], sq[:, 0, :])
                    else:
                        ins = dve.tensor_tensor(acc[:], acc[:], sq[:, m % 2, :], ALU.add)
                    if m == DB - 1:
                        ins.then_inc(s_acc, 1)
                    elif norm != "final":
                        link(ins)
                    else:
                        ins.then_inc(s_zl, 1)
                        dve.wait_ge(s_zl, NORM[norm] * DB + m + 1)

                lag = 2 if norm == "final" else 1

                for m in range(DB if done else 0):
                    dve.wait_ge(done, m + 1)
                    b = bank(group0 + m // 4, m % 4)
                    if bias:
                        ins = dve.scalar_tensor_tensor(h[:, m, :], ps[:, b, :], v(bias, m), h[:, m, :], ALU.add, ALU.add)
                    else:
                        ins = dve.tensor_tensor(h[:, m, :], ps[:, b, :], h[:, m, :], ALU.add)
                    link(ins)
                    dve.nop().then_inc(s_free[b // 4], 1)
                    if norm_next:
                        dve.nop().then_inc(s_h, 1)
                        if m >= lag:
                            low(m - lag)
                if norm_next:
                    for m in range(DB - lag if done else 0, DB):
                        low(m)

            def one_over_rms(norm):
                dve.wait_ge(s_rms, NORM[norm] + 1)
                dve.reciprocal(rstd[:], sq[:, 0, :]).then_inc(s_rstd, 1)
                dve.wait_ge(s_rstd, NORM[norm] + 1)

            def scaled(dst, g, m, done, count, free=1):
                dve.wait_ge(done, count)
                b = bank(g, m)
                link(dve.tensor_tensor(dst, ps[:, b, :], rstd[:], ALU.mult))
                dve.nop().then_inc(s_free[b // 4], free)

            def rotate(dst, src, tmp, done_sem):
                swap = list(range(8, 16)) + list(range(8)) + list(range(16, 32))
                link(dve.stream_shuffle(tmp[0][:], src, swap))
                dve.tensor_tensor(tmp[1][:], src, cos_t[:], ALU.mult)
                link(dve.tensor_tensor(tmp[0][:], tmp[0][:], sin_t[:], ALU.mult))
                dve.tensor_tensor(dst, tmp[1][:], tmp[0][:], ALU.add).then_inc(done_sem, 1)

            def memory_norm(l):
                src = (mem_nat0, mem_nat1)[l]
                dve.wait_ge(s_mr[l], 1)
                link(dve.reciprocal(small[:, 2:4], small[:, 0:2]))
                for t in range(MB):
                    dve.tensor_scalar(src[:, t, :], src[:, t, :], small[:, 2 + t:3 + t], None,
                                      ALU.mult).then_inc(s_mn[l], 1)

            def memory_low(l):
                g = GROUP0[f"mem_t{l}"]
                for m in range(DB):
                    dve.wait_ge(s_mh[l], m // 2 * 2 + 2)
                    b = bank(g, m // 2)
                    ins = dve.scalar_tensor_tensor(mem_lo[:, m, :], ps[:, b, (m % 2) * M:(m % 2 + 1) * M],
                                                   v(f"g_mem{l}", m), mem_hi[:, m, :].bitcast(F32), ALU.mult,
                                                   ALU.subtract)
                    ins.then_inc(s_ml[l], 1)
                    if m % 2:
                        dve.wait_ge(s_ml[l], m + 1)
                        dve.nop().then_inc(s_free[b // 4], 1)

            def split(u):
                half = u % SPLIT
                dve.wait_ge(s_raw[u % RAW], (u - u % RAW + RAW) * (32 // RAW))
                dve.wait_ge(s_used, u - SPLIT + 2)
                dve.tensor_copy(w_hi[:, half], raw[:, u % RAW]).then_inc(s_hi, 1)
                dve.wait_ge(s_hi, u + 1)
                dve.tensor_tensor(w_lo[:, half], raw[:, u % RAW], w_hi[:, half].bitcast(F32),
                                  ALU.subtract).then_inc(s_split, 1)

            def attention(a, extra={}):
                H = a["heads"]
                dst = (mk[:, :, :] if a["masks"] else mv[:, :, :]).rearrange("p a n -> p (a n)")

                def maxima(n):
                    st = stat[:, n % 3]
                    dve.wait_ge(a["s_scores"], n + 1)
                    b0 = BANK * (a["bank"](0) + 2 * (n % a["s_bufs"]))
                    src, s0 = flat, b0
                    if a["masks"]:
                        if n >= 3:
                            dve.wait_ge(a["s_turned"], n - 2)
                        mask = m0 if a["name"] == "attn0" else m1
                        for c, w, mc in a["masks"]:
                            ins = dve.scalar_tensor_tensor(prob[n % 3][:, c:c + w], flat[:, b0 + c:b0 + c + w], a["scale"],
                                                           mask[:, mc:mc + w], ALU.mult, ALU.add)
                        ins.then_inc(a["s_read"], 1)
                        dve.wait_ge(a["s_read"], n + 1)
                        src, s0 = prob[n % 3], 0
                    tile, direct = 0, a["name"] == "attn0"
                    for c, k, w in a["reduces"]:
                        ins = dve.tensor_reduce(st[:, 1 if direct else 0, tile:tile + k],
                                                src[:, s0 + c:s0 + c + k * w].rearrange("p (k w) -> p k w", w=w),
                                                AX.X, ALU.max, negate=True)
                        tile += k
                    if a["sink"]:
                        link(ins)
                        ins = dve.tensor_scalar(st[:, 1, :], st[:, 0, :], neg_sinks[:, n:n + 1], None, ALU.min)
                    elif not direct:
                        link(ins)
                        ins = dve.tensor_scalar(st[:, 1, :], st[:, 0, :], a["scale"], None, ALU.mult)
                    ins.then_inc(a["s_max"], 1)

                def denominator(n):
                    st = stat[:, n % 3]
                    dve.wait_ge(a["s_exp"], n + 1)
                    if a["sink"]:
                        link(dve.tensor_tensor(st[:, 2, :], st[:, 2, :], st[:, 3, :], ALU.add))
                    dve.reciprocal(st[:, 4, :], st[:, 2, :]).then_inc(a["s_rden"], 1)

                def turned(n):
                    dve.wait_ge(a["s_turned"], n + 1)
                    if n >= 2:
                        dve.wait_ge(a["s_head"], n - 1)
                    t0, c, w = a["bank"](4) * BANK, a["t_dve"], a["t_width"] - a["t_dve"]
                    dve.tensor_copy(prob_t[n % 2][:, c:c + w], flat[:, t0 + c:t0 + c + w]).then_inc(a["s_pt"], 1)

                def output(tile):
                    dve.wait_ge(a["s_o_hi"], tile + 1)
                    k = a["tile0"] + tile
                    dve.tensor_tensor(f_lo[:, k, :], ps[:, a["o_banks"][tile % 2], :], f_hi[:, k, :].bitcast(F32),
                                      ALU.subtract).then_inc(a["s_o_lo"], 1)

                for n in range(H + 4):
                    if n < H:
                        maxima(n)
                    if n == H - 1 and a["masks"] and a["tiles"] != 4:
                        dve.nop().then_inc(s_free[GROUP0[a["name"]] % 2], 4)
                    if 1 <= n <= H:
                        denominator(n - 1)
                    if n == 1:
                        for i in range(a["dve_splits"]):
                            split(UNIT0[a["name"]] + 2 + i)
                        if n in extra:
                            extra[n]()
                        for b in range(2):
                            dve.wait_ge(a["s_filler"], b + 1)
                            dve.tensor_copy(dst[:, BANK * b:BANK * (b + 1)],
                                            ps[:, a["o_banks"][b], :]).then_inc(a["s_filled"], 1)
                    if 2 <= n < H + 2 and a["turned_first"]:
                        turned(n - 2)
                    if n in a["output_at"]:
                        tile = a["output_at"][n]
                        output(tile)
                        if a["name"] == "attn0" and tile == 2:
                            dve.wait_ge(a["s_o_lo"], 3)
                            dve.nop().then_inc(s_free[GROUP0[a["name"]] % 2], 4)
                    if 2 <= n < H + 2 and a["copies"] == 2 and not a["turned_first"]:
                        turned(n - 2)
                    if n in extra and n != 1:
                        extra[n]()
                dve.wait_ge(a["s_o_lo"], a["tiles"])
                dve.nop().then_inc(s_free[(GROUP0[a["name"]] + 1) % 2], 4)

            dve.memset(ones[:], 1.0).then_inc(s_const, 1)
            for b in range(2):
                link(dve.memset(xpad[b][:, 0:CONV - 1], 0.0))
            dve.wait_ge(s_vec, 16)
            lam, S = v("lam", 0, DB), [small[:, 8 * i:8 * i + 8] for i in range(8)]
            link(dve.scalar_tensor_tensor(S[1], lam, -1.0, lam, ALU.mult, ALU.max))
            link(dve.tensor_scalar(S[1], S[1], -1.0, None, ALU.mult))
            dve.nop().then_inc(s_sp_e, 1)

            residual("mix0", None)

            dve.wait_ge(s_sp_e, 2)
            link(dve.tensor_scalar(S[3], S[2], 2.0, None, ALU.add))
            link(dve.reciprocal(S[3], S[3]))
            link(dve.tensor_tensor(S[3], S[2], S[3], ALU.mult))
            link(dve.tensor_tensor(S[4], S[3], S[3], ALU.mult))
            link(dve.tensor_scalar(S[5], S[4], 1.0 / 17.0, None, ALU.mult))
            for odd in (15, 13, 11, 9, 7, 5, 3):
                link(dve.scalar_tensor_tensor(S[5], S[5], 1.0 / odd, S[4], ALU.add, ALU.mult))
            link(dve.scalar_tensor_tensor(S[5], S[5], 1.0, S[3], ALU.add, ALU.mult))
            link(dve.tensor_scalar(S[6], lam, -1.0, 0.0, ALU.mult, ALU.max))
            link(dve.scalar_tensor_tensor(S[6], S[5], 2.0, S[6], ALU.mult, ALU.add))
            link(dve.tensor_scalar(S[7], S[6], LRU_C, None, ALU.mult))
            dve.tensor_scalar(S[6], S[6], -LRU_C, None, ALU.mult).then_inc(s_sp, 1)

            one_over_rms("mix0")
            g0 = GROUP0["in_xy"]

            def conv(m):
                dve.wait_ge(s_c0, m + 1)
                for tap in range(1, CONV):
                    ins = dve.scalar_tensor_tensor(xc[:, m, :], xpad[m % 2][:, tap:tap + T],
                                                   v("conv_w", tap * DB + m), xc[:, m, :], ALU.mult, ALU.add)
                    if tap < CONV - 1:
                        link(ins)
                ins.then_inc(s_xc, 1)

            def conv_low(m):
                dve.wait_ge(s_xch, m + 1)
                dve.tensor_tensor(f_lo[:, m, :], xc[:, m, :], f_hi[:, m, :].bitcast(F32), ALU.subtract).then_inc(s_xcl, 1)

            def in_tile(m, y):
                return g0 + 2 * (m // 4) + y, m % 4, s_done["in_xy"], 8 * (m // 4) + 4 * y + m % 4 + 1

            for m0_ in (0, 4):
                for i in range(6):
                    m = m0_ + i
                    if i < 4:
                        if m >= 2:
                            dve.wait_ge(s_xc, m - 1)
                        scaled(xpad[m % 2][:, CONV - 1:CONV - 1 + T], *in_tile(m, 0))
                        dve.nop().then_inc(s_xp, 1)
                    if 1 <= i <= 4:
                        conv(m - 1)
                    if i >= 2:
                        conv_low(m - 2)
                if m0_ == 0:
                    memory_norm(0)
                for m in range(m0_, m0_ + 4):
                    scaled(yg[:, m, :], *in_tile(m, 1))
                    dve.nop().then_inc(s_y, 1)

            for m in range(DB):
                dve.wait_ge(s_gate, m + 1)
                dve.tensor_tensor(xc[:, m, :], gate_i[:, m % 2, :], xc[:, m, :], ALU.mult).then_inc(s_gx, 1)

            def decay(m):
                dve.wait_ge(s_at, m + 1)
                link(dve.tensor_tensor(lru_d[:, m % 2, :], lru_a[:, m, :], lru_a[:, m, :], ALU.mult))
                dve.scalar_tensor_tensor(lru_r[:, m, :], lru_d[:, m % 2, :], 1.0, lru_r[:, m, :], ALU.add,
                                         ALU.mult).then_inc(s_lq, 1)

            def recur(m):
                dve.wait_ge(s_ls, m + 1)
                link(dve.tensor_tensor(lru_r[:, m, :], lru_r[:, m, :], xc[:, m, :], ALU.mult))
                link(dve.tensor_tensor_scan(xc[:, m, :], lru_a[:, m, :], lru_r[:, m, :], 0.0, ALU.mult, ALU.add))
                dve.wait_ge(s_yg, m + 1)
                dve.tensor_tensor(xc[:, m, :], xc[:, m, :], yg[:, m, :], ALU.mult).then_inc(s_rec, 1)

            def rec_low(m):
                dve.wait_ge(s_rech, m + 1)
                dve.tensor_tensor(f_lo[:, m, :], xc[:, m, :], f_hi[:, m, :].bitcast(F32), ALU.subtract).then_inc(s_recl, 1)

            memory_low(0)
            for m in range(DB):
                decay(m)
            g0 = GROUP0["in_qkv"]
            dve.wait_ge(s_rope, 32)

            def qk_tile(t):
                scaled(rope0[0][:], g0 + t // 4, t % 4, s_done["in_qkv"], t + 1)
                rotate(q0[:, t, :] if t < 4 else k0[:, t - 4, :], rope0[0][:], rope0[1:], s_q0)

            for t in range(4):
                qk_tile(t)
            for m in range(4):
                recur(m)
                if m:
                    rec_low(m - 1)
            rec_low(3)
            for t in range(4, 8):
                qk_tile(t)
            for t in range(4):
                scaled(v0_t[:, t, :], g0 + 2, t, s_done["in_qkv"], t + 9)
                dve.nop().then_inc(s_v0t, 1)
            dve.wait_ge(s_mask0, 16)

            def late_recurrence(m):
                recur(m)
                recur(m + 1)
                rec_low(m)
                rec_low(m + 1)
            attention(ATTN["attn0"], {0: lambda: late_recurrence(4), 1: lambda: late_recurrence(6)})
            residual("xa0", s_done["out0"], group0=GROUP0["out0"])

            for l in (0, 1):
                if l:
                    one_over_rms("mix1")

                    def qkv1(dst, done, group, m, t, free=1):
                        scaled(dst, GROUP0[group], m, done, m + 1, free)
                        dve.nop().then_inc(s_qkv1, 1)

                    def rotate_q(t):
                        dve.wait_ge(s_qkv1b, t + 1)
                        if t:
                            dve.wait_ge(s_q1, t if t <= 4 else t + 1)
                        rotate(q1[:, t, :], q1[:, t, :], rope1, s_q1)

                    for t in range(4):
                        qkv1(q1[:, t, :], s_done["qkv_q0"], "qkv_q0", t, t)
                    for t in range(4):
                        rotate_q(t)
                    for t in range(4, 8):
                        qkv1(q1[:, t, :], s_done["qkv_q1"], "qkv_q1", t - 4, t)
                    memory_low(1)
                    rotate_q(4)
                    qkv1(k1_in[:], s_done["qkv_kv"], "qkv_kv", 0, 8, 2)
                    qkv1(v1_t[:], s_done["qkv_kv"], "qkv_kv", 1, 9, 2)
                    dve.wait_ge(s_qkv1b, 9)
                    dve.wait_ge(s_q1, 5)
                    rotate(k1_rot[:], k1_in[:], rope1, s_q1)
                    dve.wait_ge(s_q1, 6)
                    for kv in range(2):
                        for half in range(2):
                            dve.tensor_copy(k1[HD * half:HD * half + HD, kv, :],
                                            k1_rot[HD * kv:HD * kv + HD, :]).then_inc(s_k1, 1)
                    rotate_q(5)
                    link(dve.tensor_scalar(neg_sinks[:], v("sinks", 0, C_HEADS), -1.0, None, ALU.mult))
                    dve.wait_ge(s_mask1, 16)
                    attention(ATTN["attn1"], {1: lambda: [rotate_q(6), rotate_q(7)]})
                    residual("xa1", s_done["out1"], bias="b_out", group0=GROUP0["out1"])
                one_over_rms(f"xa{l}")
                for t in range(4):
                    scaled(qx[:, t, :], GROUP0[f"xq{l}"], t, s_done[f"xq{l}"], t + 1)
                    dve.nop().then_inc(s_xq[l], 1)
                attention(ATTN[f"xattn{l}"])
                residual(f"ffn{l}", s_done[f"xo{l}"], group0=GROUP0[f"xo{l}"])
                one_over_rms(f"ffn{l}")
                if l == 0:
                    memory_norm(1)
                for c in range(2):
                    g0 = GROUP0[f"up{l}{c}"]
                    n0 = (D_FF // P * l + sum(CHUNK[:c])) // 2

                    def ff_group(i, s, g_static):
                        n = n0 + 2 * i + s
                        b0 = (g_static % 2) * 4
                        for p in range(2):
                            dve.wait_ge(s_ff, 4 * n + p + 1)
                            dve.tensor_tensor(ff_g[:, p, :], ps[:, b0 + p, :], rstd[:], ALU.mult).then_inc(s_ff_gate, 1)
                        for p in range(2):
                            dve.wait_ge(s_ff, 4 * n + p + 3)
                            dve.tensor_tensor(ff_u[:, p, :], ps[:, b0 + 2 + p, :], rstd[:], ALU.mult).then_inc(s_ff_up, 1)
                        dve.wait_ge(s_ff_gate, 2 * n + 2)
                        dve.wait_ge(s_ff_up, 2 * n + 2)
                        dve.nop().then_inc(s_free[g_static % 2], 4)
                        for p in range(2):
                            dve.wait_ge(s_ff_silu, 2 * n + p + 1)
                            dve.tensor_tensor(ff_u[:, p, :], ff_g[:, p, :], ff_u[:, p, :], ALU.mult).then_inc(s_ff_prod, 1)
                        for p in range(2):
                            tile = bass.ds(4 * i + (2 * s + p), 1)
                            dve.wait_ge(s_ff_hi, 2 * n + p + 1)
                            dve.tensor_tensor(f_lo[:, tile, :], ff_u[:, p:p + 1, :], f_hi[:, tile, :].bitcast(F32),
                                              ALU.subtract).then_inc(s_ff_lo, 1)
                        dve.wait_ge(s_ff_lo, 2 * n + 2)

                    groups = CHUNK[c] // 2

                    def body(i):
                        for s in range(2):
                            ff_group(i, s, g0 + s)
                    loop(dve, groups // 2, body)
                    if groups % 2:
                        ff_group(groups // 2, 0, g0)
                    nxt = ("mix1", "final")[l]
                    residual(nxt, s_done[f"down{l}{c}"], group0=GROUP0[f"down{l}{c}"], norm_next=c == 1)

            dve.wait_ge(s_rms, NORM["final"] + 1)
            dve.reciprocal(small[:, 4:8], small[:, 0:4]).then_inc(s_rstd, 1)
            dve.wait_ge(s_rstd, NORM["final"] + 1)
            for i, t in enumerate(OUT_ORDER):
                dve.wait_ge(s_fin[1], i + 1)
                dve.tensor_scalar(y_out[:, t, D // 2:], ps[:, bank(GROUP0["final"] + 1, t), :], small[:, 4 + t:5 + t], None,
                                  ALU.mult).then_inc(s_fin_o[1], 1)

        @block.scalar
        def _(act):
            def residual(norm):
                def high(dst, m):
                    act.activation(dst[:, m, :], h[:, m, :], ACT.Identity, scale=v(f"g_{norm}", m)).then_inc(s_zh, 1)

                act.activation(root[:], v("eps"), ACT.Sqrt)
                for m in range(DB):
                    if norm == "mix0":
                        for i in range(4) if m == 0 else (m,) if m >= 4 else ():
                            act.wait_ge(s_done["x_t"], i + 1)
                            act.activation(h[:, i, :], ps[:, i, :], ACT.Copy).then_inc(s_h, 1)
                            act.wait_ge(s_h, i + 1)
                            act.nop().then_inc(s_free[i // 4], 1)
                    act.wait_ge(s_h, NORM[norm] * DB + m + 1)
                    if norm != "final":
                        high(z_hi, m)
                    if m >= 2:
                        act.wait_ge(s_zl, NORM[norm] * DB + (m if norm != "final" else m - 1))
                    act.activation(sq[:, m % 2, :], h[:, m, :], ACT.Square).then_inc(s_sq, 1)
                    if norm == "final":
                        high(y_t, m)
                act.wait_ge(s_sum, NORM[norm] + 1)
                if norm == "final":
                    act.activation(small[:, 0:4], ps[:, bank(GROUP0["final"] + 1, 0), 0:4], ACT.Sqrt, bias=v("eps"),
                                   scale=1.0 / D).then_inc(s_rms, 1)
                else:
                    act.activation(sq[:, 0, :], ps[:, rms_bank[norm], :], ACT.Sqrt, bias=v("eps"),
                                   scale=1.0 / D).then_inc(s_rms, 1)

            rms_bank = {"mix0": bank(GROUP0["in_xy"] + 1, 3), "mix1": bank(GROUP0["qkv_q0"] + 1, 3)}
            for l in (0, 1):
                rms_bank[f"xa{l}"] = bank(GROUP0[f"xq{l}"] + 1, 3)
                rms_bank[f"ffn{l}"] = bank(GROUP0[f"up{l}0"] + 1, 3)

            def memory_norm(l):
                src = (mem_nat0, mem_nat1)[l]
                act.wait_ge(s_mem[l], 16)
                for t in range(MB):
                    for half in range(2):
                        act.activation(mk[:, 2 * half:2 * half + 2, :].rearrange("p a n -> p (a n)"),
                                       src[:, t, 512 * half:512 * half + 512], ACT.Square,
                                       accum_out=small[:, 4 + 2 * t + half:5 + 2 * t + half]).then_inc(s_ms[l], 1)
                        act.wait_ge(s_ms[l], 2 * t + half + 1)
                act.activation(small[:, 0:2], small[:, 4:8].rearrange("p (t a) -> p t a", a=2)[:, :, 0],
                               ACT.Identity).then_inc(s_ms[l], 1)
                act.wait_ge(s_ms[l], 5)
                for t in range(MB):
                    act.activation(small[:, t:t + 1], small[:, 5 + 2 * t:6 + 2 * t], ACT.Identity,
                                   bias=small[:, t:t + 1]).then_inc(s_ms[l], 1)
                act.wait_ge(s_ms[l], 7)
                act.activation(small[:, 0:2], small[:, 0:2], ACT.Sqrt, bias=v("eps"), scale=1.0 / D).then_inc(s_mr[l], 1)

            def memory_high(l):
                g = GROUP0[f"mem_t{l}"]
                for m in range(DB):
                    act.wait_ge(s_done[f"mem_t{l}"], m // 2 + 1)
                    act.activation(mem_hi[:, m, :], ps[:, bank(g, m // 2), (m % 2) * M:(m % 2 + 1) * M], ACT.Identity,
                                   scale=v(f"g_mem{l}", m)).then_inc(s_mh[l], 1)

            def attention(a, extra=None):
                H = a["heads"]

                def exps(n):
                    st = stat[:, n % 3]
                    act.wait_ge(a["s_max"], n + 1)
                    if a["masks"]:
                        src, s0, scale = prob[n % 3], 0, 1.0
                    else:
                        if n >= 3:
                            act.wait_ge(a["s_turned"], n - 2)
                        src, s0, scale = flat, BANK * (a["bank"](0) + 2 * (n % a["s_bufs"])), a["scale"]
                    if a["sink"]:
                        act.activation(st[:, 3, :], st[:, 1, :], ACT.Exp, bias=v("sinks", n))
                    for i, (c, w) in enumerate(a["probs"]):
                        ins = act.activation(prob[n % 3][:, c:c + w], src[:, s0 + c:s0 + c + w], ACT.Exp,
                                             bias=st[:, 1, i:i + 1], scale=scale, accum_out=st[:, 2, i:i + 1])
                    ins.then_inc(a["s_exp"], 1)
                    if not a["masks"]:
                        act.wait_ge(a["s_exp"], n + 1)
                        act.nop().then_inc(a["s_read"], 1)

                def turned(n):
                    act.wait_ge(a["s_turned"], n + 1)
                    if n >= 2:
                        act.wait_ge(a["s_head"], n - 1)
                    t0 = a["bank"](4) * BANK
                    for c in range(0, a["t_dve"], BANK):
                        w = min(BANK, a["t_dve"] - c)
                        ins = act.activation(prob_t[n % 2][:, c:c + w], flat[:, t0 + c:t0 + c + w], ACT.Copy)
                    ins.then_inc(a["s_pt"], 1)

                def output(tile):
                    act.wait_ge(a["s_head"], a["per"] * (tile + 1))
                    if a["name"] == "attn0" and tile == 0:
                        act.wait_ge(s_mem2, 2)
                    act.activation(f_hi[:, a["tile0"] + tile, :], ps[:, a["o_banks"][tile % 2], :], ACT.Copy).then_inc(a["s_o_hi"], 1)

                for n in range(H + 4):
                    if 2 <= n < H + 2 and a["turned_first"]:
                        turned(n - 2)
                    if n in a["output_at"]:
                        output(a["output_at"][n])
                    if 2 <= n < H + 2 and not a["turned_first"]:
                        turned(n - 2)
                    if n < H:
                        exps(n)
                    if n == H - 1 and not a["masks"]:
                        act.nop().then_inc(s_free[GROUP0[a["name"]] % 2], 4)
                    if extra and n in extra:
                        extra[n]()

            act.wait_ge(s_vec, 16)
            act.wait_ge(s_sp_e, 1)
            act.activation(small[:, 16:24], small[:, 8:16], ACT.Exp).then_inc(s_sp_e, 1)
            residual("mix0")
            for m0_ in (0, 4):
                if m0_ == 0:
                    memory_norm(0)
                for i in range(5):
                    m = m0_ + i
                    if i < 4:
                        act.wait_ge(s_xp, m + 1)
                        act.activation(xc[:, m, :], xpad[m % 2][:, 0:T], ACT.Identity, bias=v("conv_b", m),
                                       scale=v("conv_w", m)).then_inc(s_c0, 1)
                    if i >= 1:
                        act.wait_ge(s_xc, m)
                        act.activation(f_hi[:, m - 1, :], xc[:, m - 1, :], ACT.Copy).then_inc(s_xch, 1)
                for m in range(m0_, m0_ + 4):
                    act.wait_ge(s_y, m + 1)
                    act.activation(yg[:, m, :], yg[:, m, :], ACT.Gelu_apprx_tanh).then_inc(s_yg, 1)
            act.wait_ge(s_sp, 1)
            for hd in range(LRU_HEADS):
                g = GROUP0["gates"] + hd
                act.wait_ge(s_done["gates"], 4 * (hd + 1))
                for p in range(2):
                    m = 2 * hd + p
                    act.activation(lru_r[:, m, :], ps[:, bank(g, p), :], ACT.Sigmoid, bias=v("ba", m)).then_inc(s_act, 1)
                    if m >= 2:
                        act.wait_ge(s_gx, m - 1)
                    act.activation(gate_i[:, p, :], ps[:, bank(g, 2 + p), :], ACT.Sigmoid, bias=v("bx", m)).then_inc(s_gate, 1)
                act.wait_ge(s_gate, 2 * hd + 2)
                act.wait_ge(s_act, 2 * hd + 2)
                act.nop().then_inc(s_free[g % 2], 4)
            memory_high(0)
            for m in range(DB):
                act.activation(lru_a[:, m, :], lru_r[:, m, :], ACT.Exp, scale=small[:, 48:56][:, m:m + 1])
                act.activation(lru_r[:, m, :], lru_r[:, m, :], ACT.Tanh, scale=small[:, 56:64][:, m:m + 1]).then_inc(s_at, 1)
            for m in range(DB):
                act.wait_ge(s_lq, m + 1)
                act.activation(lru_r[:, m, :], lru_r[:, m, :], ACT.Sqrt).then_inc(s_ls, 1)
            def rec_high(m):
                act.wait_ge(s_rec, m + 1)
                act.activation(f_hi[:, m, :], xc[:, m, :], ACT.Copy).then_inc(s_rech, 1)
            for m in range(4):
                rec_high(m)

            def extra0(m, dst, src):
                for i in (m, m + 1):
                    rec_high(i)
                act.wait_ge(s_v0p, TB)
                act.wait_ge(s_recl, 4)
                act.activation(dst[:], src, ACT.Copy).then_inc(s_mem2, 1)
            for j in range(TB):
                act.wait_ge(s_v0p, j + 1)
                act.activation(v0[:, j, :], ps[:, ATTN["attn0"]["bank"](3 + j), :], ACT.Copy).then_inc(s_v0, 1)
            attention(ATTN["attn0"], {0: lambda: extra0(4, mem2_hi, mem_hi), 1: lambda: extra0(6, mem2_lo, mem_lo)})
            residual("xa0")
            for l in (0, 1):
                if l:
                    def bias(t, n, x_):
                        act.wait_ge(s_qkv1, n)
                        act.activation(x_, x_, ACT.Identity, bias=v("b_qkv", t)).then_inc(s_qkv1b, 1)
                    for t in range(8):
                        bias(t, t + 1, q1[:, t, :])
                    memory_high(1)
                    bias(8, 9, k1_in[:])
                    bias(9, 10, v1_t[:])
                    act.wait_ge(s_v1p, 1)
                    act.activation(v1[:, :, :].rearrange("p a n -> p (a n)"), ps[:, ATTN["attn1"]["bank"](4), :],
                                   ACT.Copy).then_inc(s_v1, 1)
                    attention(ATTN["attn1"])
                    residual("xa1")
                attention(ATTN[f"xattn{l}"])
                residual(f"ffn{l}")
                if l == 0:
                    memory_norm(1)
                for c in range(2):
                    n0 = (D_FF // P * l + sum(CHUNK[:c])) // 2

                    def ff_group(i, s):
                        n = n0 + 2 * i + s
                        for p in range(2):
                            act.wait_ge(s_ff_gate, 2 * n + p + 1)
                            act.activation(ff_g[:, p, :], ff_g[:, p, :], ACT.Silu).then_inc(s_ff_silu, 1)
                        for p in range(2):
                            act.wait_ge(s_ff_prod, 2 * n + p + 1)
                            act.activation(f_hi[:, bass.ds(4 * i + (2 * s + p), 1), :], ff_u[:, p:p + 1, :],
                                           ACT.Copy).then_inc(s_ff_hi, 1)

                    groups = CHUNK[c] // 2

                    def body(i):
                        for s in range(2):
                            ff_group(i, s)
                    loop(act, groups // 2, body)
                    if groups % 2:
                        ff_group(groups // 2, 0)
                residual(("mix1", "final")[l])
            act.wait_ge(s_rstd, NORM["final"] + 1)
            for i, t in enumerate(OUT_ORDER):
                act.wait_ge(s_fin[0], i + 1)
                act.activation(y_out[:, t, :D // 2], ps[:, bank(GROUP0["final"], t), :], ACT.Copy,
                               scale=small[:, 4 + t:5 + t]).then_inc(s_fin_o[0], 1)


def tables():
    import math
    import numpy as np

    q, k = np.arange(P)[:, None], np.arange(P)[None, :]

    def dist(blocks):
        return q - k + P * blocks
    strip = []
    for blocks in (3, 2, 1, 0):
        d = dist(blocks)
        count = (d <= 128).astype(int) + (d % 4 == 0) + (d % 16 == 0)
        strip.append(np.where((d >= 0) & (count > 0), np.log(np.maximum(count, 1)), NEG))
    mask0 = np.concatenate(strip, axis=1).astype(np.float32)
    pair = np.concatenate([np.where((dist(b) >= 0) & (dist(b) <= 127), 0.0, NEG) for b in (1, 0)], axis=1)
    mask1 = np.tile(pair, (1, TB)).astype(np.float32)
    rot = HD // 4
    inv = np.float32(500000.0) ** (-np.arange(0, rot, 2, dtype=np.float32) / np.float32(rot))
    ang = np.arange(T, dtype=np.float32)[:, None] * inv.astype(np.float32)[None, :]
    cos, sin = np.cos(ang).T, np.sin(ang).T
    cos_t, sin_t = np.ones((P, T), np.float32), np.zeros((P, T), np.float32)
    for head in (0, HD):
        for half in range(2):
            r = head + half * rot // 2
            cos_t[r:r + rot // 2] = cos
            sin_t[r:r + rot // 2] = sin if half else -sin
    return dict(mask0=mask0, mask1=mask1, rope_cos=cos_t, rope_sin=sin_t, identity=np.eye(P, dtype=np.float32))


def kernel(**inputs):
    import numpy as np
    import concourse.bacc as bacc
    from concourse.bass_utils import run_bass_kernel_spmd as run

    a = {k: np.asarray(w) for k, w in inputs.items()}

    def cols(w):
        return w.reshape(-1, P).T

    packed = [cols(a["mix_norm"][0]), cols(a["xa_norm"][0]), cols(a["ffn_norm"][0]), cols(a["mix_norm"][1]),
              cols(a["xa_norm"][1]), cols(a["ffn_norm"][1]), cols(a["final_norm"]), cols(a["xa_mem_norm"][0]),
              cols(a["xa_mem_norm"][1]), cols(a["lru_conv_w"][0].reshape(-1)), cols(a["lru_conv_b"][0]),
              cols(a["lru_ba"][0].reshape(-1)), cols(a["lru_bx"][0].reshape(-1)), cols(a["lru_lambda"][0]),
              cols(a["c_b_qkv"][0]), cols(a["c_b_out"][0]), np.broadcast_to(a["c_sinks"][0], (P, C_HEADS)),
              np.full((P, 1), EPS, np.float32)]
    arrays = dict(
        x=a["x"][0], mem=a["mem"][0], w_in=a["ab_w_in"][0], w_gates=np.stack([a["lru_wa"][0], a["lru_wx"][0]]),
        w_out0=a["ab_w_out"][0], w_qkv=a["c_w_qkv"][0], w_out1=a["c_w_out"][0], xa_wq=a["xa_wq"], xa_wkv=a["xa_wkv"],
        xa_wo=a["xa_wo"], w_gate_up=a["ffn_w_gate_up"], w_down=a["ffn_w_down"],
        vectors=np.concatenate(packed, axis=1), **tables())
    arrays = {k: np.ascontiguousarray(w) for k, w in arrays.items()}
    nc = bacc.Bacc("TRN2", target_bir_lowering=False, num_devices=1)
    args = {k: nc.dram_tensor(f"in_{k}", w.shape, mybir.dt.from_np(w.dtype), kind="ExternalInput").ap()
            for k, w in arrays.items()}
    out = nc.dram_tensor("out", (T, D), F32, kind="ExternalOutput").ap()
    trunk(nc, out=out, **args)
    r = run(nc, [{f"in_{k}": w for k, w in arrays.items()}], core_ids=[0])
    return np.asarray(r.results[0]["out"]).reshape(1, T, D)
```
